# Optimizing a Trainium2 kernel written in Bass

```python
import math
import jax
import jax.numpy as jnp
from jax import lax
import numpy as np
import jax, jax.numpy as jnp

D_MODEL = 2048
BATCH = 1
SEQ = 512
DEPTH = 1

CTX_LEN = 256
GRID_W = 64
D_MIX = D_MODEL
D_GDN = D_MIX // 2
D_RWKV = D_MIX - D_GDN
GDN_HEAD = 128
GDN_HEADS = D_GDN // GDN_HEAD
RWKV_HEAD = 64
RWKV_HEADS = D_RWKV // RWKV_HEAD
CONV_K = 5
CHUNK = 64
LORA_W = 96
LORA_A = 96
EPS = 1e-6
GN_EPS = 64e-5

GDN_COLS = 4 * D_GDN + 4 * GDN_HEADS
RWKV_SHIFT_COLS = 3 * D_RWKV + 2 * LORA_W + 2 * LORA_A
RWKV_COLS = RWKV_SHIFT_COLS + D_RWKV
IN_COLS = GDN_COLS + RWKV_COLS


def rmsnorm(x, g):
    xf = x.astype(jnp.float32)
    y = xf * lax.rsqrt(jnp.mean(xf * xf, axis=-1, keepdims=True) + EPS)
    return (y * g.astype(jnp.float32)).astype(x.dtype)

def l2norm(t):
    return t * lax.rsqrt(jnp.sum(t * t, axis=-1, keepdims=True) + EPS)

def flip_seq(t, d):
    return t if d == 0 else t[:, ::-1]

def centred_dwconv(x, w):
    return lax.conv_general_dilated(
        x, w[:, None, :].astype(x.dtype), window_strides=(1,),
        padding=[(CONV_K // 2, CONV_K // 2)],
        dimension_numbers=('NWC', 'WIO', 'NWC'), feature_group_count=x.shape[-1])

def q_shift_grid(x):
    b, n, ch = x.shape
    rows = n // GRID_W
    q = ch // 4
    p = jnp.pad(x.reshape(b, rows, GRID_W, ch), ((0, 0), (1, 1), (1, 1), (0, 0)))
    left = p[:, 1:-1, :-2, :q]
    right = p[:, 1:-1, 2:, q:2 * q]
    up = p[:, :-2, 1:-1, 2 * q:3 * q]
    down = p[:, 2:, 1:-1, 3 * q:]
    return jnp.concatenate([left, right, up, down], axis=-1).reshape(b, n, ch)

def shift_1d(x):
    h = x.shape[-1] // 2
    p = jnp.pad(x, ((0, 0), (1, 1), (0, 0)))
    return jnp.concatenate([p[:, :-2, :h], p[:, 2:, h:]], axis=-1)

def gated_delta_chunked(q, k, v, beta, g, s0):
    b, n, h, dk = q.shape
    dv = v.shape[-1]
    nc = n // CHUNK

    def chunk(t):
        t = jnp.moveaxis(t, 2, 1)
        return t.reshape((b, h, nc, CHUNK) + t.shape[3:])

    q, k, v, beta, g = (chunk(t) for t in (q, k, v, beta, g))
    g = jnp.cumsum(g, axis=-1)
    idx = jnp.arange(CHUNK)
    tril = idx[:, None] >= idx[None, :]
    strict = idx[:, None] > idx[None, :]
    decay = jnp.exp(jnp.where(tril, g[..., :, None] - g[..., None, :], -jnp.inf))
    kb = k * beta[..., None]
    lmat = jnp.where(strict, jnp.einsum('bhncd,bhnsd->bhncs', kb, k) * decay, 0.0)
    eye = jnp.eye(CHUNK, dtype=jnp.float32)
    tmat = lax.linalg.triangular_solve(eye + lmat, jnp.broadcast_to(eye, lmat.shape),
                                       left_side=True, lower=True, unit_diagonal=True)
    u = tmat @ (v * beta[..., None])
    wk = tmat @ (kb * jnp.exp(g)[..., None])
    attn = jnp.where(tril, jnp.einsum('bhncd,bhnsd->bhncs', q, k) * decay, 0.0)
    g_last = g[..., -1]
    k_tail = k * jnp.exp(g_last[..., None] - g)[..., None]
    q_head = q * jnp.exp(g)[..., None]

    def step(state, inp):
        u_i, wk_i, attn_i, q_i, k_i, gl_i = inp
        v_new = u_i - wk_i @ state
        o_i = q_i @ state + attn_i @ v_new
        state = state * jnp.exp(gl_i)[..., None, None] + jnp.einsum('bhcd,bhce->bhde', k_i, v_new)
        return state, o_i

    xs = tuple(jnp.moveaxis(t, 2, 0) for t in (u, wk, attn, q_head, k_tail, g_last))
    state, o = lax.scan(step, s0, xs)
    o = jnp.moveaxis(o, 0, 2).reshape(b, h, n, dv)
    return jnp.moveaxis(o, 1, 2), state

def gdn_prep(u, conv_w, a_log, dt_bias):
    b, n, _ = u.shape
    qkv = jax.nn.silu(centred_dwconv(u[..., :3 * D_GDN], conv_w)).astype(jnp.float32)
    qkv = qkv.reshape(b, n, 3, GDN_HEADS, GDN_HEAD)
    q = l2norm(qkv[:, :, 0]) * (GDN_HEAD ** -0.5)
    k = l2norm(qkv[:, :, 1])
    v = qkv[:, :, 2]
    z = u[..., 3 * D_GDN:4 * D_GDN]
    gates = u[..., 4 * D_GDN:].astype(jnp.float32).reshape(b, n, 2, 2, GDN_HEADS)
    g = -jnp.exp(a_log) * jax.nn.softplus(gates[:, :, 0] + dt_bias)
    beta = jax.nn.sigmoid(gates[:, :, 1])
    return q, k, v, z, g, beta

def gdn_output(o, z, norm_g):
    b, n = o.shape[:2]
    y = rmsnorm(o, norm_g).reshape(b, n, D_GDN) * jax.nn.silu(z.astype(jnp.float32))
    return y.astype(z.dtype)

def gdn_mixer(u_ctx, u_lat, conv_w, a_log, dt_bias, norm_g):
    streams = (gdn_prep(u_ctx, conv_w, a_log, dt_bias), gdn_prep(u_lat, conv_w, a_log, dt_bias))
    b = u_lat.shape[0]
    outs = [jnp.zeros_like(s[2]) for s in streams]
    for d in range(2):
        state = jnp.zeros((b, GDN_HEADS, GDN_HEAD, GDN_HEAD), jnp.float32)
        for i, (q, k, v, z, g, beta) in enumerate(streams):
            o, state = gated_delta_chunked(flip_seq(q, d), flip_seq(k, d), flip_seq(v, d),
                                           flip_seq(beta[:, :, d], d), flip_seq(g[:, :, d], d), state)
            outs[i] = outs[i] + flip_seq(o, d)
    return (gdn_output(outs[0], streams[0][3], norm_g), gdn_output(outs[1], streams[1][3], norm_g))

def rwkv_heads(t):
    return t.reshape(t.shape[:-1] + (RWKV_HEADS, RWKV_HEAD))

def rwkv_prep(u, shifted, mu, w0, w_up, a0, a_up, k_k, k_a):
    b, n, _ = u.shape
    xs = u[..., :RWKV_SHIFT_COLS]
    xs = (xs + mu * (shifted - xs)).astype(jnp.float32)
    r = xs[..., :D_RWKV]
    k = xs[..., D_RWKV:2 * D_RWKV]
    v = xs[..., 2 * D_RWKV:3 * D_RWKV]
    lo = 3 * D_RWKV
    wd = xs[..., lo:lo + 2 * LORA_W].reshape(b, n, 2, LORA_W)
    ad = xs[..., lo + 2 * LORA_W:].reshape(b, n, 2, LORA_A)
    w_log = -jax.nn.softplus(-(w0 + jnp.einsum('bndr,drc->bndc', jnp.tanh(wd), w_up))) - 0.5
    decay = jnp.exp(-jnp.exp(w_log))
    a = jax.nn.sigmoid(a0 + jnp.einsum('bndr,drc->bndc', ad, a_up))
    kk = l2norm(rwkv_heads(k * k_k))
    k_dir = k[:, :, None] * (1.0 + (a - 1.0) * k_a)
    z = u[..., RWKV_SHIFT_COLS:]
    return rwkv_heads(r), rwkv_heads(v), kk, rwkv_heads(decay), rwkv_heads(a), rwkv_heads(k_dir), z

def rwkv7_scan(r, w, k, v, kk, b_vec, s0):
    def step(state, inp):
        r_t, w_t, k_t, v_t, kk_t, b_t = inp
        sa = -jnp.einsum('bhvk,bhk->bhv', state, kk_t)
        state = (state * w_t[:, :, None, :] + sa[..., None] * b_t[:, :, None, :]
                 + v_t[..., None] * k_t[:, :, None, :])
        return state, jnp.einsum('bhvk,bhk->bhv', state, r_t)

    xs = tuple(jnp.moveaxis(t, 1, 0) for t in (r, w, k, v, kk, b_vec))
    state, o = lax.scan(step, s0, xs)
    return jnp.moveaxis(o, 0, 1), state

def rwkv_output(o, bonus, z, gn_g, gn_b):
    b, n = o.shape[:2]
    mu = jnp.mean(o, axis=-1, keepdims=True)
    var = jnp.mean(jnp.square(o - mu), axis=-1, keepdims=True)
    y = ((o - mu) * lax.rsqrt(var + GN_EPS)).reshape(b, n, D_RWKV) * gn_g + gn_b
    y = (y + bonus.reshape(b, n, D_RWKV)) * jax.nn.silu(z.astype(jnp.float32))
    return y.astype(z.dtype)

def rwkv_mixer(u_ctx, u_lat, mu, w0, w_up, a0, a_up, k_k, k_a, r_k, gn_g, gn_b):
    streams = (
        rwkv_prep(u_ctx, shift_1d(u_ctx[..., :RWKV_SHIFT_COLS]), mu, w0, w_up, a0, a_up, k_k, k_a),
        rwkv_prep(u_lat, q_shift_grid(u_lat[..., :RWKV_SHIFT_COLS]), mu, w0, w_up, a0, a_up, k_k, k_a),
    )
    b = u_lat.shape[0]
    outs = [jnp.zeros_like(s[0]) for s in streams]
    bonus = [jnp.zeros_like(s[0]) for s in streams]
    for d in range(2):
        state = jnp.zeros((b, RWKV_HEADS, RWKV_HEAD, RWKV_HEAD), jnp.float32)
        for i, (r, v, kk, decay, a, k_dir, z) in enumerate(streams):
            k_d = k_dir[:, :, d]
            o, state = rwkv7_scan(flip_seq(r, d), flip_seq(decay[:, :, d], d), flip_seq(k_d, d),
                                  flip_seq(v, d), flip_seq(kk, d), flip_seq(kk * a[:, :, d], d), state)
            outs[i] = outs[i] + flip_seq(o, d)
            bonus[i] = bonus[i] + jnp.sum(r * k_d * r_k, axis=-1, keepdims=True) * v
    return (rwkv_output(outs[0], bonus[0], streams[0][6], gn_g, gn_b),
            rwkv_output(outs[1], bonus[1], streams[1][6], gn_g, gn_b))

def first_inputs(seed: int = 0) -> dict:
    key = jax.random.key(seed)
    ks = jax.random.split(key, 24)
    f32 = jnp.float32

    def nrm(k, shape, s):
        return s * jax.random.normal(k, shape, f32)

    dt = jnp.exp(jax.random.uniform(ks[9], (DEPTH, 2, GDN_HEADS), f32, math.log(1e-3), math.log(1e-1)))
    return {
        "x": nrm(ks[0], (BATCH, SEQ, D_MODEL), 1.0),
        "c": nrm(ks[1], (BATCH, D_MODEL), 1.0),
        "ctx": nrm(ks[2], (BATCH, CTX_LEN, D_MODEL), 1.0),
        "c_ctx": nrm(ks[3], (D_MODEL,), 1.0),
        "w_ada": nrm(ks[4], (DEPTH, D_MODEL, 3 * D_MODEL), 0.5 * D_MODEL ** -0.5),
        "b_ada": nrm(ks[5], (DEPTH, 3 * D_MODEL), 0.02),
        "norm_g": 1.0 + nrm(ks[6], (DEPTH, D_MODEL), 0.02),
        "w_in": nrm(ks[7], (DEPTH, D_MODEL, IN_COLS), D_MODEL ** -0.5),
        "gdn_conv_w": nrm(ks[8], (DEPTH, CONV_K, 3 * D_GDN), CONV_K ** -0.5),
        "gdn_a_log": jnp.log(jax.random.uniform(ks[10], (DEPTH, 2, GDN_HEADS), f32, 1.0, 16.0)),
        "gdn_dt_bias": dt + jnp.log(-jnp.expm1(-dt)),
        "gdn_norm_g": 1.0 + nrm(ks[11], (DEPTH, GDN_HEAD), 0.02),
        "rwkv_mu": jax.random.uniform(ks[12], (DEPTH, RWKV_SHIFT_COLS), f32),
        "rwkv_w0": jax.random.uniform(ks[13], (DEPTH, 2, D_RWKV), f32, -4.0, 1.0),
        "rwkv_w_up": nrm(ks[14], (DEPTH, 2, LORA_W, D_RWKV), 0.5 * LORA_W ** -0.5),
        "rwkv_a0": nrm(ks[15], (DEPTH, 2, D_RWKV), 0.5),
        "rwkv_a_up": nrm(ks[16], (DEPTH, 2, LORA_A, D_RWKV), 0.5 * LORA_A ** -0.5),
        "rwkv_k_k": 0.85 + nrm(ks[17], (DEPTH, D_RWKV), 0.05),
        "rwkv_k_a": 1.0 + nrm(ks[18], (DEPTH, D_RWKV), 0.05),
        "rwkv_r_k": nrm(ks[19], (DEPTH, RWKV_HEADS, RWKV_HEAD), 0.1),
        "rwkv_gn_g": 1.0 + nrm(ks[20], (DEPTH, D_RWKV), 0.02),
        "rwkv_gn_b": nrm(ks[21], (DEPTH, D_RWKV), 0.02),
        "w_out": nrm(ks[22], (DEPTH, D_MIX, D_MODEL), D_MIX ** -0.5),
        "final_norm_g": 1.0 + nrm(ks[23], (D_MODEL,), 0.02),
    }

def first_block(x, c, ctx, c_ctx, w_ada, b_ada, norm_g, w_in, gdn_conv_w, gdn_a_log, gdn_dt_bias,
              gdn_norm_g, rwkv_mu, rwkv_w0, rwkv_w_up, rwkv_a0, rwkv_a_up, rwkv_k_k, rwkv_k_a,
              rwkv_r_k, rwkv_gn_g, rwkv_gn_b, w_out, final_norm_g):
    for layer in range(DEPTH):
        shift, scale, gate = jnp.split(jax.nn.silu(c) @ w_ada[layer] + b_ada[layer], 3, axis=-1)
        shift_c, scale_c, gate_c = jnp.split(jax.nn.silu(c_ctx) @ w_ada[layer] + b_ada[layer], 3, axis=-1)
        h = rmsnorm(x, norm_g[layer]) * (1.0 + scale[:, None]) + shift[:, None]
        hc = rmsnorm(ctx, norm_g[layer]) * (1.0 + scale_c) + shift_c
        u = h @ w_in[layer]
        uc = hc @ w_in[layer]
        ya_c, ya = gdn_mixer(uc[..., :GDN_COLS], u[..., :GDN_COLS], gdn_conv_w[layer],
                             gdn_a_log[layer], gdn_dt_bias[layer], gdn_norm_g[layer])
        yb_c, yb = rwkv_mixer(uc[..., GDN_COLS:], u[..., GDN_COLS:], rwkv_mu[layer], rwkv_w0[layer],
                              rwkv_w_up[layer], rwkv_a0[layer], rwkv_a_up[layer], rwkv_k_k[layer],
                              rwkv_k_a[layer], rwkv_r_k[layer], rwkv_gn_g[layer], rwkv_gn_b[layer])
        if layer + 1 < DEPTH:
            ctx = ctx + gate_c * (jnp.concatenate([ya_c, yb_c], axis=-1) @ w_out[layer])
        x = x + gate[:, None] * (jnp.concatenate([ya, yb], axis=-1) @ w_out[layer])
    return rmsnorm(x, final_norm_g)


_first_inputs = first_inputs


def first_inputs(seed=0):
    import zlib

    import numpy as np

    out = dict(_first_inputs(seed))
    spreads = {}
    factors = {'c_ctx': 26.08,
     'b_ada': 3.068,
     'norm_g': 7.446,
     'gdn_norm_g': 64.0,
     'rwkv_w_up': 53.504,
     'rwkv_k_k': 64.0,
     'rwkv_k_a': 5.387,
     'rwkv_gn_g': 64.0,
     'rwkv_gn_b': 64.0,
     'final_norm_g': 8.167,
     'ctx': 8.0,
     'gdn_conv_w': 7.118,
     'gdn_a_log': 8.0,
     'gdn_dt_bias': 8.0,
     'rwkv_w0': 8.0}
    for name, (base, spread) in spreads.items():
        noise = np.random.default_rng([zlib.crc32(name.encode()), seed]).standard_normal(out[name].shape)
        drawn = base * np.exp(spread * noise) if base else spread * noise
        out[name] = jnp.asarray(drawn.astype(out[name].dtype))
    for name, factor in factors.items():
        out[name] = (out[name] * factor).astype(out[name].dtype)
    return out


_narrow_inputs = first_inputs


def first_inputs(seed=0):
    out = dict(_narrow_inputs(seed))
    wider = {'gdn_norm_g': 12.0,
     'rwkv_k_k': 12.0,
     'rwkv_gn_g': 12.0,
     'rwkv_gn_b': 12.0,
     'final_norm_g': 3.19}
    for name, times in wider.items():
        mean = out[name].mean()
        out[name] = (mean + times * (out[name] - mean)).astype(out[name].dtype)
    return out


D_MIX_2 = D_MODEL
HEAD_DIM = 64
D_ATTN = D_MIX_2 // 2
D_CONV = D_MIX_2 - D_ATTN
N_Q_HEADS = D_ATTN // HEAD_DIM
N_KV_HEADS = 4
GQA_GROUP = N_Q_HEADS // N_KV_HEADS
D_KV = N_KV_HEADS * HEAD_DIM
WINDOW = 128
BLOCK = 128
CONV_WIDTH = 31
CONV_GROUPS = D_CONV // HEAD_DIM
N_BUCKETS = 32
MAX_DISTANCE = 128
LN_EPS = 1e-5
ALPHA = (2.0 * DEPTH) ** 0.25
BETA = (8.0 * DEPTH) ** -0.25

SPLIT_SIZES = (D_ATTN, D_KV, D_KV, D_ATTN, D_CONV, D_CONV, D_CONV)
D_IN = sum(SPLIT_SIZES)
SPLIT_POINTS = [int(s) for s in np.cumsum(SPLIT_SIZES)[:-1]]


def layer_norm(x, g, b):
    xf = x.astype(jnp.float32)
    mu = jnp.mean(xf, axis=-1, keepdims=True)
    var = jnp.mean(jnp.square(xf - mu), axis=-1, keepdims=True)
    y = (xf - mu) * lax.rsqrt(var + LN_EPS)
    return (y * g.astype(jnp.float32) + b.astype(jnp.float32)).astype(x.dtype)

def t5_bucket(dist):
    max_exact = N_BUCKETS // 2
    d = jnp.maximum(dist, 1).astype(jnp.float32)
    large = max_exact + (jnp.log(d / max_exact) / math.log(MAX_DISTANCE / max_exact)
                         * (N_BUCKETS - max_exact)).astype(jnp.int32)
    large = jnp.minimum(large, N_BUCKETS - 1)
    return jnp.where(dist < max_exact, dist, large)

def banded_sink_attention(q, k, v, rel_bias, sinks):
    B, S = q.shape[0], q.shape[1]
    nb = S // BLOCK
    f32 = jnp.float32
    qb = q.astype(f32).reshape(B, nb, BLOCK, N_KV_HEADS, GQA_GROUP, HEAD_DIM)
    kb = k.astype(f32).reshape(B, nb, BLOCK, N_KV_HEADS, HEAD_DIM)
    vb = v.astype(f32).reshape(B, nb, BLOCK, N_KV_HEADS, HEAD_DIM)
    prev = lambda t: jnp.concatenate([jnp.zeros_like(t[:, :1]), t[:, :-1]], axis=1)
    kw = jnp.concatenate([prev(kb), kb], axis=2)
    vw = jnp.concatenate([prev(vb), vb], axis=2)
    scores = jnp.einsum('bnqhgd,bnkhd->bnhgqk', qb, kw) * (HEAD_DIM ** -0.5)

    qi = jnp.arange(BLOCK, dtype=jnp.int32)[:, None]
    kj = jnp.arange(2 * BLOCK, dtype=jnp.int32)[None, :]
    dist = qi + BLOCK - kj
    in_window = (dist >= 0) & (dist < WINDOW)
    bias = rel_bias.astype(f32)[t5_bucket(jnp.maximum(dist, 0))]
    bias = bias.transpose(2, 0, 1).reshape(N_KV_HEADS, GQA_GROUP, BLOCK, 2 * BLOCK)
    key_pos = jnp.arange(nb, dtype=jnp.int32)[:, None] * BLOCK - BLOCK + kj
    valid = in_window[None] & (key_pos[:, None, :] >= 0)

    scores = jnp.where(valid[None, :, None, None], scores + bias, jnp.finfo(f32).min)
    sink = jnp.broadcast_to(sinks.astype(f32).reshape(1, 1, N_KV_HEADS, GQA_GROUP, 1, 1),
                            scores.shape[:-1] + (1,))
    probs = jax.nn.softmax(jnp.concatenate([scores, sink], axis=-1), axis=-1)[..., :-1]
    out = jnp.einsum('bnhgqk,bnkhd->bnqhgd', probs, vw)
    return out.reshape(B, S, N_Q_HEADS * HEAD_DIM).astype(q.dtype)

def conformer_conv(glu_a, glu_b, conv_w, conv_b, ln_g, ln_b, w_pw, b_pw):
    u = glu_a * jax.nn.sigmoid(glu_b)
    u = lax.conv_general_dilated(
        u, conv_w.reshape(CONV_WIDTH, 1, D_CONV).astype(u.dtype),
        window_strides=(1,), padding=[(CONV_WIDTH - 1, 0)],
        dimension_numbers=('NWC', 'WIO', 'NWC'), feature_group_count=D_CONV) + conv_b
    u = jax.nn.silu(layer_norm(u, ln_g, ln_b))
    return u @ w_pw + b_pw

def second_inputs(seed: int = 0) -> dict:
    key = jax.random.key(seed)
    ks = jax.random.split(key, 20)
    n = jax.random.normal
    f32 = jnp.float32
    x = n(ks[0], (BATCH, SEQ, D_MODEL), f32)
    c = n(ks[1], (BATCH, D_MODEL), f32)
    w_ada = 0.5 * D_MODEL ** -0.5 * n(ks[2], (DEPTH, D_MODEL, 3 * D_MODEL), f32)
    b_ada = 0.01 * n(ks[3], (DEPTH, 3 * D_MODEL), f32)
    col_scale = jnp.ones((D_IN,), f32).at[D_ATTN + D_KV:D_ATTN + 2 * D_KV].set(BETA)
    w_in = D_MODEL ** -0.5 * n(ks[4], (DEPTH, D_MODEL, D_IN), f32) * col_scale
    rel_bias = 0.5 * n(ks[5], (N_BUCKETS, N_Q_HEADS), f32)
    sinks = n(ks[6], (DEPTH, N_Q_HEADS), f32)
    conv_w = CONV_WIDTH ** -0.5 * n(ks[7], (DEPTH, CONV_WIDTH, D_CONV), f32)
    conv_b = 0.01 * n(ks[8], (DEPTH, D_CONV), f32)
    conv_ln_g = 1.0 + 0.01 * n(ks[9], (DEPTH, D_CONV), f32)
    conv_ln_b = 0.01 * n(ks[10], (DEPTH, D_CONV), f32)
    w_pw = BETA * D_CONV ** -0.5 * n(ks[11], (DEPTH, D_CONV, D_CONV), f32)
    b_pw = 0.01 * n(ks[12], (DEPTH, D_CONV), f32)
    w_out = BETA * D_MIX_2 ** -0.5 * n(ks[13], (DEPTH, D_MIX_2, D_MODEL), f32)
    ln_g = 1.0 + 0.01 * n(ks[14], (DEPTH, D_MODEL), f32)
    ln_b = 0.01 * n(ks[15], (DEPTH, D_MODEL), f32)
    return {"x": x, "c": c, "w_ada": w_ada, "b_ada": b_ada, "w_in": w_in,
            "rel_bias": rel_bias, "sinks": sinks, "conv_w": conv_w, "conv_b": conv_b,
            "conv_ln_g": conv_ln_g, "conv_ln_b": conv_ln_b, "w_pw": w_pw, "b_pw": b_pw,
            "w_out": w_out, "ln_g": ln_g, "ln_b": ln_b}

def second_block(x, c, w_ada, b_ada, w_in, rel_bias, sinks, conv_w, conv_b, conv_ln_g,
              conv_ln_b, w_pw, b_pw, w_out, ln_g, ln_b):
    c_act = jax.nn.silu(c)
    for l in range(DEPTH):
        mod = (c_act @ w_ada[l] + b_ada[l])[:, None, :]
        shift, scale, gate = jnp.split(mod, 3, axis=-1)
        h = x * (1.0 + scale) + shift
        proj = h @ w_in[l]
        q, k, v, g_attn, glu_a, glu_b, g_conv = jnp.split(proj, SPLIT_POINTS, axis=-1)
        y_attn = banded_sink_attention(q, k, v, rel_bias, sinks[l]) * jax.nn.silu(g_attn)
        y_conv = conformer_conv(glu_a, glu_b, conv_w[l], conv_b[l], conv_ln_g[l], conv_ln_b[l],
                                w_pw[l], b_pw[l]) * jax.nn.silu(g_conv)
        y = jnp.concatenate([y_attn, y_conv], axis=-1) @ w_out[l]
        x = layer_norm(ALPHA * x + gate * y, ln_g[l], ln_b[l])
    return x


_first_inputs_2 = second_inputs


def second_inputs(seed=0):
    import zlib

    import numpy as np

    out = dict(_first_inputs_2(seed))
    spreads = {}
    factors = {'b_ada': 8.0,
     'rel_bias': 8.0,
     'sinks': 8.0,
     'conv_b': 8.0,
     'conv_ln_g': 8.0,
     'conv_ln_b': 8.0,
     'b_pw': 8.0,
     'ln_g': 5.574,
     'ln_b': 5.499}
    for name, (base, spread) in spreads.items():
        noise = np.random.default_rng([zlib.crc32(name.encode()), seed]).standard_normal(out[name].shape)
        drawn = base * np.exp(spread * noise) if base else spread * noise
        out[name] = __import__('jax').numpy.asarray(drawn.astype(out[name].dtype))
    for name, factor in factors.items():
        out[name] = (out[name] * factor).astype(out[name].dtype)
    return out


_narrow_inputs_2 = second_inputs


def second_inputs(seed=0):

    out = dict(_narrow_inputs_2(seed))
    wider = {'rel_bias': 3.31,
     'sinks': 6.63,
     'conv_ln_g': 12.0,
     'conv_ln_b': 12.0,
     'b_pw': 11.45,
     'ln_g': 6.27,
     'ln_b': 6.27}
    for name, times in wider.items():
        mean = out[name].mean()
        out[name] = (mean + times * (out[name] - mean)).astype(out[name].dtype)
    return out


def setup_inputs(seed=0):
    out = dict(first_inputs(seed))
    for name, value in second_inputs(seed + 1).items():
        if name != "x":
            out[name + "_2"] = value
    return out


def reference(
    x, c, ctx, c_ctx, w_ada, b_ada, norm_g, w_in, gdn_conv_w, gdn_a_log, gdn_dt_bias,
    gdn_norm_g, rwkv_mu, rwkv_w0, rwkv_w_up, rwkv_a0, rwkv_a_up, rwkv_k_k, rwkv_k_a, rwkv_r_k,
    rwkv_gn_g, rwkv_gn_b, w_out, final_norm_g, c_2, w_ada_2, b_ada_2, w_in_2, rel_bias_2,
    sinks_2, conv_w_2, conv_b_2, conv_ln_g_2, conv_ln_b_2, w_pw_2, b_pw_2, w_out_2, ln_g_2,
    ln_b_2,
):
    x = first_block(
        x, c, ctx, c_ctx, w_ada, b_ada, norm_g, w_in, gdn_conv_w, gdn_a_log, gdn_dt_bias,
        gdn_norm_g, rwkv_mu, rwkv_w0, rwkv_w_up, rwkv_a0, rwkv_a_up, rwkv_k_k, rwkv_k_a,
        rwkv_r_k, rwkv_gn_g, rwkv_gn_b, w_out, final_norm_g,
    )
    return second_block(
        x, c_2, w_ada_2, b_ada_2, w_in_2, rel_bias_2, sinks_2, conv_w_2, conv_b_2, conv_ln_g_2,
        conv_ln_b_2, w_pw_2, b_pw_2, w_out_2, ln_g_2, ln_b_2,
    )


_drawn_inputs = setup_inputs


def setup_inputs(seed=0):
    import zlib

    import numpy as np

    out = dict(_drawn_inputs(seed))
    spreads = {}
    factors = {'sinks_2': 2.88, 'conv_b_2': 8.0}
    for name, (base, spread) in spreads.items():
        noise = np.random.default_rng([zlib.crc32(name.encode()), seed]).standard_normal(out[name].shape)
        drawn = base * np.exp(spread * noise) if base else spread * noise
        out[name] = jnp.asarray(drawn.astype(out[name].dtype))
    for name, factor in factors.items():
        out[name] = (out[name] * factor).astype(out[name].dtype)
    return out
```

```python
import math
from contextlib import ExitStack

import concourse.bass as bass
from concourse import mybir

F32 = mybir.dt.float32
ALU = mybir.AluOpType
ACT = mybir.ActivationFunctionType
AX_X = mybir.AxisListType.X

P = 128
D = 2048
KT = D // P
LAT, CTX = 512, 256
TOK = LAT + CTX
GH = 8
PAIRS = 8
LORA = 96
CONVK = 5
GT = TOK + 4
GC = LAT + 4
UN = 6
EXPM = 0.6065306597126334
RING = 4
HK = KT // 2
LEVELS = 7

G_ORDER = [[4, 5, 0, 1, 2, 3], [5, 4, 3, 2, 1, 0]]
R_ORDER = [[8, 9, 10, 11, 0, 1, 2, 3, 4, 5, 6, 7], [11, 10, 9, 8, 7, 6, 5, 4, 3, 2, 1, 0]]

R_W0, R_A0, R_KK, R_KA, R_KA1, R_RK, R_GG, R_GB = 21, 23, 25, 26, 27, 28, 29, 30
R_NPAR = 31


def gcol(t):
    return t * P if t < 4 else GC + (t - 4) * P


def halves(view, block, which):
    return view.rearrange("p u (n h b) -> p u n h b", h=2, b=block)[:, :, :, which, :]


def loads(half):
    return (half - RING) // RING * 16


def program(nc, io, out):
    ctx = ExitStack()
    with ctx:
        def sb(name, shape):
            return ctx.enter_context(nc.sbuf_tensor(name, shape, F32))

        def pb(name, shape):
            return ctx.enter_context(nc.psum_tensor(name, shape, F32))

        def sem(name):
            return ctx.enter_context(nc.semaphore(name))

        hT = sb("hT", [P, KT, TOK])
        ring = sb("ring", [P, RING, HK, P])
        par = sb("par", [P, io["par"].shape[1]])
        cst = sb("cst", [P, io["cst"].shape[1]])
        rows = sb("rows", [16, 4])
        gate = sb("gate", [P, KT])
        gc = sb("gc", [P, GH, 6, UN])
        RP = sb("RP", [P, PAIRS, R_NPAR])
        mod2 = sb("mod2", [P, 48])
        unused = sb("unused", [P, 8])
        arena = sb("arena", [P, io["arena"]])

        pjl, pjc = pb("pjl", [P, 512]), pb("pjc", [P, 512])
        xu = [pb(f"xu{i}", [P, 512]) for i in range(2)]
        tp8 = pb("tp", [P, 2, 8, P])
        tp = tp8[:, :, 0:UN]
        pj = [pjl, tp8[:, 0, 0:4].rearrange("p a b -> p (a b)"), pjc]

        C = io["cst_at"]
        ident = cst[:, C["ident"]:C["ident"] + P]
        ones = cst[:, C["ones"]:C["ones"] + P]
        blk = cst[:, C["blk"]:C["blk"] + P]
        istk = cst[:, C["istk"]:C["istk"] + 64]
        rst = [cst[:, C["rst0"]:C["rst0"] + 384], cst[:, C["rst1"]:C["rst1"] + 384]]
        incl = [cst[:, C["incl"] + d * P:C["incl"] + (d + 1) * P] for d in range(2)]
        strict = [cst[:, C["strict"] + d * P:C["strict"] + (d + 1) * P] for d in range(2)]

        def lmask(level, d):
            at = C["lmask"] + (level * 2 + d) * 64
            return cst[:, at:at + 64]

        Q = io["par_at"]

        def pr(name, n=1, k=0):
            return par[:, Q[name] + k:Q[name] + k + n]

        gate_rows = nc.dram_tensor("gate_rows", [2, 2, GH, GT], F32, kind="Internal").ap()
        bias_rows = nc.dram_tensor("bias_rows", [16, 384], F32, kind="Internal").ap()
        bias_copies_t = nc.dram_tensor("bias_copies", [16, P, 384], F32, kind="Internal")
        ydram = nc.dram_tensor("ydram", [16, P, LAT], F32, kind="Internal").ap()

        w_loaded = [sem(f"w_loaded{i}") for i in range(RING)]
        w_used = sem("w_used")

        at = [0]

        def carve(*shape):
            n = 1
            for s in shape:
                n *= s
            v = arena[:, at[0]:at[0] + n]
            at[0] += n
            assert at[0] <= io["arena"], at[0]
            if len(shape) == 1:
                return v
            names = "abcd"[:len(shape)]
            return v.rearrange("p (" + " ".join(names) + ") -> p " + " ".join(names),
                               **{k: s for k, s in zip(names[1:], shape[1:])})

        S = {}
        counts = io["counts"]
        env = dict(locals())
        phases = io["phases"]
        for f, prefixes in phases:
            at[0] = 0
            own = [n for n in io["sems"] if n[0] in prefixes]
            for n in own:
                S[n] = nc.alloc_semaphore(name=n)
            f(nc, env)
            nc.clear_and_free_semaphores([S.pop(n) for n in own])
            nc.all_engine_barrier()


def phase_mod(nc, e):
    io, hT, par, cst, gate, mod2, carve, pr = (e[k] for k in ("io", "hT", "par", "cst", "gate", "mod2", "carve", "pr"))
    S, pj, xu, tp8, ones, ident, rows = (e[k] for k in ("S", "pj", "xu", "tp8", "ones", "ident", "rows"))
    SLOTS, SK = 8, 4
    ada = carve(SLOTS, SK, 512)
    cs = carve(KT, 3)
    csg = carve(KT, 3)
    sq = carve(2, TOK)
    rstd = carve(TOK)
    scl = carve(KT, 2)
    mod = carve(32, 2)
    modr = carve(2, 512)
    modc = carve(96, 3)
    eps = carve(1)
    GROUPS = 24
    H_GROUPS = 8
    ssl, ssc = pj[0], pj[2]
    turned = tp8[:, 0].rearrange("p (b n) s -> p b n s", b=2)

    def half_loops(engine, body):
        with engine.Fori(0, H_GROUPS // 2) as i:
            body(i)

    def rest_loops(engine, body):
        with engine.Fori(H_GROUPS // 2, GROUPS // 2) as i:
            body(i)

    unused = e["unused"]
    with nc.Block() as block:
        @block.gpsimd
        def _(pool):
            for n, name in enumerate(("a_row",)):
                pool.memset(unused[:, n:n + 1], 0.0).then_inc(S[name], 1)

        @block.sync
        def _(sp):
            sp.dma_start(par[:], io["par"]).then_inc(S["a_par"], 16)
            sp.dma_start(cst[:], io["cst"]).then_inc(S["a_par"], 16)
            sp.dma_start(rows[:], io["rows"]).then_inc(S["a_par"], 16)
            for s in range(SLOTS):
                sp.dma_start(ada[:, s], io["w_ada"][s // 4, :, (s % 4) * SK:(s % 4 + 1) * SK]).then_inc(S[f"a_w{s}"], 16)
            with sp.Fori(1, GROUPS // 2) as i:
                for s in range(SLOTS):
                    sp.wait_ge(S["a_used"], (i - 1) * SLOTS + s + 1)
                    sp.dma_start(ada[:, s], io["w_ada"][bass.ds(i * 2 + s // 4, 1), :, (s % 4) * SK:(s % 4 + 1) * SK]
                                 .rearrange("a p k c -> p (a k) c")).then_inc(S[f"a_w{s}"], 16)

        @block.scalar
        def _(act):
            act.dma_start(hT[:, :, 0:LAT], io["xT"]).then_inc(S["a_x"], 16)
            act.dma_start(hT[:, :, LAT:TOK], io["ctxT"]).then_inc(S["a_x"], 16)
            act.wait_ge(S["a_par"], 48)
            act.activation(csg[:], pr("c", 3 * KT).rearrange("p (k s) -> p k s", s=3), ACT.Sigmoid).then_inc(S["a_sig"], 1)
            act.wait_ge(S["a_x"], 32)
            for k in range(KT):
                if k >= 2:
                    act.wait_ge(S["a_ss"], k - 1)
                act.activation(sq[:, k % 2], hT[:, k], ACT.Square).then_inc(S["a_sq"], 1)
            act.wait_ge(S["a_ss"], KT)
            act.wait_ge(S["a_eps"], 1)
            act.activation(rstd[:, 0:LAT], ssl[:, 0:LAT], ACT.Sqrt, bias=eps[:], scale=1.0 / D).then_inc(S["a_rt"], 1)
            act.activation(rstd[:, LAT:TOK], ssc[:, 0:CTX], ACT.Sqrt, bias=eps[:], scale=1.0 / D).then_inc(S["a_rt"], 1)
            act.wait_ge(S["a_scl"], 1)
            for k in range(KT):
                act.wait_ge(S["a_xn"], k + 1)
                act.activation(hT[:, k, 0:LAT], hT[:, k, 0:LAT], ACT.Identity, bias=mod[:, k, 0:1],
                               scale=scl[:, k, 0:1]).then_inc(S["a_h"], 1)
                act.activation(hT[:, k, LAT:TOK], hT[:, k, LAT:TOK], ACT.Identity, bias=mod[:, k, 1:2],
                               scale=scl[:, k, 1:2]).then_inc(S["a_h"], 1)
            act.wait_ge(S["a_h"], 2 * KT)

        @block.tensor
        def _(pe):
            pe.wait_ge(S["a_par"], 48)
            for k in range(KT):
                pe.wait_ge(S["a_sq"], k + 1)
                pe.matmul(ssl[:, 0:LAT], ones, sq[:, k % 2, 0:LAT], start=k == 0, stop=k == KT - 1)
                pe.matmul(ssc[:, 0:CTX], ones, sq[:, k % 2, LAT:TOK], start=k == 0, stop=k == KT - 1).then_inc(S["a_ss"], 1)
            pe.wait_ge(S["a_cs"], 1)

            def groups(i):
                for b in range(2):
                    if b == 0:
                        pe.wait_ge(S["a_row"], 1 + i * 2)
                    for s in range(4):
                        pe.wait_ge(S[f"a_w{4 * b + s}"], i * 16 + 16)
                        for k in range(SK):
                            last = pe.matmul(xu[b][0:3, :], cs[:, s * SK + k], ada[:, 4 * b + s, k],
                                             start=s == 0 and k == 0, stop=s == 3 and k == SK - 1)
                        last.then_inc(S["a_used"], 1)
                for b in range(2):
                    pe.wait_ge(S["a_row"], 1 + i * 2 + b + 1)
                    for n in range(4):
                        last = pe.transpose(turned[:, b, n], modr[:, b, n * P:n * P + P], ident)
                    last.then_inc(S["a_turn"], 1)
            half_loops(pe, groups)
            rest_loops(pe, groups)

        @block.vector
        def _(dve):
            dve.memset(modr[:], 0.0).then_inc(e["w_used"], RING)
            dve.memset(eps[:], 1e-6).then_inc(S["a_eps"], 1)
            dve.wait_ge(S["a_sig"], 1)
            dve.tensor_tensor(cs[:], csg[:], pr("c", 3 * KT).rearrange("p (k s) -> p k s", s=3), ALU.mult).then_inc(S["a_cs"], 1)

            def groups(i):
                for b in range(2):
                    dve.wait_ge(S["a_used"], i * SLOTS + 4 * b + 4)
                    dve.tensor_copy(modr[0:3, b], xu[b][0:3, :]).then_inc(S["a_row"], 1)
                dve.wait_ge(S["a_turn"], i * 2 + 2)
                dve.tensor_copy(modc[:, bass.ds(i * 8, 8)].rearrange("p (b n) s -> p b n s", b=2), turned[:, :, :, 0:3]).then_inc(S["a_mc"], 1)

            half_loops(dve, groups)
            dve.wait_ge(S["a_mc"], H_GROUPS // 2)
            dve.tensor_tensor(mod[:], modc[:, 0:32, 0:2], pr("b_ada", 64).rearrange("p (n s) -> p n s", s=2), ALU.add).then_inc(S["a_d"], 1)
            dve.wait_ge(S["a_d"], 1)
            for s in range(2):
                dve.scalar_tensor_tensor(scl[:, :, s], mod[:, KT:2 * KT, s], 1.0, pr("norm_g", KT), ALU.add, ALU.mult).then_inc(S["a_d"], 1)
            dve.wait_ge(S["a_d"], 3)
            dve.wait_ge(S["a_rt"], 2)
            dve.reciprocal(rstd[:], rstd[:]).then_inc(S["a_scl"], 1)
            dve.wait_ge(S["a_scl"], 1)
            for k in range(KT):
                dve.tensor_tensor(hT[:, k], hT[:, k], rstd[:], ALU.mult).then_inc(S["a_xn"], 1)
            rest_loops(dve, groups)
            dve.wait_ge(S["a_mc"], GROUPS // 2)
            dve.tensor_tensor(gate[:], modc[:, 32:48, 0], pr("b_ada", 96).rearrange("p (n s) -> p n s", s=2)[:, 32:48, 0], ALU.add).then_inc(S["a_d"], 1)
            dve.tensor_tensor(mod2[:], modc[:, 48:96, 2], pr("b_ada2", 48), ALU.add).then_inc(S["a_d"], 1)
            dve.wait_ge(S["a_d"], 5)


def phase_gates(nc, e):
    io, hT, carve, S, pj, rows = (e[k] for k in ("io", "hT", "carve", "S", "pj", "rows"))
    ident, gate_rows = e["ident"], e["gate_rows"]
    gw = carve(KT, 48)
    x = carve(GT)
    bt = carve(GT)
    y = carve(GT)
    z = carve(GT)
    z2 = carve(GT)
    pl = carve(GT)
    gs = [carve(GT), carve(GT)]
    gx = [carve(GT), carve(GT)]
    start16 = carve(2, LAT)
    tot = carve(2, 48)
    start4 = carve(2, 48)
    ea = carve(1)
    gc = e["gc"]
    R = slice(0, 16)
    B = slice(32, 48)
    tpos = pj[1][:, 0:4 * UN * 16].rearrange("p (q t c) -> p q t c", q=4, t=UN)
    tposb = pj[2][:, 0:UN * 16].rearrange("p (t c) -> p t c", t=UN)

    with nc.Block() as block:
        @block.sync
        def _(sp):
            sp.wait_ge(S["b_z"], 4)
            sp.dma_start(gw[:, :, 0:16], io["wg"]).then_inc(S["b_w"], 16)
            sp.dma_start(gw[:, :, 32:48], io["wb"]).then_inc(S["b_w"], 16)
            sp.wait_ge(S["b_scan"], 2)
            for d in range(2):
                sp.dma_start(gate_rows[0, d], gs[d][8 * d:8 * d + 8]).then_inc(S["b_out"], 16)
            sp.wait_ge(S["b_x"], 4)
            for d in range(2):
                sp.dma_start(gate_rows[1, d], bt[32 + 8 * d:40 + 8 * d]).then_inc(S["b_out"], 16)
            sp.wait_ge(S["b_out"], 64)

        @block.tensor
        def _(pe):
            pe.wait_ge(S["b_w"], 32)
            for k in range(KT):
                pe.matmul(pj[0][0:48, 0:LAT], gw[:, k], hT[:, k, 0:LAT], start=k == 0, stop=k == KT - 1)
                pe.matmul(pj[2][0:48, 0:CTX], gw[:, k], hT[:, k, LAT:TOK], start=k == 0, stop=k == KT - 1).then_inc(S["b_p"], 1)
            pe.wait_ge(S["b_x"], 4)
            pe.wait_ge(S["b_scan"], 2)
            for t in range(UN):
                for q, src in enumerate((gs[0], gs[1], gx[0], gx[1])):
                    pe.transpose(tpos[:, q, t], src[R, gcol(t):gcol(t) + P], ident[R, 0:16])
                last = pe.transpose(tposb[:, t], bt[B, gcol(t):gcol(t) + P], ident[B, 32:48])
            last.then_inc(S["b_tr"], 1)

        @block.scalar
        def _(act):
            act.wait_ge(S["b_z"], 4)
            act.activation(ea[R], rows[:, 0:1], ACT.Exp).then_inc(S["b_ea"], 1)
            act.wait_ge(S["b_p"], KT)
            for n, (a, b, src) in enumerate(((0, LAT, pj[0]), (GC, GT, pj[2]))):
                act.activation(x[R, a:b], src[R, 0:b - a], ACT.Identity, bias=rows[:, 1:2]).then_inc(S["b_x"], 1)
                act.activation(bt[B, a:b], src[B, 0:b - a], ACT.Sigmoid).then_inc(S["b_x"], 1)
            act.wait_ge(S["b_x"], 4)
            act.activation(y[R], x[R], ACT.Abs).then_inc(S["b_y"], 1)
            act.wait_ge(S["b_y"], 1)
            act.activation(y[R], y[R], ACT.Exp, scale=-1.0).then_inc(S["b_y"], 1)

        @block.vector
        def _(dve):
            n = [0]

            def link(ins):
                n[0] += 1
                ins.then_inc(S["b_v"], 1)
                dve.wait_ge(S["b_v"], n[0])

            for t in (gw[:, :, 16:32], x[:, LAT:GC], bt[:, LAT:GC]):
                dve.memset(t, 0.0).then_inc(S["b_z"], 1)
            dve.memset(z[:], 0.0).then_inc(S["b_z"], 1)
            dve.wait_ge(S["b_y"], 2)
            link(dve.tensor_scalar(z[R], y[R], 2.0, None, ALU.add))
            link(dve.reciprocal(z[R], z[R]))
            link(dve.tensor_tensor(z[R], z[R], y[R], ALU.mult))
            link(dve.tensor_tensor(z2[R], z[R], z[R], ALU.mult))
            link(dve.tensor_scalar(pl[R], z2[R], 1.0 / 17, None, ALU.mult))
            for c in (15, 13, 11, 9, 7, 5, 3):
                link(dve.scalar_tensor_tensor(pl[R], pl[R], 1.0 / c, z2[R], ALU.add, ALU.mult))
            link(dve.scalar_tensor_tensor(pl[R], pl[R], 1.0, z[R], ALU.add, ALU.mult))
            link(dve.tensor_scalar(x[R], x[R], 0.0, None, ALU.max))
            link(dve.scalar_tensor_tensor(x[R], pl[R], 2.0, x[R], ALU.mult, ALU.add))
            dve.wait_ge(S["b_ea"], 1)
            link(dve.tensor_scalar(x[R], x[R], ea[R], -1.0, ALU.mult, ALU.mult))
            runs = lambda v: v.rearrange("p (n b t) -> p n b t", b=4, t=16)
            for d in range(2):
                first = 15 if d else 0
                last = 0 if d else 15
                back = slice(None, None, -1 if d else 1)
                link(dve.memset(gs[d][:, LAT:GC], 0.0))
                link(dve.memset(start16[:, d], 1.0))
                link(dve.memset(start16[:, d, first:LAT:16], 0.0))
                link(dve.memset(start4[:, d], 1.0))
                link(dve.memset(start4[:, d, 3 if d else 0:48:4], 0.0))
                for a, b, k0 in ((0, LAT, 0), (GC, GT, 32)):
                    m, k1 = b - a, k0 + (b - a) // 16
                    link(dve.tensor_tensor_scan(gs[d][R, a:b][:, back], start16[R, d, 0:m][:, back], x[R, a:b][:, back], 0.0, ALU.mult, ALU.add))
                    link(dve.tensor_copy(tot[R, d, k0:k1], gs[d][R, a + last:b:16]))
                    link(dve.tensor_tensor_scan(tot[R, d, k0:k1][:, back], start4[R, d, k0:k1][:, back], tot[R, d, k0:k1][:, back], 0.0,
                                                ALU.mult, ALU.add))
                    to = runs(gs[d][R, a:b])[:, :, 0:3] if d else runs(gs[d][R, a:b])[:, :, 1:4]
                    t4 = tot[R, d, k0:k1].rearrange("p (n b) -> p n b", b=4)
                    of = t4[:, :, 1:4] if d else t4[:, :, 0:3]
                    link(dve.tensor_tensor(to, to, of.unsqueeze(3).to_broadcast([16, m // 64, 3, 16]), ALU.add))
                link(dve.tensor_copy(gx[d][R], gs[d][R]))
                for a, b in ((0, LAT), (GC, GT)):
                    half = lambda v: v[R, a:b].rearrange("p (u h t) -> p u h t", h=2, t=64)[:, :, d]
                    end = 0 if d else 63
                    link(dve.tensor_tensor(half(gx[d]), half(gs[d]), half(gs[d])[:, :, end:end + 1].to_broadcast([16, (b - a) // P, 64]), ALU.subtract))
                dve.tensor_copy(tot[R, d, 0:1], gs[d][R, 0:1]).then_inc(S["b_scan"], 1)
            dve.wait_ge(S["b_tr"], 1)
            for d in range(2):
                dve.tensor_copy(gc[:, :, d], tpos[:, d, :, 8 * d:8 * d + 8].rearrange("p t h -> p h t")).then_inc(S["b_gc"], 1)
                dve.tensor_copy(gc[:, :, 2 + d], tposb[:, :, 8 * d:8 * d + 8].rearrange("p t h -> p h t")).then_inc(S["b_gc"], 1)
                dve.tensor_copy(gc[:, :, 4 + d], tpos[:, 2 + d, :, 8 * d:8 * d + 8].rearrange("p t h -> p h t")).then_inc(S["b_gc"], 1)
            dve.wait_ge(S["b_gc"], 6)


def project(pe, e, i, j, base, lat, ctxp, k0=0, k1=KT):
    S, ring, hT, w_loaded, w_used = (e[k] for k in ("S", "ring", "hT", "w_loaded", "w_used"))
    for kk in range(k0, k1):
        s = (2 * j + kk // HK) % RING
        if kk % HK == 0:
            pe.wait_ge(w_loaded[s], base + (i * 2 + j // 2 + 1) * 16)
        last = pe.matmul(lat, ring[:, s, kk % HK], hT[:, kk, 0:LAT], start=kk == 0, stop=kk == KT - 1)
        if ctxp is not None:
            last = pe.matmul(ctxp, ring[:, s, kk % HK], hT[:, kk, LAT:TOK], start=kk == 0, stop=kk == KT - 1)
        if kk % HK == HK - 1:
            last.then_inc(w_used, 1)


def load_tiles(sp, e, src, base_used, i, n0=0, n1=8):
    ring, w_loaded, w_used = e["ring"], e["w_loaded"], e["w_used"]
    for n in range(n0, n1):
        j, hf, s = n // 2, n % 2, n % RING
        sp.wait_ge(w_used, base_used + i * 8 + n - RING + 1)
        sp.dma_start(ring[:, s], src[bass.ds(i * 4 + j, 1), :, hf * HK:(hf + 1) * HK]
                     .rearrange("a p k c -> p (a k) c")).then_inc(w_loaded[s], 16)


def invert_pe(pe, S, q, i, lv, LT, T, TT, Xs, xu, tp, ident, fill):
    n2 = 2 * lv
    for l in range(lv):
        b = 1 << l
        if l:
            for d in range(2):
                pe.wait_ge(S[q + "tt"], i * n2 + (l - 1) * 2 + d + 1)
                for u in range(UN):
                    last = pe.matmul(xu[d][:, u * 64:u * 64 + 64], LT[:, d, u], halves(T[:, d], b, d)[:, u],
                                     start=True, stop=True)
                last.then_inc(S[q + "x"], 1)
            if fill:
                fill(3 * l)
            for d in range(2):
                pe.wait_ge(S[q + "xs"], i * (n2 - 2) + (l - 1) * 2 + d + 1)
                for u in range(UN):
                    last = pe.matmul(xu[d][:, u * 64:u * 64 + 64], TT[:, d, u], Xs[:, d, u], start=True, stop=True)
                last.then_inc(S[q + "u"], 1)
            if fill:
                fill(3 * l + 1)
        for d in range(2):
            pe.wait_ge(S[q + "t"], i * n2 + l * 2 + d + 1)
            for u in range(UN):
                last = pe.transpose(tp[:, d, u], T[:, d, u], ident)
            last.then_inc(S[q + "tr"], 1)
        if fill:
            fill(3 * l + 2)


def invert_dve(dve, S, q, i, lv, T, Xs, xu, lmask):
    n2 = 2 * lv
    for l in range(1, lv):
        b = 1 << l
        for d in range(2):
            dve.wait_ge(S[q + "x"], i * (n2 - 2) + (l - 1) * 2 + d + 1)
            dve.tensor_tensor(Xs[:, d], xu[d][:, 0:384].rearrange("p (u c) -> p u c", u=UN),
                              lmask(l, d).unsqueeze(1).to_broadcast([P, UN, 64]), ALU.mult).then_inc(S[q + "xs"], 1)
        for d in range(2):
            dve.wait_ge(S[q + "u"], i * (n2 - 2) + (l - 1) * 2 + d + 1)
            v = halves(T[:, d], b, d)
            dve.tensor_tensor(v, v, xu[d][:, 0:384].rearrange("p (u n b) -> p u n b", u=UN, b=b), ALU.add).then_inc(S[q + "t"], 1)


def invert_act(act, S, q, i, lv, TT, tp):
    n2 = 2 * lv
    for l in range(lv):
        b = 1 << l
        for d in range(2):
            act.wait_ge(S[q + "tr"], i * n2 + l * 2 + d + 1)
            o, s = (TT[:, d], tp[:, d]) if l == 0 else (halves(TT[:, d], b, 1 - d), halves(tp[:, d], b, 1 - d))
            act.activation(o, s, ACT.Copy).then_inc(S[q + "tt"], 1)


def phase_gdn(nc, e):
    io, carve, S, pj, xu, tp, ident, ones, lmask, incl, pr = (
        e[k] for k in ("io", "carve", "S", "pj", "xu", "tp", "ident", "ones", "lmask", "incl", "pr"))
    gc, gate_rows, ydram, w_used = e["gc"], e["gate_rows"], e["ydram"], e["w_used"]
    raw = carve(3, GT + 4)
    zraw, zs = carve(LAT), carve(LAT)
    qkv = carve(3, GT)
    sg = carve(4, GT)
    G = carve(2, GT)
    KB = carve(2, GT)
    EG = carve(2, GT)
    KBG = carve(2, GT)
    QG = carve(2, LAT)
    ET = carve(2, UN, P)
    E0 = carve(2, UN, 64)
    LT = carve(2, UN, P)
    T = carve(2, UN, P)
    TT = carve(2, UN, P)
    Xs = carve(2, UN, 64)
    MT = carve(2, 4, P)
    bV = carve(2, UN, P)
    KL = carve(2, UN, P)
    W = carve(2, P)
    SA = carve(2, P)
    St = carve(2, P)
    oT = carve(LAT)
    ybuf = carve(LAT)
    tail = carve(2, UN)
    gcs = carve(6, UN)
    hp = carve(16)
    eps = carve(1)
    half = io["base_g"]
    wb = loads(half)
    sq, nr = sg[:, 0:2], sg[:, 2:4]
    DV = io["DV_G"]

    unused = e["unused"]
    with nc.Block() as block:
        @block.gpsimd
        def _(pool):
            for n, name in enumerate(("g_y", "g_st", "g_raw")):
                pool.memset(unused[:, n:n + 1], 0.0).then_inc(S[name], 1)

        @block.sync
        def _(sp):
            def gate_rows_of(i):
                for d in range(2):
                    sp.dma_start(G[:, d], gate_rows[0, d, bass.ds(i, 1)].rearrange("a t -> (a t)").partition_broadcast(P)).then_inc(S["g_rows"], 16)
                    sp.dma_start(KB[:, d], gate_rows[1, d, bass.ds(i, 1)].rearrange("a t -> (a t)").partition_broadcast(P)).then_inc(S["g_rows"], 16)


            gate_rows_of(0)
            load_tiles(sp, e, io["w_g"], half, 0, 0, 8)
            with sp.Fori(0, GH - 1) as i:
                load_tiles(sp, e, io["w_g"], half, i + 1, 0, 4)
                sp.wait_ge(S["g_pre"], i + 1)
                sp.wait_ge(S["g_l0"], i * 2 + 2)
                gate_rows_of(i + 1)
                load_tiles(sp, e, io["w_g"], half, i + 1, 4, 8)

        @block.tensor
        def _(pe):
            def column(i, j, k0=0, k1=KT):
                if k0 == 0:
                    pe.wait_ge(S["g_raw"], 1 + i * 6 + (0, 1, 3, 5)[j])
                project(pe, e, i, j, wb, pj[0][:, 0:LAT], pj[2][:, 0:CTX] if j in (1, 2) else None, k0, k1)

            def turn(i, more):
                def fill(n):
                    if more and 3 <= n < 3 + KT:
                        column(i + 1, 2, n - 3, n - 2)

                def fill_scan(n):
                    if more and n < KT:
                        column(i + 1, 3, n, n + 1)

                if more:
                    column(i + 1, 0)
                    column(i + 1, 1, 0, 6)
                pe.wait_ge(S["g_y"], 1 + i)
                pe.wait_ge(S["g_sq"], i * 3 + 1)
                pe.matmul(xu[0][:, 0:LAT], ones, sq[:, 0, 0:LAT], start=True, stop=True).then_inc(S["g_ss"], 1)
                pe.wait_ge(S["g_sq"], i * 3 + 2)
                pe.matmul(pj[1][:, 0:LAT], ones, sq[:, 1, 0:LAT], start=True, stop=True)
                pe.matmul(xu[1][:, 0:CTX], ones, sq[:, 1, GC:GT], start=True, stop=True).then_inc(S["g_ss"], 1)
                if more:
                    column(i + 1, 1, 6, KT)
                pe.wait_ge(S["g_kb"], i * 2 + 2)
                for d in range(2):
                    for u in range(UN):
                        c = gcol(u)
                        last = pe.matmul(tp[:, d, u], qkv[:, 1, c:c + P], KB[:, d, c:c + P], start=True, stop=True)
                    last.then_inc(S["g_lt"], 1)
                    for u in range(UN):
                        c = gcol(u)
                        last = pe.matmul(xu[d][:, u * 64:u * 64 + 64], KB[:, d, c:c + P], qkv[:, 1, c + d:c + P:2],
                                         start=True, stop=True)
                    last.then_inc(S["g_l0"], 1)
                for d in range(2):
                    pe.wait_ge(S["g_ltc"], i * 2 + d + 1)
                    for u in range(4):
                        last = pe.matmul(tp[:, d, u], qkv[:, 1, u * P:u * P + P], qkv[:, 0, u * P:u * P + P], start=True, stop=True)
                    last.then_inc(S["g_mt"], 1)
                pe.wait_ge(S["g_mtc"], i * 2 + 2)
                for d in range(2):
                    for u in range(UN):
                        last = pe.transpose(tp[:, d, u], qkv[:, 2 - d, gcol(u):gcol(u) + P], ident)
                last.then_inc(S["g_vk"], 1)
                pe.wait_ge(S["g_vkc"], i + 1)
                invert_pe(pe, S, "g_", i, LEVELS, LT, T, TT, Xs, xu, tp, ident, fill)
                pe.wait_ge(S["g_pre"], i + 1)
                for j in range(UN):
                    for d in range(2):
                        u = G_ORDER[d][j]
                        c = gcol(u)
                        if j == 0:
                            pe.wait_ge(S["g_tt"], i * 14 + 12 + d + 1)
                        pe.wait_ge(S["g_s"], i * 14 + 2 * j + d + 1)
                        pe.matmul(xu[d][:, 0:P], KBG[:, d, c:c + P], St[:, d], start=True, stop=True).then_inc(S["g_w"], 1)
                    fill_scan(3 * j)
                    for d in range(2):
                        u = G_ORDER[d][j]
                        pe.wait_ge(S["g_wc"], i * 12 + 2 * j + d + 1)
                        pe.matmul(xu[d][:, P:2 * P], TT[:, d, u], W[:, d], start=True, stop=True).then_inc(S["g_sa"], 1)
                    fill_scan(3 * j + 1)
                    for d in range(2):
                        u = G_ORDER[d][j]
                        pe.wait_ge(S["g_sac"], i * 12 + 2 * j + d + 1)
                        last = pe.matmul(xu[d][:, 2 * P:3 * P], KL[:, d, u], SA[:, d], start=True, stop=True)
                        if u < 4:
                            pe.matmul(xu[d][:, 3 * P:4 * P], St[:, d], QG[:, d, u * P:u * P + P], start=True, stop=False)
                            last = pe.matmul(xu[d][:, 3 * P:4 * P], SA[:, d], MT[:, d, u], start=False, stop=True)
                        last.then_inc(S["g_ds"], 1)
                    fill_scan(3 * j + 2)
                pe.wait_ge(S["g_sq"], i * 3 + 3)
                pe.matmul(pj[1][:, 0:LAT], ones, sq[:, 0, 0:LAT], start=True, stop=True).then_inc(S["g_ss"], 1)

            for j in range(4):
                column(0, j)
            with pe.Fori(0, GH - 1) as i:
                turn(i, True)
            turn(GH - 1, False)

        @block.scalar
        def _(act):
            act.wait_ge(S["g_v0"], 4)

            def copy_column(i, j):
                act.wait_ge(w_used, half + i * 8 + 2 * j + 2)
                act.activation(zraw[:] if j == 3 else raw[:, j, 2:2 + LAT], pj[0][:, 0:LAT], ACT.Copy).then_inc(S["g_raw"], 1)
                if j in (1, 2):
                    act.activation(raw[:, j, GC + 2:GT + 2], pj[2][:, 0:CTX], ACT.Copy).then_inc(S["g_raw"], 1)

            def turn(i, more):
                act.wait_ge(S["g_raw"], 1 + i * 6 + 6)
                act.activation(sg[:, 3, 0:LAT], zraw[:], ACT.Sigmoid).then_inc(S["g_sig"], 1)
                for j in range(3):
                    act.wait_ge(S["g_conv"], i * 3 + j + 1)
                    n = LAT if j == 0 else GT
                    act.activation(sg[:, j, 0:n], qkv[:, j, 0:n], ACT.Sigmoid).then_inc(S["g_sig"], 1)
                for j in range(2):
                    act.wait_ge(S["g_silu"], i * 4 + 4)
                    n = LAT if j == 0 else GT
                    act.activation(sq[:, j, 0:n], qkv[:, j, 0:n], ACT.Square).then_inc(S["g_sq"], 1)
                if more:
                    copy_column(i + 1, 0)
                act.wait_ge(S["g_ss"], i * 3 + 2)
                act.activation(nr[:, 0, 0:LAT], xu[0][:, 0:LAT], ACT.Sqrt, bias=eps[:]).then_inc(S["g_rt"], 1)
                act.activation(nr[:, 1, 0:LAT], pj[1][:, 0:LAT], ACT.Sqrt, bias=eps[:]).then_inc(S["g_rt"], 1)
                act.activation(nr[:, 1, GC:GT], xu[1][:, 0:CTX], ACT.Sqrt, bias=eps[:]).then_inc(S["g_rt"], 1)
                act.wait_ge(S["g_rows"], i * 64 + 64)
                act.activation(EG[:], G[:], ACT.Exp).then_inc(S["g_e"], 1)
                act.wait_ge(S["g_d"], i + 1)
                act.activation(ET[:], ET[:], ACT.Exp).then_inc(S["g_e"], 1)
                act.activation(E0[:], E0[:], ACT.Exp, scale=-1.0).then_inc(S["g_e"], 1)
                act.activation(tail[:], tail[:], ACT.Exp).then_inc(S["g_e"], 1)
                if more:
                    copy_column(i + 1, 1)
                invert_act(act, S, "g_", i, LEVELS, TT, tp)
                if more:
                    copy_column(i + 1, 2)
                for j in range(UN):
                    for d in range(2):
                        act.wait_ge(S["g_sa"], i * 12 + 2 * j + d + 1)
                        if j:
                            act.wait_ge(S["g_ds"], i * 12 + 2 * (j - 1) + d + 1)
                        act.activation(SA[:, d], xu[d][:, P:2 * P], ACT.Copy).then_inc(S["g_sac"], 1)
                if more:
                    act.wait_ge(S["g_silu"], i * 4 + 4)
                    copy_column(i + 1, 3)
                act.wait_ge(S["g_o"], i * 8 + 8)
                act.activation(sq[:, 0, 0:LAT], oT[:], ACT.Square).then_inc(S["g_sq"], 1)
                act.wait_ge(S["g_ss"], i * 3 + 3)
                act.activation(nr[:, 0, 0:LAT], pj[1][:, 0:LAT], ACT.Sqrt, bias=eps[:], scale=1.0 / P).then_inc(S["g_rt"], 1)
                act.wait_ge(S["g_y"], 1 + i + 1)
                act.dma_start(ydram[bass.ds(i, 1)].rearrange("a p t -> p (a t)"), ybuf[:]).then_inc(S["g_st"], 16)

            for j in range(4):
                copy_column(0, j)
            with act.Fori(0, GH - 1) as i:
                turn(i, True)
            turn(GH - 1, False)
            act.wait_ge(S["g_st"], 1 + 16 * GH)

        @block.vector
        def _(dve):
            dve.memset(eps[:], 1e-6).then_inc(S["g_v0"], 1)
            dve.memset(raw[:], 0.0).then_inc(S["g_v0"], 1)
            dve.memset(sg[:], 1.0).then_inc(S["g_v0"], 1)
            dve.memset(qkv[:], 0.0).then_inc(S["g_v0"], 1)
            dve.wait_ge(S["g_v0"], 4)

            def turn(i):
                dve.wait_ge(S["g_y"], 1 + i)
                n = [0]

                def link(ins):
                    n[0] += 1
                    ins.then_inc(S["g_v"], 1)
                    dve.wait_ge(S["g_v"], i * DV + n[0])

                link(dve.tensor_copy(hp[:], pr("gp", 16 * GH).rearrange("p (h c) -> p h c", h=GH)[:, bass.ds(i, 1), :]
                                     .rearrange("p a c -> p (a c)")))
                link(dve.tensor_copy(gcs[:], gc[:, bass.ds(i, 1)].rearrange("p a q t -> p (a q) t")))
                for d in range(2):
                    dve.memset(St[:, d], 0.0).then_inc(S["g_s"], 1)
                link(dve.memset(oT[:], 0.0))
                for j in range(3):
                    m = LAT if j == 0 else GT
                    dve.wait_ge(S["g_raw"], 1 + i * 6 + (1, 3, 5)[j])
                    link(dve.tensor_scalar(qkv[:, j, 0:m], raw[:, j, 0:m], hp[:, 5 * j:5 * j + 1], None, ALU.mult))
                    for o in range(1, CONVK):
                        ins = dve.scalar_tensor_tensor(qkv[:, j, 0:m], raw[:, j, o:o + m], hp[:, 5 * j + o:5 * j + o + 1],
                                                       qkv[:, j, 0:m], ALU.mult, ALU.add)
                        if o < CONVK - 1:
                            link(ins)
                        else:
                            ins.then_inc(S["g_conv"], 1)
                dve.wait_ge(S["g_conv"], i * 3 + 3)
                for j in range(3):
                    m = LAT if j == 0 else GT
                    dve.wait_ge(S["g_sig"], i * 4 + j + 2)
                    dve.tensor_tensor(qkv[:, j, 0:m], qkv[:, j, 0:m], sg[:, j, 0:m], ALU.mult).then_inc(S["g_silu"], 1)
                dve.tensor_tensor(zs[:], zraw[:], sg[:, 3, 0:LAT], ALU.mult).then_inc(S["g_silu"], 1)
                dve.wait_ge(S["g_silu"], i * 4 + 4)
                dve.wait_ge(S["g_rows"], i * 64 + 64)
                for d in range(2):
                    for u in range(UN):
                        c = gcol(u)
                        for hf in range(2):
                            q = d if hf == d else 4 + d
                            dve.tensor_scalar(ET[:, d, u, 64 * hf:64 * hf + 64], G[:, d, c + 64 * hf:c + 64 * hf + 64], gcs[:, q, u:u + 1], 0.0,
                                              ALU.subtract, ALU.min)
                        dve.tensor_scalar(E0[:, d, u], G[:, d, c + d:c + P:2], gcs[:, d, u:u + 1], 0.0, ALU.subtract, ALU.max)
                    end = 0 if d else P - 1
                    dve.tensor_tensor(tail[:, d, 0:4], G[:, d, end:LAT:P], gcs[:, 4 + d, 0:4], ALU.subtract)
                    last = dve.tensor_tensor(tail[:, d, 4:6], G[:, d, GC + end:GT:P], gcs[:, 4 + d, 4:6], ALU.subtract)
                last.then_inc(S["g_d"], 1)
                dve.wait_ge(S["g_rt"], i * 4 + 3)
                link(dve.reciprocal(nr[:, 0:1, 0:LAT], nr[:, 0:1, 0:LAT]))
                link(dve.reciprocal(nr[:, 1], nr[:, 1]))
                link(dve.scalar_tensor_tensor(qkv[:, 0, 0:LAT], qkv[:, 0, 0:LAT], float(P) ** -0.5, nr[:, 0, 0:LAT], ALU.mult, ALU.mult))
                link(dve.tensor_tensor(qkv[:, 1], qkv[:, 1], nr[:, 1], ALU.mult))
                for d in range(2):
                    dve.tensor_tensor(KB[:, d], KB[:, d], qkv[:, 1], ALU.mult).then_inc(S["g_kb"], 1)
                dve.wait_ge(S["g_kb"], i * 2 + 2)
                dve.wait_ge(S["g_e"], i * 4 + 4)
                for d in range(2):
                    for a, b in ((0, LAT), (GC, GT)):
                        v = EG[:, d, a:b].rearrange("p (u h t) -> p u h t", h=2, t=64)
                        end = 0 if d else 63
                        link(dve.tensor_tensor(v[:, :, 1 - d], v[:, :, 1 - d], v[:, :, d, end:end + 1].to_broadcast([P, (b - a) // P, 64]), ALU.mult))
                for d in range(2):
                    dve.tensor_tensor(KBG[:, d], KB[:, d], EG[:, d], ALU.mult)
                    last = dve.tensor_tensor(QG[:, d], qkv[:, 0, 0:LAT], EG[:, d, 0:LAT], ALU.mult)
                last.then_inc(S["g_pre"], 1)
                for d in range(2):
                    dve.wait_ge(S["g_lt"], i * 2 + d + 1)
                    dve.tensor_tensor(LT[:, d], tp[:, d], ET[:, d], ALU.mult).then_inc(S["g_ltc"], 1)
                    link(dve.tensor_tensor(E0[:, d], E0[:, d], lmask(0, d).unsqueeze(1).to_broadcast([P, UN, 64]), ALU.mult))
                    link(dve.tensor_copy(T[:, d], ident.unsqueeze(1).to_broadcast([P, UN, P])))
                    dve.wait_ge(S["g_l0"], i * 2 + d + 1)
                    link(dve.tensor_tensor(E0[:, d], E0[:, d], xu[d][:, 0:384].rearrange("p (u c) -> p u c", u=UN), ALU.mult))
                    v = T[:, d, :, d:P:2]
                    dve.tensor_tensor(v, v, E0[:, d], ALU.add).then_inc(S["g_t"], 1)
                for d in range(2):
                    dve.wait_ge(S["g_ltc"], i * 2 + 2)
                    link(dve.tensor_tensor(ET[:, d, 0:4], ET[:, d, 0:4], incl[d].unsqueeze(1).to_broadcast([P, 4, P]), ALU.mult))
                    dve.wait_ge(S["g_mt"], i * 2 + d + 1)
                    dve.tensor_tensor(MT[:, d], tp[:, d, 0:4], ET[:, d, 0:4], ALU.mult).then_inc(S["g_mtc"], 1)
                dve.wait_ge(S["g_vk"], i + 1)
                for d in range(2):
                    dve.tensor_tensor(bV[:, d], tp[:, 0], gcs[:, 2 + d].unsqueeze(2).to_broadcast([P, UN, P]), ALU.mult)
                    last = dve.tensor_tensor(KL[:, d], tp[:, 1], tail[:, d].unsqueeze(2).to_broadcast([P, UN, P]), ALU.mult)
                last.then_inc(S["g_vkc"], 1)
                dve.wait_ge(S["g_vkc"], i + 1)
                invert_dve(dve, S, "g_", i, LEVELS, T, Xs, xu, lmask)
                no = 0
                for j in range(UN):
                    for d in range(2):
                        u = G_ORDER[d][j]
                        dve.wait_ge(S["g_w"], i * 12 + 2 * j + d + 1)
                        dve.tensor_tensor(W[:, d], bV[:, d, u], xu[d][:, 0:P], ALU.subtract).then_inc(S["g_wc"], 1)
                    for d in range(2):
                        u = G_ORDER[d][j]
                        c = gcol(u) + (0 if d else P - 1)
                        dve.wait_ge(S["g_ds"], i * 12 + 2 * j + d + 1)
                        if u < 4:
                            o = oT[:, u * P:u * P + P]
                            if no:
                                dve.wait_ge(S["g_o"], i * 8 + no)
                            dve.tensor_tensor(o, o, xu[d][:, 3 * P:4 * P], ALU.add).then_inc(S["g_o"], 1)
                            no += 1
                        dve.scalar_tensor_tensor(St[:, d], St[:, d], EG[:, d, c:c + 1], xu[d][:, 2 * P:3 * P],
                                                 ALU.mult, ALU.add).then_inc(S["g_s"], 1)
                dve.wait_ge(S["g_rt"], i * 4 + 4)
                dve.wait_ge(S["g_o"], i * 8 + 8)
                link(dve.reciprocal(nr[:, 0:1, 0:LAT], nr[:, 0:1, 0:LAT]))
                link(dve.tensor_tensor(oT[:], oT[:], nr[:, 0, 0:LAT], ALU.mult))
                dve.wait_ge(S["g_st"], 1 + i * 16)
                dve.scalar_tensor_tensor(ybuf[:], oT[:], hp[:, 15:16], zs[:], ALU.mult, ALU.mult).then_inc(S["g_y"], 1)
                e["counts"]["DV_G"] = n[0]

            with dve.Fori(0, GH - 1) as i:
                turn(i)
            turn(GH - 1)


def mix(dve, link, out, x, c, n_part=P, ctx=True, done=None):
    p = slice(0, n_part)
    lat_o, lat_x = out[p, 0:LAT], x[p, 0:LAT]
    link(dve.tensor_scalar(out[p, 0:TOK if ctx else LAT], x[p, 0:TOK if ctx else LAT], c[p, 0:1], None, ALU.mult))
    grid_o, grid_x = (v.rearrange("p (r w) -> p r w", w=64) for v in (lat_o, lat_x))
    pairs = [(grid_o[:, :, 1:64], grid_x[:, :, 0:63], 1), (grid_o[:, :, 0:63], grid_x[:, :, 1:64], 2),
             (lat_o[:, 64:LAT], lat_x[:, 0:LAT - 64], 3), (lat_o[:, 0:LAT - 64], lat_x[:, 64:LAT], 4)]
    if ctx:
        pairs += [(out[p, LAT + 1:TOK], x[p, LAT:TOK - 1], 5), (out[p, LAT:TOK - 1], x[p, LAT + 1:TOK], 6)]
    for o, s, k in pairs:
        ins = dve.scalar_tensor_tensor(o, s, c[p, k:k + 1], o, ALU.mult, ALU.add)
        if done is None or k < pairs[-1][2]:
            link(ins)
        else:
            ins.then_inc(done, 1)


def phase_lora(nc, e):
    io, carve, S, pj, pr, RP, ring, hT = (e[k] for k in ("io", "carve", "S", "pj", "pr", "RP", "ring", "hT"))
    w_loaded, w_used = e["w_loaded"], e["w_used"]
    lora = carve(4, TOK)
    raw = carve(4, TOK)
    lc = carve(4, 7)
    half = io["base_l"]
    C, cst = e["C"], e["cst"]

    with nc.Block() as block:
        @block.sync
        def _(sp):
            for n in range(8):
                sp.wait_ge(w_used, half + n - RING + 1)
                sp.dma_start(ring[:, n % RING, :, 0:LORA], io["w_l"][n // 2, :, n % 2 * HK:(n % 2 + 1) * HK]).then_inc(w_loaded[n % RING], 16)

        @block.tensor
        def _(pe):
            for j in range(4):
                if j:
                    pe.wait_ge(S["l_raw"], 2 * j)
                for hf in range(2):
                    s = (2 * j + hf) % RING
                    pe.wait_ge(w_loaded[s], loads(half) + (j // 2 + 1) * 16)
                    for k in range(HK):
                        kk = hf * HK + k
                        pe.matmul(pj[0][0:LORA, 0:LAT], ring[:, s, k, 0:LORA], hT[:, kk, 0:LAT], start=kk == 0, stop=kk == KT - 1)
                        last = pe.matmul(pj[2][0:LORA, 0:CTX], ring[:, s, k, 0:LORA], hT[:, kk, LAT:TOK],
                                         start=kk == 0, stop=kk == KT - 1)
                    last.then_inc(w_used, 1)

        @block.scalar
        def _(act):
            for j in range(4):
                act.wait_ge(w_used, half + 2 * j + 2)
                act.activation(raw[0:LORA, j, 0:LAT], pj[0][0:LORA, 0:LAT], ACT.Copy).then_inc(S["l_raw"], 1)
                act.activation(raw[0:LORA, j, LAT:TOK], pj[2][0:LORA, 0:CTX], ACT.Copy).then_inc(S["l_raw"], 1)
            for j in range(2):
                act.wait_ge(S["l_mix"], j + 1)
                act.activation(lora[0:LORA, j], lora[0:LORA, j], ACT.Tanh).then_inc(S["l_th"], 1)
            act.wait_ge(S["l_th"], 2)

        @block.vector
        def _(dve):
            n = [0]

            def link(ins):
                n[0] += 1
                ins.then_inc(S["l_v"], 1)
                dve.wait_ge(S["l_v"], n[0])

            kinds = cst[:, C["kinds"]:C["kinds"] + 24 * 7].rearrange("p (h j k) -> p h j k", h=8, k=7)
            mu = pr("mu", 24).rearrange("p (h j) -> p h j", h=8)
            for j in range(3):
                tab = RP[:, :, 7 * j:7 * j + 7]
                link(dve.tensor_tensor(tab, kinds[:, :, j], mu[:, :, j:j + 1].to_broadcast([P, 8, 7]), ALU.mult))
                link(dve.tensor_scalar(tab[:, :, 0:1], tab[:, :, 0:1], 1.0, None, ALU.add))
            link(dve.tensor_copy(RP[:, :, R_W0:R_NPAR], pr("rp", 80).rearrange("p (h c) -> p h c", h=8)))
            link(dve.tensor_scalar(RP[:, :, R_KA1:R_KA1 + 1], RP[:, :, R_KA:R_KA + 1], -1.0, 1.0, ALU.mult, ALU.add))
            lk = cst[:, C["lkinds"]:C["lkinds"] + 7]
            for j in range(4):
                link(dve.tensor_scalar(lc[:, j], lk, pr("mul", 4)[:, j:j + 1], None, ALU.mult))
                link(dve.tensor_scalar(lc[:, j, 0:1], lc[:, j, 0:1], 1.0, None, ALU.add))
            for j in range(4):
                dve.wait_ge(S["l_raw"], 2 * j + 2)
                mix(dve, link, lora[:, j], raw[:, j], lc[:, j], LORA, done=S["l_mix"])
            dve.wait_ge(S["l_mix"], 4)


def r_slots(d, hh):
    return sorted(R_ORDER[d][6 * hh:6 * hh + 6])


def r_segs(d, hh):
    s, out = r_slots(d, hh), []
    for n, c in enumerate(s):
        if n and s[n - 1] == c - 1:
            out[-1][1] += 64
        else:
            out.append([64 * c, 64, n])
    return out


def phase_rwkv(nc, e):
    io, carve, S, pj, xu, tp, ident, blk, istk, lmask, incl, strict, rst, RP = (
        e[k] for k in ("io", "carve", "S", "pj", "xu", "tp", "ident", "blk", "istk", "lmask", "incl", "strict", "rst", "RP"))
    ydram, w_used = e["ydram"], e["w_used"]
    LV = LEVELS - 1
    lora = carve(4, TOK)
    tmp = carve(7, 384)
    sg, av, cs, gi, gn, bb, kd = (tmp[:, k] for k in range(7))
    flat = tmp.rearrange("p a b -> p (a b)")
    raw = [flat[:, 0:LAT], flat[:, LAT:LAT + TOK], flat[:, LAT + TOK:LAT + 2 * TOK]]
    sq, nr = flat[:, 0:TOK], flat[:, TOK:2 * TOK]
    r, k, v, z = carve(LAT), carve(TOK), carve(TOK), carve(LAT)
    kk = carve(TOK)
    KX, BX, CX, RX = carve(2, UN, P), carve(2, UN, P), carve(2, UN, P), carve(2, UN, P)
    VX = carve(12, P)
    V = carve(12, 64)
    BT, CT = carve(2, UN, P), carve(2, UN, P)
    LT, T, TT = carve(2, UN, P), carve(2, UN, P), carve(2, UN, P)
    Xs = carve(2, UN, 64)
    LC, MB, MC = carve(2, UN, P), carve(2, UN, P), carve(2, UN, P)
    lw = carve(2, 2, P)
    kds = carve(LAT)
    O = carve(8, 64)
    W, SA, St = carve(2, 64), carve(2, 64), carve(2, 64)
    egc = carve(2, UN)
    rp = carve(R_NPAR)
    mean = carve(8)
    eps = carve(2)
    ybuf = T[:, 0, 0:4].rearrange("p a b -> p (a b)")
    zs = T[:, 1, 0:4].rearrange("p a b -> p (a b)")
    bon = TT[:, 0, 0:4].rearrange("p a b -> p (a b)")
    osq = TT[:, 1, 0:4].rearrange("p a b -> p (a b)")
    yT = tp[:, 1, 0:4].rearrange("p a b -> p (a b)")
    half = io["base_r"]
    wb = loads(half)
    DV = io["DV_R"]

    def diag(view, h):
        return view[64 * h:64 * h + 64, :, 64 * h:64 * h + 64]

    def chunked(view, h):
        return view[64 * h:64 * h + 64].rearrange("p (u t) -> p u t", t=64)

    unused = e["unused"]
    with nc.Block() as block:
        @block.gpsimd
        def _(pool):
            for n, name in enumerate(("r_y", "r_st", "r_raw")):
                pool.memset(unused[:, n:n + 1], 0.0).then_inc(S[name], 1)

        @block.sync
        def _(sp):
            def lora_up(i):
                sp.dma_start(lw[0:LORA].rearrange("p a b c -> p (a b c)"), io["w_lup"][bass.ds(i, 1)].rearrange("a p c -> p (a c)")).then_inc(S["r_lw"], 16)

            lora_up(0)
            load_tiles(sp, e, io["w_r"], half, 0, 0, 6)
            with sp.Fori(0, PAIRS - 1) as i:
                load_tiles(sp, e, io["w_r"], half, i, 6, 8)
                load_tiles(sp, e, io["w_r"], half, i + 1, 0, 4)
                sp.wait_ge(S["r_lo"], i * 4 + 4)
                lora_up(i + 1)
                load_tiles(sp, e, io["w_r"], half, i + 1, 4, 6)
            load_tiles(sp, e, io["w_r"], half, PAIRS - 1, 6, 8)

        @block.tensor
        def _(pe):
            def column(i, j, k0=0, k1=KT):
                if k0 == 0:
                    pe.wait_ge(S["r_raw"], 1 + i * 6 + (0, 1, 3, 5)[j])
                project(pe, e, i, j, wb, pj[0][:, 0:LAT], pj[2][:, 0:CTX] if j in (1, 2) else None, k0, k1)

            def turn(i, more):
                def fill_products(n):
                    if more:
                        column(i + 1, 0, 4 * n, 4 * n + 4)

                def fill(n):
                    if more and 3 <= n < 3 * LV:
                        column(i + 1, 1, n - 3, n - 2)
                        if n == 3 * LV - 1:
                            column(i + 1, 1, n - 2, KT)

                def fill_scan(n):
                    if more and n < KT:
                        column(i + 1, 2, n, n + 1)

                column(i, 3)
                pe.wait_ge(S["r_y"], 1 + i)
                pe.wait_ge(S["r_sq"], i * 2 + 1)
                pe.matmul(xu[0][:, 0:LAT], blk, sq[:, 0:LAT], start=True, stop=True)
                pe.matmul(xu[1][:, 0:CTX], blk, sq[:, LAT:TOK], start=True, stop=True).then_inc(S["r_ss"], 1)
                pe.wait_ge(S["r_vx"], i * 2 + 2)
                vt = tp[:, 0].rearrange("p u t -> p (u t)")
                for c in range(12):
                    last = pe.matmul(vt[:, 64 * c:64 * c + 64], VX[:, c], istk, start=True, stop=True)
                last.then_inc(S["r_vt"], 1)
                pe.wait_ge(S["r_lw"], i * 16 + 16)
                pe.wait_ge(S["r_kk"], i + 1)
                pe.wait_ge(S["r_vc"], i + 1)
                pe.wait_ge(S["r_raw"], 1 + i * 6 + 6)
                for hh in range(2):
                    m = i * 2 + hh
                    nl = 2 if hh == 0 else 6
                    for d in range(2):
                        if hh * 2 + d:
                            pe.wait_ge(S["r_sg"], i * 8 + (hh * 2 + d) * 2)
                        for q in range(2):
                            for t0, nt, s0 in r_segs(d, hh):
                                last = pe.matmul(pj[2 * q][:, 64 * s0:64 * s0 + nt], lw[0:LORA, d, q], lora[0:LORA, 2 * q + d, t0:t0 + nt],
                                                 start=True, stop=True)
                        last.then_inc(S["r_lo"], 1)
                    for d in range(2):
                        pe.wait_ge(S["r_xd"], m * 2 + d + 1)
                        for u in range(UN):
                            last = pe.matmul(tp[:, d, u], BX[:, d, u], KX[:, d, u], start=True, stop=True)
                        last.then_inc(S["r_p"], 1)
                        for u in range(UN):
                            last = pe.matmul(xu[d][:, u * 64:u * 64 + 64], KX[:, d, u], BX[:, d, u, d:P:2], start=True, stop=True)
                        last.then_inc(S["r_l0"], 1)
                    if hh:
                        pe.wait_ge(S["r_sg"], i * 8 + 8)
                        fill_products(0)
                    for d in range(2):
                        pe.wait_ge(S["r_pa"], m * 6 + d + 1)
                        for u in range(UN):
                            last = pe.transpose(tp[:, d, u], BX[:, d, u], ident)
                        last.then_inc(S["r_p"], 1)
                    if hh:
                        fill_products(1)
                    for d in range(2):
                        pe.wait_ge(S["r_pa"], m * 6 + 2 + d + 1)
                        for u in range(UN):
                            last = pe.transpose(tp[:, d, u], CX[:, d, u], ident)
                        last.then_inc(S["r_p"], 1)
                    if hh:
                        fill_products(2)
                    for d in range(2):
                        pe.wait_ge(S["r_pa"], m * 6 + 4 + d + 1)
                        for u in range(UN):
                            last = pe.matmul(tp[:, d, u], CX[:, d, u], KX[:, d, u], start=True, stop=True)
                        last.then_inc(S["r_q"], 1)
                    for d in range(2):
                        pe.wait_ge(S["r_pd"], m * 6 + d + 1)
                        for u in range(nl):
                            last = pe.matmul(tp[:, d, u], BX[:, d, u], RX[:, d, u], start=True, stop=True)
                        last.then_inc(S["r_q"], 1)
                    if hh:
                        fill_products(3)
                    for d in range(2):
                        pe.wait_ge(S["r_pd"], m * 6 + 2 + d + 1)
                        for u in range(nl):
                            last = pe.matmul(tp[:, d, u], CX[:, d, u], RX[:, d, u], start=True, stop=True)
                        last.then_inc(S["r_q"], 1)
                    pe.wait_ge(S["r_pd"], m * 6 + 6)
                    invert_pe(pe, S, "r_", m, LV, LT, T, TT, Xs, xu, tp, ident, fill if hh else None)
                    for j in range(UN):
                        for d in range(2):
                            c = R_ORDER[d][6 * hh + j]
                            u = r_slots(d, hh).index(c)
                            if j == 0:
                                pe.wait_ge(S["r_tt"], m * 2 * LV + 2 * (LV - 1) + d + 1)
                            pe.wait_ge(S["r_s"], i * 26 + hh * 12 + 2 * j + d + 1)
                            pe.matmul(xu[d][:, 0:64], LC[:, d, u], V[:, c], start=True, stop=False)
                            pe.matmul(xu[d][:, 0:64], KX[:, d, u], St[:, d], start=False, stop=True).then_inc(S["r_w"], 1)
                        if hh:
                            fill_scan(3 * j)
                        for d in range(2):
                            u = r_slots(d, hh).index(R_ORDER[d][6 * hh + j])
                            pe.wait_ge(S["r_wc"], m * 12 + 2 * j + d + 1)
                            pe.matmul(xu[d][:, 64:128], TT[:, d, u], W[:, d], start=True, stop=True).then_inc(S["r_sa"], 1)
                        if hh:
                            fill_scan(3 * j + 1)
                        for d in range(2):
                            c = R_ORDER[d][6 * hh + j]
                            u = r_slots(d, hh).index(c)
                            pe.wait_ge(S["r_sac"], m * 12 + 2 * j + d + 1)
                            pe.matmul(xu[d][:, 128:192], BT[:, d, u], SA[:, d], start=True, stop=False)
                            last = pe.matmul(xu[d][:, 128:192], CT[:, d, u], V[:, c], start=False, stop=True)
                            if c < 8:
                                pe.matmul(xu[d][:, 192:256], RX[:, d, u], St[:, d], start=True, stop=False)
                                pe.matmul(xu[d][:, 192:256], MB[:, d, u], SA[:, d], start=False, stop=False)
                                last = pe.matmul(xu[d][:, 192:256], MC[:, d, u], V[:, c], start=False, stop=True)
                            last.then_inc(S["r_ds"], 1)
                        if hh:
                            fill_scan(3 * j + 2)
                pe.wait_ge(S["r_rk"], i + 1)
                pe.matmul(pj[1][:, 0:LAT], blk, bon, start=True, stop=True).then_inc(S["r_bs"], 1)
                pe.wait_ge(S["r_yx"], i * 2 + 2)
                for c in range(8):
                    last = pe.matmul(yT[:, 64 * c:64 * c + 64], VX[:, c], istk, start=True, stop=True)
                last.then_inc(S["r_yt"], 1)

            for j in range(3):
                column(0, j)
            with pe.Fori(0, PAIRS - 1) as i:
                turn(i, True)
            turn(PAIRS - 1, False)

        @block.scalar
        def _(act):
            act.wait_ge(S["r_v0"], 7)
            dsts = [[raw[0]], [raw[1][:, 0:LAT], raw[1][:, LAT:TOK]], [raw[2][:, 0:LAT], raw[2][:, LAT:TOK]], [z]]

            def copy_column(i, j):
                act.wait_ge(w_used, half + i * 8 + 2 * j + 2)
                act.activation(dsts[j][0], pj[0][:, 0:LAT], ACT.Copy).then_inc(S["r_raw"], 1)
                if j in (1, 2):
                    act.activation(dsts[j][1], pj[2][:, 0:CTX], ACT.Copy).then_inc(S["r_raw"], 1)

            def turn(i, more):
                copy_column(i, 3)
                act.wait_ge(S["r_kr"], i + 1)
                act.activation(sq, kk[:], ACT.Square).then_inc(S["r_sq"], 1)
                for h in range(2):
                    act.activation(diag(VX, h), chunked(v, h), ACT.Copy).then_inc(S["r_vx"], 1)
                act.wait_ge(S["r_ss"], i + 1)
                act.activation(nr[:, 0:LAT], xu[0][:, 0:LAT], ACT.Sqrt, bias=eps[:, 0:1]).then_inc(S["r_rt"], 1)
                act.activation(nr[:, LAT:TOK], xu[1][:, 0:CTX], ACT.Sqrt, bias=eps[:, 0:1]).then_inc(S["r_rt"], 1)
                act.wait_ge(S["r_vt"], i + 1)
                act.activation(V[:].rearrange("p c t -> p (c t)"), tp[:, 0].rearrange("p u t -> p (u t)"), ACT.Copy).then_inc(S["r_vc"], 1)
                act.wait_ge(S["r_kk"], i + 1)
                for hh in range(2):
                    m = i * 2 + hh
                    for d in range(2):
                        act.wait_ge(S["r_lo"], m * 2 + d + 1)
                        if hh * 2 + d:
                            act.wait_ge(S["r_xd"], m * 2 + d)
                        act.activation(sg, pj[0][:, 0:384], ACT.Sigmoid, bias=rp[:, R_W0 + d:R_W0 + d + 1]).then_inc(S["r_sg"], 1)
                        act.activation(av, pj[2][:, 0:384], ACT.Sigmoid, bias=rp[:, R_A0 + d:R_A0 + d + 1]).then_inc(S["r_sg"], 1)
                        act.wait_ge(S["r_cs"], m * 2 + d + 1)
                        act.activation(gi, cs, ACT.Exp, scale=-EXPM).then_inc(S["r_ex"], 1)
                        act.activation(gn, cs, ACT.Exp, scale=EXPM).then_inc(S["r_ex"], 1)
                        act.activation(sg, sg, ACT.Exp, scale=-EXPM).then_inc(S["r_ex"], 1)
                    for q, dst in enumerate((LT, BT, CT)):
                        for d in range(2):
                            act.wait_ge(S["r_p"], m * 6 + 2 * q + d + 1)
                            act.activation(dst[:, d], tp[:, d], ACT.Copy).then_inc(S["r_pa"], 1)
                    if hh and more:
                        act.wait_ge(S["r_xd"], i * 4 + 4)
                        copy_column(i + 1, 0)
                    invert_act(act, S, "r_", m, LV, TT, tp)
                    if hh and more:
                        copy_column(i + 1, 1)
                    for j in range(UN):
                        for d in range(2):
                            act.wait_ge(S["r_w"], m * 12 + 2 * j + d + 1)
                            if j:
                                act.wait_ge(S["r_sa"], m * 12 + 2 * (j - 1) + d + 1)
                            act.activation(W[:, d], xu[d][:, 0:64], ACT.Copy, scale=-1.0).then_inc(S["r_wc"], 1)
                if more:
                    copy_column(i + 1, 2)
                act.wait_ge(S["r_oc"], i + 1)
                act.activation(osq, O[:].rearrange("p c t -> p (c t)"), ACT.Square).then_inc(S["r_sq"], 1)
                act.wait_ge(S["r_vr"], i + 1)
                act.activation(mean[:], mean[:], ACT.Sqrt, bias=eps[:, 1:2], scale=1.0 / 64).then_inc(S["r_sd"], 1)
                act.activation(zs, z[:], ACT.Sigmoid).then_inc(S["r_zs"], 1)
                act.wait_ge(S["r_y"], 1 + i + 1)
                act.dma_start(ydram[bass.ds(i + 8, 1)].rearrange("a p t -> p (a t)"), ybuf).then_inc(S["r_st"], 16)

            for j in range(3):
                copy_column(0, j)
            with act.Fori(0, PAIRS - 1) as i:
                turn(i, True)
            turn(PAIRS - 1, False)
            act.wait_ge(S["r_st"], 1 + 16 * PAIRS)

        @block.vector
        def _(dve):
            dve.memset(eps[:, 0:1], 1e-6).then_inc(S["r_v0"], 1)
            dve.memset(eps[:, 1:2], 64e-5).then_inc(S["r_v0"], 1)
            for t in (KX, BX, CX, RX, VX):
                dve.memset(t[:], 0.0).then_inc(S["r_v0"], 1)
            dve.wait_ge(S["r_v0"], 7)

            def turn(i):
                dve.wait_ge(S["r_y"], 1 + i)
                n = [0]

                def link(ins):
                    n[0] += 1
                    ins.then_inc(S["r_v"], 1)
                    dve.wait_ge(S["r_v"], i * DV + n[0])

                link(dve.tensor_copy(rp[:], RP[:, bass.ds(i, 1)].rearrange("p a c -> p (a c)")))
                for d in range(2):
                    dve.memset(St[:, d], 0.0).then_inc(S["r_s"], 1)
                link(dve.memset(O[:], 0.0))
                link(dve.memset(kds[:], 0.0))
                for j, dst in enumerate((r, k, v)):
                    dve.wait_ge(S["r_raw"], 1 + i * 6 + (1, 3, 5)[j])
                    mix(dve, link, dst, raw[j], rp[:, 7 * j:7 * j + 7], ctx=j > 0)
                dve.tensor_scalar(kk[:], k[:], rp[:, R_KK:R_KK + 1], None, ALU.mult).then_inc(S["r_kr"], 1)
                dve.wait_ge(S["r_kr"], i + 1)
                dve.wait_ge(S["r_rt"], i * 2 + 2)
                link(dve.reciprocal(nr, nr))
                dve.tensor_tensor(kk[:], kk[:], nr, ALU.mult).then_inc(S["r_kk"], 1)
                dve.wait_ge(S["r_kk"], i + 1)
                for hh in range(2):
                    m = i * 2 + hh
                    nl = 2 if hh == 0 else 6
                    for d in range(2):
                        back = slice(None, None, -1 if d else 1)
                        dve.wait_ge(S["r_sg"], m * 4 + 2 * d + 2)
                        link(dve.tensor_tensor_scan(cs[:, back], rst[d][:, back], sg[:, back], 0.0, ALU.mult, ALU.add))
                        dve.tensor_tensor(sg, cs, sg, ALU.subtract).then_inc(S["r_cs"], 1)
                        link(dve.tensor_scalar(kd, av, rp[:, R_KA:R_KA + 1], rp[:, R_KA1:R_KA1 + 1], ALU.mult, ALU.add))
                        for t0, nt, s0 in r_segs(d, hh):
                            o = slice(64 * s0, 64 * s0 + nt)
                            dve.tensor_tensor(bb[:, o], kk[:, t0:t0 + nt], av[:, o], ALU.mult)
                            link(dve.tensor_tensor(kd[:, o], kd[:, o], k[:, t0:t0 + nt], ALU.mult))
                            if t0 < LAT:
                                w = min(nt, LAT - t0)
                                link(dve.tensor_tensor(kds[:, t0:t0 + w], kds[:, t0:t0 + w], kd[:, 64 * s0:64 * s0 + w], ALU.add))
                        dve.wait_ge(S["r_ex"], m * 6 + 3 * d + 3)
                        for h in range(2):
                            dve.tensor_tensor(diag(BX[:, d], h), chunked(bb, h), chunked(gn, h), ALU.mult)
                            dve.tensor_tensor(diag(CX[:, d], h), chunked(kd, h), chunked(gn, h), ALU.mult)
                            for t0, nt, s0 in r_segs(d, hh):
                                us = slice(s0, s0 + nt // 64)
                                dve.tensor_tensor(diag(KX[:, d], h)[:, us], chunked(kk, h)[:, t0 // 64:(t0 + nt) // 64],
                                                  chunked(sg, h)[:, us], ALU.mult)
                            t0 = r_segs(d, hh)[0][0]
                            dve.tensor_tensor(diag(RX[:, d], h)[:, 0:nl], chunked(r, h)[:, t0 // 64:t0 // 64 + nl],
                                              chunked(gi, h)[:, 0:nl], ALU.mult)
                        end = 0 if d else 63
                        dve.tensor_copy(egc[:, d], gi[:, end:384:64]).then_inc(S["r_xd"], 1)
                    dve.wait_ge(S["r_st"], 1 + i * 16)
                    for d in range(2):
                        link(dve.tensor_copy(T[:, d], ident.unsqueeze(1).to_broadcast([P, UN, P])))
                        dve.wait_ge(S["r_l0"], m * 2 + d + 1)
                        link(dve.tensor_tensor(Xs[:, d], xu[d][:, 0:384].rearrange("p (u c) -> p u c", u=UN),
                                               lmask(0, d).unsqueeze(1).to_broadcast([P, UN, 64]), ALU.mult))
                        w = T[:, d, :, d:P:2]
                        dve.tensor_tensor(w, w, Xs[:, d], ALU.add).then_inc(S["r_t"], 1)
                    for q, (dst, mask, nu) in enumerate(((LC, strict, UN), (MB, incl, nl), (MC, incl, nl))):
                        for d in range(2):
                            dve.wait_ge(S["r_q"], m * 6 + 2 * q + d + 1)
                            dve.tensor_tensor(dst[:, d, 0:nu], tp[:, d, 0:nu], mask[d].unsqueeze(1).to_broadcast([P, nu, P]),
                                              ALU.mult).then_inc(S["r_pd"], 1)
                    invert_dve(dve, S, "r_", m, LV, T, Xs, xu, lmask)
                    for j in range(UN):
                        for d in range(2):
                            dve.wait_ge(S["r_sa"], m * 12 + 2 * j + d + 1)
                            dve.tensor_copy(SA[:, d], xu[d][:, 64:128]).then_inc(S["r_sac"], 1)
                        for d in range(2):
                            c = R_ORDER[d][6 * hh + j]
                            u = r_slots(d, hh).index(c)
                            dve.wait_ge(S["r_ds"], m * 12 + 2 * j + d + 1)
                            if c < 8:
                                link(dve.tensor_tensor(O[:, c], O[:, c], xu[d][:, 192:256], ALU.add))
                            link(dve.tensor_tensor(St[:, d], St[:, d], xu[d][:, 128:192], ALU.add))
                            dve.tensor_scalar(St[:, d], St[:, d], egc[:, d, u:u + 1], None, ALU.mult).then_inc(S["r_s"], 1)
                link(dve.tensor_reduce(mean[:], O[:], AX_X, ALU.add))
                link(dve.tensor_scalar(mean[:], mean[:], 1.0 / 64, None, ALU.mult))
                dve.tensor_tensor(O[:], O[:], mean.unsqueeze(2).to_broadcast([P, 8, 64]), ALU.subtract).then_inc(S["r_oc"], 1)
                link(dve.tensor_tensor(bon, r[:], kds[:], ALU.mult))
                dve.tensor_scalar(bon, bon, rp[:, R_RK:R_RK + 1], None, ALU.mult).then_inc(S["r_rk"], 1)
                dve.wait_ge(S["r_oc"], i + 1)
                dve.wait_ge(S["r_sq"], i * 2 + 2)
                dve.tensor_reduce(mean[:], osq.rearrange("p (c t) -> p c t", t=64), AX_X, ALU.add).then_inc(S["r_vr"], 1)
                dve.wait_ge(S["r_sd"], i + 1)
                link(dve.reciprocal(mean[:], mean[:]))
                for h in range(2):
                    hs = slice(64 * h, 64 * h + 64)
                    dve.tensor_tensor(diag(VX[:, 0:8], h), O[hs], mean[hs].unsqueeze(2).to_broadcast([64, 8, 64]), ALU.mult).then_inc(S["r_yx"], 1)
                dve.wait_ge(S["r_bs"], i + 1)
                link(dve.tensor_tensor(kds[:], v[:, 0:LAT], pj[1][:, 0:LAT], ALU.mult))
                dve.wait_ge(S["r_zs"], i + 1)
                link(dve.tensor_tensor(z[:], z[:], zs, ALU.mult))
                dve.wait_ge(S["r_yt"], i + 1)
                link(dve.scalar_tensor_tensor(kds[:], yT, rp[:, R_GG:R_GG + 1], kds[:], ALU.mult, ALU.add))
                dve.scalar_tensor_tensor(ybuf, kds[:], rp[:, R_GB:R_GB + 1], z[:], ALU.add, ALU.mult).then_inc(S["r_y"], 1)
                e["counts"]["DV_R"] = n[0]

            with dve.Fori(0, PAIRS - 1) as i:
                turn(i)
            turn(PAIRS - 1)


def stream(sp, e, src, half, tiles):
    ring, w_loaded, w_used = e["ring"], e["w_loaded"], e["w_used"]
    with sp.Fori(0, tiles // 2) as i:
        for s in range(RING):
            sp.wait_ge(w_used, half + (i - 1) * RING + s + 1)
            sp.dma_start(ring[:, s], src[bass.ds(i * 2 + s // 2, 1), :, (s % 2) * HK:(s % 2 + 1) * HK]
                         .rearrange("a p k c -> p (a k) c")).then_inc(w_loaded[s], 16)


def column_tile(pe, e, lat, s0, loaded):
    ring, hT, w_loaded, w_used = e["ring"], e["hT"], e["w_loaded"], e["w_used"]
    for hf in range(2):
        pe.wait_ge(w_loaded[s0 + hf], loaded)
        for k in range(HK):
            kk = hf * HK + k
            last = pe.matmul(lat, ring[:, s0 + hf, k], hT[:, kk, 0:LAT], start=kk == 0, stop=kk == KT - 1)
        last.then_inc(w_used, 1)


def phase_out(nc, e):
    io, hT, carve, S, pj, gate, mod2, pr, ones = (e[k] for k in ("io", "hT", "carve", "S", "pj", "gate", "mod2", "pr", "ones"))
    ydram, w_used, bias_rows, cst, C = e["ydram"], e["w_used"], e["bias_rows"], e["cst"], e["C"]
    X = carve(KT, LAT)
    sq = carve(2, LAT)
    rstd = carve(LAT)
    eps = carve(1)
    scl = carve(KT)
    rel = carve(384)
    win = carve(768)
    half = io["base_o"]
    wb = loads(half)

    unused = e["unused"]
    with nc.Block() as block:
        @block.gpsimd
        def _(pool):
            for n, name in enumerate(("o_r",)):
                pool.memset(unused[:, n:n + 1], 0.0).then_inc(S[name], 1)

        @block.sync
        def _(sp):
            for q in range(4):
                sp.dma_start(hT[:, 4 * q:4 * q + 4, 0:LAT], ydram[4 * q:4 * q + 4].rearrange("k p t -> p k t")).then_inc(S["o_y"], 16)
            stream(sp, e, io["w_out"], half, KT)

        @block.scalar
        def _(act):
            act.dma_start(win[0:32], io["win"]).then_inc(S["o_w"], 16)
            act.dma_start(X[:], io["xT"]).then_inc(S["o_x"], 16)
            with act.Fori(0, KT // 2) as i:
                for t in range(2):
                    act.wait_ge(S["o_r"], 1 + i * 2 + t + 1)
                    act.wait_ge(S["o_ss"], i * 2 + 1)
                    act.activation(sq[:, t], X[:, bass.ds(i * 2 + t, 1)].rearrange("p a t -> p (a t)"), ACT.Square).then_inc(S["o_sq"], 1)
            act.wait_ge(S["o_ss"], KT + 1)
            act.wait_ge(S["o_v"], 1)
            act.activation(rstd[:], pj[2][:, 0:LAT], ACT.Sqrt, bias=eps[:], scale=1.0 / D).then_inc(S["o_rt"], 1)
            for k in range(KT):
                act.wait_ge(S["o_n"], k + 1)
                act.activation(hT[:, k, 0:LAT], X[:, k], ACT.Identity, bias=mod2[:, k:k + 1], scale=scl[:, k:k + 1]).then_inc(S["o_h"], 1)
            act.wait_ge(S["o_h"], KT)
            act.wait_ge(S["o_b"], 1)
            act.dma_start(bias_rows, rel[0:16]).then_inc(S["o_bd"], 16)
            act.wait_ge(S["o_bd"], 16)
            copies = bass.AP(tensor=e["bias_copies_t"], offset=0, ap=[[P * 384, 16], [384, P], [1, 384]])
            rows = bass.AP(tensor=bias_rows.tensor, offset=0, ap=[[384, 16], [0, P], [1, 384]])
            act.dma_start(copies, rows).then_inc(S["o_bd"], 16)
            act.wait_ge(S["o_bd"], 32)
            skew = bass.AP(tensor=e["bias_copies_t"], offset=127, ap=[[383, P], [P * 384, 16], [1, 256]])
            act.dma_start(hT[:, :, LAT:TOK], skew).then_inc(S["o_bd"], 16)
            act.wait_ge(S["o_bd"], 48)

        @block.tensor
        def _(pe):
            pe.wait_ge(S["o_w"], 16)
            pe.matmul(pj[1][0:16, 0:384], pr("rel", 16)[0:32], win[0:32, 0:384], start=True, stop=True).then_inc(S["o_bm"], 1)
            pe.wait_ge(S["o_v"], 2)
            pe.matmul(pj[2][:, 0:LAT], ones, sq[:, 0], start=True, stop=True).then_inc(S["o_ss"], 1)
            pe.wait_ge(S["o_y"], 64)
            with pe.Fori(0, KT // 2) as i:
                for t in range(2):
                    pe.wait_ge(S["o_r"], 1 + i * 2 + t)
                    column_tile(pe, e, pj[0][:, 0:LAT], 2 * t, wb + i * 16 + 16)
                for t in range(2):
                    pe.wait_ge(S["o_sq"], i * 2 + t + 1)
                    pe.matmul(pj[2][:, 0:LAT], ones, sq[:, t], start=False, stop=True,
                              skip_group_check=True).then_inc(S["o_ss"], 1)

        @block.vector
        def _(dve):
            dve.memset(eps[:], 1e-6).then_inc(S["o_v"], 1)
            dve.memset(sq[:, 0], 0.0).then_inc(S["o_v"], 1)
            dve.wait_ge(S["o_bm"], 1)
            dve.tensor_tensor(rel[0:16], pj[1][0:16, 0:384], win[0:16, 384:768], ALU.add).then_inc(S["o_b"], 1)
            dve.wait_ge(S["o_x"], 16)
            with dve.Fori(0, KT // 2) as i:
                for t in range(2):
                    dve.wait_ge(w_used, half + i * RING + 2 * t + 2)
                    x = X[:, bass.ds(i * 2 + t, 1)].rearrange("p a t -> p (a t)")
                    g = gate[:, bass.ds(i * 2 + t, 1)]
                    dve.scalar_tensor_tensor(x, pj[0][:, 0:LAT], g, x, ALU.mult, ALU.add).then_inc(S["o_r"], 1)
            dve.tensor_scalar(scl[:], mod2[:, KT:2 * KT], 1.0, None, ALU.add).then_inc(S["o_v"], 1)
            dve.wait_ge(S["o_rt"], 1)
            dve.reciprocal(rstd[:], rstd[:]).then_inc(S["o_v"], 1)
            dve.wait_ge(S["o_v"], 4)
            for k in range(KT):
                dve.scalar_tensor_tensor(X[:, k], X[:, k], pr("fng", KT)[:, k:k + 1], rstd[:], ALU.mult, ALU.mult).then_inc(S["o_n"], 1)
            dve.wait_ge(S["o_n"], KT)


ALPHA = 2.0 ** 0.25


def phase_two(nc, e):
    io, hT, ring, carve, S, pj, xu, tp8, pr, ones, ident, mod2, out = (
        e[k] for k in ("io", "hT", "ring", "carve", "S", "pj", "xu", "tp8", "pr", "ones", "ident", "mod2", "out"))
    w_loaded, w_used = e["w_loaded"], e["w_used"]
    X = carve(KT, LAT)
    Y = carve(KT, LAT)
    kT = carve(4, LAT)
    V = carve(4, 256)
    uc = carve(8, LAT)
    at0 = e["at"][0]
    ks_buf = carve(LAT)
    qs, vs, ab, sb_ = carve(2, LAT), carve(4, 64), carve(LAT), carve(LAT)
    ub = carve(LAT + 30)
    ca = carve(LAT)
    sc = carve(4, 256)
    pT = carve(8, P)
    at_ = carve(2, LAT)
    ga, gs = carve(LAT), carve(LAT)
    cw, mx, sm, rd, sk, es = carve(2, 32), carve(4), carve(4), carve(4), carve(4), carve(4)
    e["at"][0] = at0
    gcv = carve(8, LAT)
    sq = carve(2, LAT)
    mean, rstd = carve(LAT), carve(LAT)
    sa_ = carve(LAT)
    eps = carve(1)
    graw = carve(2, LAT)
    half = io["base_2"]
    wb = loads(half)
    DV = io["DV_2"]
    bias = hT[:, :, LAT:TOK]
    A = 8
    BODY = 16
    half_g = half + A + 4 * BODY
    half_p = half_g + 16
    half_o = half_p + 8
    SLOT0 = {s: A // RING for s in range(RING)}

    unused = e["unused"]
    with nc.Block() as block:
        @block.gpsimd
        def _(pool):
            for n, name in enumerate(("n_y", "n_cv", "n_ev", "z_g", "z_gm", "z_y", "z_r")):
                pool.memset(unused[:, n:n + 1], 0.0).then_inc(S[name], 1)

        @block.sync
        def _(sp):
            stream(sp, e, io["w_kv"], half, 4)
            sp.wait_ge(S["n_kv"], 2)
            for g in range(4):
                a, b = 64 * (g % 2), 64 - 64 * (g % 2)
                sp.dma_start(kT[b:b + 64, g], kT[a:a + 64, g]).then_inc(S["n_dup"], 16)
            stream(sp, e, io["w_2"], half + A, 32)
            stream(sp, e, io["w_gc"], half_g, 8)
            with sp.Fori(0, 2) as i:
                for s in range(RING):
                    sp.wait_ge(w_used, half_p + (i - 1) * RING + s + 1)
                    sp.dma_start(ring[:, s], io["w_pw"][bass.ds(i * RING + s, 1)].rearrange("a p k c -> p (a k) c")).then_inc(w_loaded[s], 16)
            stream(sp, e, io["w_out2"], half_o, KT)
            for k in range(4):
                sp.wait_ge(S["z_o"], 4 * k + 4)
                sp.dma_start(out[4 * k:4 * k + 4].rearrange("k p t -> p k t"), X[:, 4 * k:4 * k + 4]).then_inc(S["z_st"], 16)
            sp.wait_ge(S["z_st"], 64)

        @block.tensor
        def _(pe):
            P0 = pj[0][:, 0:LAT]
            for j in range(2):
                if j:
                    pe.wait_ge(S["n_kv"], 1)
                column_tile(pe, e, P0, 2 * j, wb + 16)
            pe.wait_ge(S["n_kv"], 2)
            for j in range(2):
                for hf in range(2):
                    pe.wait_ge(w_loaded[2 * j + hf], wb + 32)
                if j:
                    pe.wait_ge(S["n_kv"], 3)
                for t in range(4):
                    for kk in range(KT):
                        last = pe.matmul(pj[0][:, t * P:t * P + P], hT[:, kk, t * P:t * P + P], ring[:, 2 * j + kk // HK, kk % HK],
                                         start=kk == 0, stop=kk == KT - 1)
                        if t == 3 and kk % HK == HK - 1:
                            last.then_inc(w_used, 1)
            pe.wait_ge(S["n_dup"], 64)
            pe.wait_ge(S["n_kv"], 4)
            with pe.Fori(0, 4) as i:
                tiles = [0]

                def tile():
                    t = tiles[0]
                    tiles[0] += 1
                    pe.wait_ge(S["n_ev"], 1 + i * 8 + t)
                    column_tile(pe, e, P0, 2 * (t % 2), wb + A // RING * 16 + (i * 4 + t // 2 + 1) * 16)

                def scores(h):
                    if h >= 2:
                        pe.wait_ge(S["n_at"], i * 2 + h // 2)
                    hs = slice(64 * (h % 2), 64 * (h % 2) + 64)
                    q, k = qs[hs, h // 2], ks[hs]
                    for n in range(4):
                        a = 0 if n else P
                        last = pe.matmul(tp8[:, h % 2].rearrange("p a b -> p (a b)")[:, 256 * n + a:256 * n + 256], q[:, n * P:n * P + P],
                                         k[:, (n - 1) * P + a:(n + 1) * P], start=True, stop=True)
                    last.then_inc(S["n_sc"], 1)

                def turn(h):
                    pe.wait_ge(S["n_p"], i * 4 + h + 1)
                    for n in range(4):
                        for c in range(2):
                            if n or c:
                                last = pe.transpose(xu[n // 2][:, (2 * n + c) % 4 * P:(2 * n + c) % 4 * P + P], sc[:, n, c * P:c * P + P], ident)
                    last.then_inc(S["n_tr"], 1)

                def values(h):
                    pe.wait_ge(S["n_pt"], i * 8 + 2 * h + 2)
                    hs = slice(64 * (h % 2), 64 * (h % 2) + 64)
                    for n in range(4):
                        o = pj[2][hs, n * P:n * P + P]
                        if n:
                            pe.matmul(o, vs[:, n - 1], pT[:, 2 * n], start=True, stop=False)
                        last = pe.matmul(o, vs[:, n], pT[:, 2 * n + 1], start=not n, stop=True)
                    last.then_inc(S["n_pv"], 1)

                ks = ks_buf
                pe.wait_ge(S["n_y"], 1 + i * 2)
                tile()
                tile()
                pe.wait_ge(S["n_ev"], 1 + i * 8 + 2)
                pe.wait_ge(S["n_ks"], i * 2 + 2)
                scores(0)
                tile()
                turn(0)
                scores(1)
                tile()
                values(0)
                turn(1)
                tile()
                values(1)
                scores(2)
                tile()
                turn(2)
                scores(3)
                tile()
                values(2)
                turn(3)
                tile()
                values(3)
            with pe.Fori(0, 4) as i:
                for t in range(2):
                    if t:
                        pe.wait_ge(S["z_g"], 1 + i * 2 + 1)
                    else:
                        pe.wait_ge(S["z_g"], 1 + i * 2)
                        pe.wait_ge(S["n_ev"], 1 + 32)
                    column_tile(pe, e, P0, 2 * t, loads(half_g) + (i + 1) * 16)
            pe.wait_ge(S["n_cv"], 1 + 8)
            for k in range(8):
                last = pe.matmul(pj[2][:, 0:LAT], ones, uc[:, k], start=k == 0, stop=k == 7)
            last.then_inc(S["z_s"], 1)
            for k in range(8):
                pe.wait_ge(S["z_sq"], k + 1)
                last = pe.matmul(pj[2][:, 0:LAT], ones, sq[:, k % 2], start=k == 0, stop=k == 7)
                last.then_inc(S["z_ss"], 1)
            pe.wait_ge(S["z_u"], 8)
            pe.wait_ge(S["z_g"], 1 + 8)
            with pe.Fori(0, 2) as i:
                for t in range(4):
                    pe.wait_ge(S["z_y"], 1 + i * 4 + t)
                    pe.wait_ge(w_loaded[t], loads(half_p) + (i + 1) * 16)
                    for k in range(8):
                        last = pe.matmul(P0, ring[:, t, k], uc[:, k], start=k == 0, stop=k == 7)
                    last.then_inc(w_used, 1)
            pe.wait_ge(S["z_y"], 1 + 8)
            pe.wait_ge(S["n_y"], 1 + 8)
            with pe.Fori(0, KT // 2) as i:
                for t in range(2):
                    pe.wait_ge(S["z_r"], 1 + i * 2 + t)
                    for hf in range(2):
                        s = 2 * t + hf
                        pe.wait_ge(w_loaded[s], loads(half_o) + (i + 1) * 16)
                        for k in range(HK):
                            kk = hf * HK + k
                            last = pe.matmul(P0, ring[:, s, k], Y[:, kk], start=kk == 0, stop=kk == KT - 1)
                        last.then_inc(w_used, 1)
            pe.wait_ge(S["z_r"], 1 + KT)
            for k in range(KT):
                last = pe.matmul(pj[2][:, 0:LAT], ones, X[:, k], start=k == 0, stop=k == KT - 1)
            last.then_inc(S["z_s"], 1)
            for k in range(KT):
                pe.wait_ge(S["z_sq"], 8 + k + 1)
                last = pe.matmul(pj[2][:, 0:LAT], ones, sq[:, k % 2], start=k == 0, stop=k == KT - 1)
                last.then_inc(S["z_ss"], 1)

        @block.scalar
        def _(act):
            P0 = pj[0][:, 0:LAT]
            for j in range(2):
                act.wait_ge(w_used, half + 2 * j + 2)
                for g in (2 * j, 2 * j + 1):
                    a = 64 * (g % 2)
                    last = act.activation(kT[a:a + 64, g], pj[0][a:a + 64, 0:LAT], ACT.Copy)
                last.then_inc(S["n_kv"], 1)
            for j in range(2):
                act.wait_ge(w_used, half + 4 + 2 * j + 2)
                act.activation(V[:, :, j * P:j * P + P], pj[0].rearrange("p (t c) -> p t c", t=4), ACT.Copy).then_inc(S["n_kv"], 1)
            act.wait_ge(S["n_dup"], 64)
            act.wait_ge(S["n_kv"], 4)
            act.activation(X[:], X[:], ACT.Copy, scale=ALPHA).then_inc(S["n_al"], 1)
            act.wait_ge(S["n_al"], 1)
            with act.Fori(0, 4) as i:
                hw = half + A + i * BODY
                act.wait_ge(S["n_y"], 1 + i * 2)
                act.wait_ge(S["n_cv"], 1 + i * 2)
                act.activation(ks_buf, kT[:, bass.ds(i, 1)].rearrange("p a t -> p (a t)"), ACT.Copy).then_inc(S["n_ks"], 1)
                act.activation(vs[:], V[:].rearrange("p t (g c) -> p t g c", g=4)[:, :, bass.ds(i, 1)].rearrange("p t a c -> p t (a c)"),
                               ACT.Copy).then_inc(S["n_ks"], 1)

                def soft(h):
                    act.wait_ge(S["n_m"], i * 4 + h + 1)
                    for n in range(4):
                        act.activation(sc[:, n], sc[:, n], ACT.Exp, bias=mx[:, n:n + 1], accum_out=sm[:, n:n + 1])
                    act.activation(es[:], mx[:], ACT.Exp, bias=sk[:, h:h + 1]).then_inc(S["n_x"], 1)

                def flip(h):
                    act.wait_ge(S["n_tr"], i * 4 + h + 1)
                    if h:
                        act.wait_ge(S["n_pv"], i * 4 + h)
                    act.activation(pT[:, 1:4].rearrange("p a b -> p (a b)"), xu[0][:, P:4 * P], ACT.Copy).then_inc(S["n_pt"], 1)
                    act.activation(pT[:, 4:8].rearrange("p a b -> p (a b)"), xu[1][:], ACT.Copy).then_inc(S["n_pt"], 1)

                def heads(j):
                    act.wait_ge(S["n_pv"], i * 4 + 2 * j + 2)
                    act.activation(at_[:, j], pj[2][:, 0:LAT], ACT.Copy).then_inc(S["n_at"], 1)

                act.wait_ge(w_used, hw + 2)
                act.activation(qs[:, 0], P0, ACT.Copy).then_inc(S["n_ev"], 1)
                act.wait_ge(w_used, hw + 4)
                act.activation(qs[:, 1], P0, ACT.Copy).then_inc(S["n_ev"], 1)
                soft(0)
                act.wait_ge(w_used, hw + 6)
                act.activation(ab[:], P0, ACT.Copy).then_inc(S["n_ev"], 1)
                flip(0)
                soft(1)
                act.wait_ge(w_used, hw + 8)
                act.activation(sb_[:], P0, ACT.Sigmoid).then_inc(S["n_ev"], 1)
                flip(1)
                act.wait_ge(w_used, hw + 10)
                act.wait_ge(S["n_u"], i * 2 + 1)
                act.activation(ab[:], P0, ACT.Copy).then_inc(S["n_ev"], 1)
                heads(0)
                soft(2)
                act.wait_ge(w_used, hw + 12)
                act.activation(sb_[:], P0, ACT.Sigmoid).then_inc(S["n_ev"], 1)
                flip(2)
                soft(3)
                act.wait_ge(w_used, hw + 14)
                act.activation(ga[:], P0, ACT.Copy)
                act.activation(gs[:], P0, ACT.Sigmoid).then_inc(S["n_ev"], 1)
                flip(3)
                heads(1)
                act.wait_ge(w_used, hw + 16)
                act.wait_ge(S["n_y"], 1 + i * 2 + 1)
                act.activation(ga[:], P0, ACT.Copy)
                act.activation(gs[:], P0, ACT.Sigmoid).then_inc(S["n_ev"], 1)
            act.wait_ge(S["n_y"], 1 + 8)
            act.wait_ge(S["n_cv"], 1 + 8)
            with act.Fori(0, 4) as i:
                for t in range(2):
                    act.wait_ge(w_used, half_g + i * RING + 2 * t + 2)
                    act.wait_ge(S["z_gm"], 1 + i * 2 + t)
                    act.activation(graw[:, 0], P0, ACT.Copy)
                    act.activation(graw[:, 1], P0, ACT.Sigmoid).then_inc(S["z_g"], 1)

            def norm_squares(n, view, base):
                for k in range(n):
                    act.wait_ge(S["z_c"], base + k + 1)
                    if base + k >= 2:
                        act.wait_ge(S["z_ss"], base + k - 1)
                    act.activation(sq[:, k % 2], view[:, k], ACT.Square).then_inc(S["z_sq"], 1)
                act.wait_ge(S["z_ss"], base + n)
                act.activation(rstd[:], pj[2][:, 0:LAT], ACT.Sqrt, bias=eps[:], scale=1.0 / (n * P)).then_inc(S["z_rt"], 1)

            norm_squares(8, uc, 0)
            for k in range(8):
                act.wait_ge(S["z_n"], k + 1)
                if k:
                    act.wait_ge(S["z_u"], k)
                act.activation(sa_[:], uc[:, k], ACT.Sigmoid, bias=pr("cln", 16)[:, 8 + k:9 + k], scale=pr("cln", 16)[:, k:k + 1])
                act.activation(uc[:, k], uc[:, k], ACT.Identity, bias=pr("cln", 16)[:, 8 + k:9 + k], scale=pr("cln", 16)[:, k:k + 1]).then_inc(S["z_i"], 1)
            norm_squares(KT, X, 8)
            for k in range(KT):
                act.wait_ge(S["z_n"], 8 + k + 1)
                act.activation(X[:, k], X[:, k], ACT.Identity, bias=pr("ln2", 32)[:, 16 + k:17 + k], scale=pr("ln2", 32)[:, k:k + 1]).then_inc(S["z_o"], 1)

        @block.vector
        def _(dve):
            dve.memset(sc[:], -1e30).then_inc(S["n_v0"], 1)
            dve.memset(ub[:], 0.0).then_inc(S["n_v0"], 1)
            dve.wait_ge(S["n_v0"], 2)
            with dve.Fori(0, 4) as i:
                dve.wait_ge(S["n_y"], 1 + i * 2)
                dve.wait_ge(S["n_cv"], 1 + i * 2)
                n = [0]

                def link(ins):
                    n[0] += 1
                    ins.then_inc(S["n_v"], 1)
                    dve.wait_ge(S["n_v"], i * DV + n[0])

                link(dve.tensor_copy(cw[:], pr("cw2", 8 * 32).rearrange("p (n c) -> p n c", c=32)[:, bass.ds(i * 2, 2)]))
                link(dve.tensor_copy(sk[:], pr("sink", 16)[:, bass.ds(i * 4, 4)]))

                def rows(h):
                    dve.wait_ge(S["n_sc"], i * 4 + h + 1)
                    if h:
                        dve.wait_ge(S["n_tr"], i * 4 + h)
                    b = bias[:, bass.ds(i * 4 + h, 1)]
                    t = tp8[:, h % 2].rearrange("p (n a) b -> p n (a b)", a=2)
                    dve.memset(sc[:, 0, 0:P], -1e30)
                    dve.scalar_tensor_tensor(sc[:, 0, P:256], t[:, 0, P:256], 0.125, b[:, :, P:256].rearrange("p a c -> p (a c)"), ALU.mult, ALU.add)
                    link(dve.scalar_tensor_tensor(sc[:, 1:4], t[:, 1:4], 0.125, b.to_broadcast([P, 3, 256]), ALU.mult, ALU.add))
                    link(dve.tensor_reduce(mx[:], sc[:], AX_X, ALU.max))
                    dve.tensor_scalar(mx[:], mx[:], sk[:, h:h + 1], -1.0, ALU.max, ALU.mult).then_inc(S["n_m"], 1)

                def norm(h):
                    dve.wait_ge(S["n_x"], i * 4 + h + 1)
                    link(dve.tensor_tensor(sm[:], sm[:], es[:], ALU.add))
                    link(dve.reciprocal(rd[:], sm[:]))
                    dve.tensor_tensor(sc[:], sc[:], rd.unsqueeze(2).to_broadcast([P, 4, 256]), ALU.mult).then_inc(S["n_p"], 1)

                def unit(c):
                    dve.wait_ge(S["n_ev"], 1 + i * 8 + 4 + 2 * c)
                    dve.tensor_tensor(ub[:, 30:], ab[:], sb_[:], ALU.mult).then_inc(S["n_u"], 1)
                    dve.wait_ge(S["n_u"], i * 2 + c + 1)

                def conv(c, a, b):
                    for o in range(a, b):
                        if o == 0:
                            link(dve.tensor_scalar(ca[:], ub[:, 0:LAT], cw[:, c, 0:1], cw[:, c, 31:32], ALU.mult, ALU.add))
                        elif o < 30:
                            link(dve.scalar_tensor_tensor(ca[:], ub[:, o:o + LAT], cw[:, c, o:o + 1], ca[:], ALU.mult, ALU.add))
                        else:
                            d = uc[:, bass.ds(i * 2 + c, 1)].rearrange("p a t -> p (a t)")
                            dve.scalar_tensor_tensor(d, ub[:, o:o + LAT], cw[:, c, o:o + 1], ca[:], ALU.mult, ALU.add).then_inc(S["n_cv"], 1)

                def gate(j):
                    dve.wait_ge(S["n_ev"], 1 + i * 8 + 7 + j)
                    dve.wait_ge(S["n_at"], i * 2 + j + 1)
                    link(dve.tensor_tensor(at_[:, j], at_[:, j], gs[:], ALU.mult))
                    d = Y[:, bass.ds(i * 2 + j, 1)].rearrange("p a t -> p (a t)")
                    dve.tensor_tensor(d, at_[:, j], ga[:], ALU.mult).then_inc(S["n_y"], 1)

                rows(0)
                norm(0)
                rows(1)
                norm(1)
                unit(0)
                conv(0, 0, 12)
                rows(2)
                norm(2)
                conv(0, 12, 20)
                rows(3)
                norm(3)
                conv(0, 20, 31)
                dve.wait_ge(S["n_cv"], 1 + i * 2 + 1)
                unit(1)
                gate(0)
                conv(1, 0, 15)
                gate(1)
                conv(1, 15, 31)
                e["counts"]["DV_2"] = n[0]
            dve.wait_ge(S["n_cv"], 1 + 8)
            dve.wait_ge(S["n_y"], 1 + 8)
            dve.wait_ge(S["z_g"], 1 + 1)
            dve.memset(eps[:], 1e-5).then_inc(S["n_v0"], 1)
            with dve.Fori(0, 4) as i:
                for t in range(2):
                    dve.wait_ge(S["z_g"], 1 + i * 2 + t + 1)
                    dve.tensor_tensor(gcv[:, bass.ds(i * 2 + t, 1)].rearrange("p a t -> p (a t)"), graw[:, 0], graw[:, 1], ALU.mult).then_inc(S["z_gm"], 1)

            def norm_rows(n, view, base, which):
                dve.wait_ge(S["z_s"], which)
                dve.tensor_scalar(mean[:], pj[2][:, 0:LAT], 1.0 / (n * P), None, ALU.mult).then_inc(S["z_m"], 1)
                dve.wait_ge(S["z_m"], which)
                for k in range(n):
                    dve.tensor_tensor(view[:, k], view[:, k], mean[:], ALU.subtract).then_inc(S["z_c"], 1)
                dve.wait_ge(S["z_rt"], which)
                dve.reciprocal(rstd[:], rstd[:]).then_inc(S["z_rr"], 1)
                dve.wait_ge(S["z_rr"], which)
                dve.wait_ge(S["z_c"], base + n)
                for k in range(n):
                    dve.tensor_tensor(view[:, k], view[:, k], rstd[:], ALU.mult).then_inc(S["z_n"], 1)

            norm_rows(8, uc, 0, 1)
            for k in range(8):
                dve.wait_ge(S["z_i"], k + 1)
                dve.tensor_tensor(uc[:, k], uc[:, k], sa_[:], ALU.mult).then_inc(S["z_u"], 1)
            with dve.Fori(0, 2) as i:
                for t in range(4):
                    k = bass.ds(i * 4 + t, 1)
                    dve.wait_ge(w_used, half_p + i * RING + t + 1)
                    dve.scalar_tensor_tensor(Y[:, bass.ds(i * 4 + t + 8, 1)].rearrange("p a t -> p (a t)"), pj[0][:, 0:LAT],
                                             pr("b_pw", 8)[:, k], gcv[:, k].rearrange("p a t -> p (a t)"), ALU.add, ALU.mult).then_inc(S["z_y"], 1)
            with dve.Fori(0, KT // 2) as i:
                for t in range(2):
                    dve.wait_ge(w_used, half_o + i * RING + 2 * t + 2)
                    x = X[:, bass.ds(i * 2 + t, 1)].rearrange("p a t -> p (a t)")
                    dve.scalar_tensor_tensor(x, pj[0][:, 0:LAT], mod2[:, bass.ds(i * 2 + t + 32, 1)], x, ALU.mult, ALU.add).then_inc(S["z_r"], 1)
            dve.wait_ge(S["z_r"], 1 + KT)
            norm_rows(KT, X, 8, 2)



PHASES = [(phase_mod, "a"), (phase_gates, "b"), (phase_gdn, "g"), (phase_lora, "l"), (phase_rwkv, "r"),           (phase_out, "o"), (phase_two, "nz")]
SEMS = """a_par a_x a_sig a_sq a_ss a_eps a_rt a_scl a_xn a_h a_cs a_mc a_d a_used a_row a_turn a_w0 a_w1 a_w2 a_w3 a_w4 a_w5 a_w6 a_w7
b_z b_w b_out b_scan b_x b_p b_tr b_ea b_y b_v b_gc
g_rows g_y g_st g_raw g_sq g_ss g_kb g_lt g_l0 g_ltc g_mt g_mtc g_vk g_vkc g_x g_xs g_u g_t g_tr g_tt g_pre g_s g_w g_wc
g_sa g_sac g_ds g_o g_sig g_conv g_silu g_rt g_e g_d g_v g_v0
l_raw l_mix l_th l_v
r_y r_lw r_st r_raw r_sq r_ss r_vx r_vt r_kk r_vc r_sg r_lo r_xd r_p r_l0 r_pa r_q r_pd r_tt r_s r_w r_wc r_sa r_sac r_ds
r_rk r_bs r_yx r_yt r_kr r_rt r_cs r_ex r_x r_xs r_u r_t r_tr r_oc r_vr r_sd r_zs r_v r_v0
o_y o_w o_x o_r o_ss o_sq o_v o_rt o_n o_h o_b o_bd o_bm
n_kv n_dup n_ev n_at n_sc n_p n_tr n_pt n_pv n_y n_ks n_cv n_al n_m n_x n_u n_v0 n_v
z_g z_gm z_s z_sq z_ss z_u z_y z_r z_c z_rt z_n z_i z_m z_rr z_o z_st""".split()


def constants():
    import numpy as np
    cols, at, n = [], {}, 0

    def add(name, a):
        nonlocal n
        a = np.asarray(a, np.float32).reshape(P, -1)
        at[name] = n
        n += a.shape[1]
        cols.append(a)

    r = np.arange(P)
    add("ident", np.eye(P))
    add("ones", np.ones((P, P)))
    add("blk", r[:, None] // 64 == r[None] // 64)
    add("istk", r[:, None] % 64 == np.arange(64)[None])
    t = np.arange(384)
    add("rst0", np.broadcast_to(t % 64 != 0, (P, 384)))
    add("rst1", np.broadcast_to(t % 64 != 63, (P, 384)))
    add("incl", np.stack([r[:, None] <= r[None], r[:, None] >= r[None]], 1))
    add("strict", np.stack([r[:, None] < r[None], r[:, None] > r[None]], 1))
    lm = np.zeros((P, LEVELS, 2, 64))
    for lv in range(LEVELS):
        b = 1 << lv
        for d in range(2):
            c = np.arange(64)
            pair = c // b
            lm[:, lv, d] = -1.0 * (r[:, None] // b == (2 * pair + 1 - d)[None])
    add("lmask", lm)
    ch = np.arange(3456)
    q, h = 864, 1728
    kinds = np.zeros((3456, 7))
    kinds[:, 0] = -1
    for k in range(4):
        kinds[:, 1 + k] = ch // q == k
    kinds[:, 5], kinds[:, 6] = ch < h, ch >= h
    add("kinds", kinds[:3072].reshape(3, PAIRS, P, 7).transpose(2, 1, 0, 3))
    add("lkinds", np.broadcast_to(kinds[-1], (P, 7)))
    j = np.arange(384)
    dist = 255 - j
    inside = (dist >= 0) & (dist < 128)
    dd = np.maximum(dist, 1).astype(np.float32)
    large = 16 + (np.log(dd / 16) / math.log(128 / 16) * 16).astype(np.int32)
    bucket = np.where(dist < 16, dist, np.minimum(large, 31))
    onehot = np.zeros((P, 384))
    onehot[:32] = (np.arange(32)[:, None] == bucket[None]) & inside[None]
    win = np.concatenate([onehot[:32], np.broadcast_to(np.where(inside, 0.0, -1e30), (32, 384))], 1)
    return np.concatenate(cols, 1), at, win.astype(np.float32)


def kernel(**inputs):
    import numpy as np
    import concourse.bacc as _bacc
    from concourse import mybir as _mybir
    from concourse.bass_utils import run_bass_kernel_spmd as _run

    a = {k: np.asarray(v) for k, v in inputs.items()}
    a = {k: (v[0] if v.ndim > 1 and v.shape[0] == 1 else v) for k, v in a.items()}

    def cols(v):
        return v.reshape(-1, P).T

    def tiles(w, width=P):
        return np.ascontiguousarray(w.reshape(w.shape[0] // P, P, -1, width).transpose(2, 1, 0, 3))

    arr = {}
    arr["xT"] = np.ascontiguousarray(a["x"].T.reshape(KT, P, LAT).transpose(1, 0, 2))
    arr["ctxT"] = np.ascontiguousarray(a["ctx"].T.reshape(KT, P, CTX).transpose(1, 0, 2))
    arr["w_ada"] = np.concatenate([tiles(a["w_ada"], 512), tiles(a["w_ada_2"], 512)])
    w = a["w_in"]
    gd = [w[:, n * 1024:(n + 1) * 1024].reshape(D, GH, P) for n in range(4)]
    arr["w_g"] = tiles(np.stack(gd, 2).reshape(D, GH * 4 * P))
    gates = w[:, 4096:4128].reshape(KT, P, 2, 2, GH)
    arr["wg"], arr["wb"] = (np.ascontiguousarray(gates[:, :, q].reshape(KT, P, 16).transpose(1, 0, 2)) for q in range(2))
    u = w[:, 4128:]
    rk = [u[:, n * 1024:(n + 1) * 1024].reshape(D, PAIRS, P) for n in range(3)] + [u[:, 3456:].reshape(D, PAIRS, P)]
    arr["w_r"] = tiles(np.stack(rk, 2).reshape(D, PAIRS * 4 * P))
    arr["w_l"] = tiles(u[:, 3072:3456], LORA)
    up = np.stack([a["rwkv_w_up"], a["rwkv_a_up"]], 1).reshape(2, 2, LORA, PAIRS, P)
    arr["w_lup"] = np.ascontiguousarray(up.transpose(3, 2, 0, 1, 4).reshape(PAIRS, LORA, 4 * P))
    arr["rows"] = np.ascontiguousarray(np.stack([a["gdn_a_log"].reshape(16), a["gdn_dt_bias"].reshape(16)] * 2, 1))
    arr["cst"], cst_at, arr["win"] = constants()

    packs, par_at, n = [], {}, 0

    def pack(name, v):
        nonlocal n
        v = np.asarray(v).reshape(P, -1)
        par_at[name] = n
        n += v.shape[1]
        packs.append(v)

    pack("c", np.stack([cols(a["c"]), cols(a["c_ctx"]), cols(a["c_2"])], 2))
    pack("b_ada", np.stack([cols(a["b_ada"])] * 2, 2))
    pack("norm_g", cols(a["norm_g"]))
    cw = a["gdn_conv_w"].reshape(CONVK, 3, GH, P).transpose(3, 2, 1, 0).reshape(P, GH, 15)
    ng = np.broadcast_to(a["gdn_norm_g"][:, None, None], (P, GH, 1))
    pack("gp", np.concatenate([cw, ng], 2))
    mu = a["rwkv_mu"]
    pack("mu", mu[:3072].reshape(3, PAIRS, P).transpose(2, 1, 0))
    mul = np.zeros((P, 4), mu.dtype)
    mul[:LORA] = mu[3072:].reshape(4, LORA).T
    pack("mul", mul)
    pc = lambda v: v.reshape(PAIRS, P).T[:, :, None]
    w0, a0 = a["rwkv_w0"], a["rwkv_a0"]
    pack("rp", np.concatenate([pc(w0[0]), pc(w0[1]), pc(a0[0]), pc(a0[1]), pc(a["rwkv_k_k"]), pc(a["rwkv_k_a"]),
                               pc(a["rwkv_k_a"]), pc(a["rwkv_r_k"]), pc(a["rwkv_gn_g"]), pc(a["rwkv_gn_b"])], 2))
    extra(a, arr, pack, tiles, cols)
    arr["par"] = np.ascontiguousarray(np.concatenate(packs, 1))
    return launch(arr, cst_at, par_at, _bacc, _mybir, _run)


def extra(a, arr, pack, tiles, cols):
    import numpy as np
    arr["w_out"] = tiles(a["w_out"])
    w = a["w_in_2"]
    q, kv, ga, ua, ub, gc = (w[:, a0:a1] for a0, a1 in ((0, 1024), (1024, 1536), (1536, 2560), (2560, 3584), (3584, 4608), (4608, 5632)))
    arr["w_kv"] = tiles(kv)
    two = lambda v: v.reshape(D, 4, 2, P)
    q, ga, ua, ub = two(q), two(ga), two(ua), two(ub)
    arr["w_2"] = tiles(np.stack([q[:, :, 0], q[:, :, 1], ua[:, :, 0], ub[:, :, 0], ua[:, :, 1], ub[:, :, 1], ga[:, :, 0], ga[:, :, 1]], 2)
                       .reshape(D, 32 * P))
    arr["w_gc"] = tiles(gc)
    arr["w_pw"] = tiles(a["w_pw_2"])
    arr["w_out2"] = tiles(a["w_out_2"])
    pack("b_ada2", cols(a["b_ada_2"]))
    pack("fng", cols(a["final_norm_g"]))
    rel = np.zeros((P, 16), np.float32)
    rel[:32] = a["rel_bias_2"]
    pack("rel", rel)
    pack("sink", np.broadcast_to(a["sinks_2"], (P, 16)))
    cw = np.concatenate([a["conv_w_2"], a["conv_b_2"][None]], 0)
    pack("cw2", cw.reshape(32, 8, P).transpose(2, 1, 0))
    pack("cln", np.concatenate([cols(a["conv_ln_g_2"]), cols(a["conv_ln_b_2"])], 1))
    pack("b_pw", cols(a["b_pw_2"]))
    pack("ln2", np.concatenate([cols(a["ln_g_2"]), cols(a["ln_b_2"])], 1))


def launch(arr, cst_at, par_at, _bacc, _mybir, _run):
    import numpy as np
    nc = _bacc.Bacc("TRN2", target_bir_lowering=False, num_devices=1)
    io = {}
    feed = {}
    for name, v in arr.items():
        feed[f"in_{name}"] = np.ascontiguousarray(v)
        io[name] = nc.dram_tensor(f"in_{name}", v.shape, _mybir.dt.from_np(v.dtype), kind="ExternalInput").ap()
    out = nc.dram_tensor("out_xT", [KT, P, LAT], F32, kind="ExternalOutput").ap()
    io["cst_at"], io["par_at"] = cst_at, par_at
    io["arena"] = ARENA
    io["sems"], io["phases"] = SEMS, PHASES
    io["base_g"] = RING
    io["base_l"] = io["base_g"] + 8 * GH
    io["base_r"] = io["base_l"] + 8
    io["base_o"] = io["base_r"] + 8 * PAIRS
    io["base_2"] = io["base_o"] + 32
    io["DV_G"], io["DV_R"], io["DV_2"] = DV_G, DV_R, DV_2
    io["counts"] = {}
    program(nc, io, out)
    for k in ("DV_G", "DV_R", "DV_2"):
        if k in io["counts"]:
            assert io["counts"][k] == io[k], (k, io["counts"])
    r = _run(nc, [feed], core_ids=[0])
    got = r.results[0]["out_xT"]
    return np.ascontiguousarray(got.reshape(D, LAT).T)[None]


ARENA = 32586
DV_G, DV_R, DV_2 = 33, 95, 80
```

```python
import math
from contextlib import ExitStack

import concourse.bass as bass
from concourse import mybir

F32 = mybir.dt.float32
F32R = mybir.dt.float32r
ALU = mybir.AluOpType
ACT = mybir.ActivationFunctionType
AX_X = mybir.AxisListType.X

P = 128
D = 2048
KT = D // P
LAT, CTX = 512, 256
TOK = LAT + CTX
GH = 8
PAIRS = 8
LORA = 96
CONVK = 5
GT = TOK + 4
GC = LAT + 4
UN = 6
EXPM = 0.6065306597126334
RING = 4
HK = KT // 2
LEVELS = 7

G_ORDER = [[4, 5, 0, 1, 2, 3], [5, 4, 3, 2, 1, 0]]
R_ORDER = [[8, 9, 10, 11, 0, 1, 2, 3, 4, 5, 6, 7], [11, 10, 9, 8, 7, 6, 5, 4, 3, 2, 1, 0]]

R_W0, R_A0, R_KK, R_KA, R_KA1, R_RK, R_GG, R_GB = 21, 23, 25, 26, 27, 28, 29, 30
R_NPAR = 31


def gcol(t):
    return t * P if t < 4 else GC + (t - 4) * P


def halves(view, block, which):
    return view.rearrange("p u (n h b) -> p u n h b", h=2, b=block)[:, :, :, which, :]


def loads(half):
    return (half - RING) // RING * 16


def twice(v):
    return v.unsqueeze(1).to_broadcast([P, 2, 64])


def program(nc, io, out):
    ctx = ExitStack()
    with ctx:
        def sb(name, shape, dtype=F32, scope=ctx):
            return scope.enter_context(nc.sbuf_tensor(name, shape, dtype))

        def pb(name, shape):
            return ctx.enter_context(nc.psum_tensor(name, shape, F32))

        def sem(name):
            return ctx.enter_context(nc.semaphore(name))

        ring = sb("ring", [P, RING, HK, P])
        par = sb("par", [P, io["par"].shape[1]])
        cst = sb("cst", [P, io["cst"].shape[1]])
        rows = sb("rows", [16, 4])
        gate = sb("gate", [P, KT])
        gc = sb("gc", [P, GH, 6, UN])
        RP = sb("RP", [P, PAIRS, R_NPAR])
        mod2 = sb("mod2", [P, 48])
        unused = sb("unused", [P, 10])
        mixers = ctx.enter_context(ExitStack())
        hT = sb("hT", [P, KT, TOK], scope=mixers)
        arena = sb("arena", [P, io["arena"]], scope=mixers)

        pjl, pjc = pb("pjl", [P, 512]), pb("pjc", [P, 512])
        xu = [pb(f"xu{i}", [P, 512]) for i in range(2)]
        tp8 = pb("tp", [P, 2, 8, P])
        tp = tp8[:, :, 0:UN]
        pj = [pjl, tp8[:, 0, 0:4].rearrange("p a b -> p (a b)"), pjc]

        C = io["cst_at"]
        ident = cst[:, C["ident"]:C["ident"] + P]
        ones = cst[:, C["ones"]:C["ones"] + P]
        blk = cst[:, C["blk"]:C["blk"] + P]
        istk = cst[:, C["istk"]:C["istk"] + 64]
        rst = [cst[:, C["rst0"]:C["rst0"] + 384], cst[:, C["rst1"]:C["rst1"] + 384]]
        incl = [cst[:, C["incl"] + d * P:C["incl"] + (d + 1) * P] for d in range(2)]
        strict = [cst[:, C["strict"] + d * P:C["strict"] + (d + 1) * P] for d in range(2)]

        def lmask(level, d):
            at = C["lmask"] + (level * 2 + d) * 64
            return cst[:, at:at + 64]

        Q = io["par_at"]

        def pr(name, n=1, k=0):
            return par[:, Q[name] + k:Q[name] + k + n]

        gate_rows = nc.dram_tensor("gate_rows", [2, 2, GH, GT], F32, kind="Internal").ap()
        bias_rows = nc.dram_tensor("bias_rows", [16, 384], F32, kind="Internal").ap()
        bias_copies_t = nc.dram_tensor("bias_copies", [16, P, 384], F32, kind="Internal")
        xdram = nc.dram_tensor("xdram", [16, P, LAT], F32, kind="Internal").ap()
        ydram = nc.dram_tensor("ydram", [16, P, LAT], F32, kind="Internal").ap()

        w_loaded = [sem(f"w_loaded{i}") for i in range(RING)]
        x_saved = sem("x_saved")
        w_used = sem("w_used")

        at = [0]

        def carve(*shape):
            n = 1
            for s in shape:
                n *= s
            v = env["arena"][:, at[0]:at[0] + n]
            at[0] += n
            assert at[0] <= env["arena"].shape[1], at[0]
            if len(shape) == 1:
                return v
            names = "abcd"[:len(shape)]
            return v.rearrange("p (" + " ".join(names) + ") -> p " + " ".join(names),
                               **{k: s for k, s in zip(names[1:], shape[1:])})

        S = {}
        counts = io["counts"]
        env = dict(locals())
        phases = io["phases"]
        for f, prefixes in phases:
            at[0] = 0
            if prefixes == "o":
                mixers.close()
                env["high"] = sb("high", [P, KT, LAT], F32R)
                env["low"] = sb("low", [P, KT, LAT], F32R)
                env["parts"] = (sb("w_high", [P, 2, HK * P], F32R), sb("w_low", [P, 2, HK * P], F32R))
                env["bias"] = sb("bias", [P, KT, 256])
                env["arena"] = sb("arena2", [P, io["arena"] - KT * LAT - 4 * HK * P])
            own = [n for n in io["sems"] if n[0] in prefixes]
            for n in own:
                S[n] = nc.alloc_semaphore(name=n)
            f(nc, env)
            nc.clear_and_free_semaphores([S.pop(n) for n in own])
            nc.all_engine_barrier()


def phase_mod(nc, e):
    io, hT, par, cst, gate, mod2, carve, pr = (e[k] for k in ("io", "hT", "par", "cst", "gate", "mod2", "carve", "pr"))
    S, pj, xu, tp8, ones, ident, rows = (e[k] for k in ("S", "pj", "xu", "tp8", "ones", "ident", "rows"))
    SLOTS, SK = 8, 4
    ada = carve(SLOTS, SK, 512)
    cs = carve(KT, 3)
    csg = carve(KT, 3)
    sq = carve(2, TOK)
    rstd = carve(TOK)
    scl = carve(KT, 2)
    mod = carve(32, 2)
    modr = carve(2, 512)
    modc = carve(96, 3)
    eps = carve(1)
    GROUPS = 24
    H_GROUPS = 8
    ssl, ssc = pj[0], pj[2]
    turned = tp8[:, 0].rearrange("p (b n) s -> p b n s", b=2)

    def half_loops(engine, body):
        with engine.Fori(0, H_GROUPS // 2) as i:
            body(i)

    def rest_loops(engine, body):
        with engine.Fori(H_GROUPS // 2, GROUPS // 2) as i:
            body(i)

    unused = e["unused"]
    with nc.Block() as block:
        @block.gpsimd
        def _(pool):
            for n, name in enumerate(("a_row",)):
                pool.memset(unused[:, n:n + 1], 0.0).then_inc(S[name], 1)

        @block.sync
        def _(sp):
            sp.dma_start(par[:], io["par"]).then_inc(S["a_par"], 16)
            sp.dma_start(cst[:], io["cst"]).then_inc(S["a_par"], 16)
            sp.dma_start(rows[:], io["rows"]).then_inc(S["a_par"], 16)
            for s in range(SLOTS):
                sp.dma_start(ada[:, s], io["w_ada"][s // 4, :, (s % 4) * SK:(s % 4 + 1) * SK]).then_inc(S[f"a_w{s}"], 16)
            with sp.Fori(1, GROUPS // 2) as i:
                for s in range(SLOTS):
                    sp.wait_ge(S["a_used"], (i - 1) * SLOTS + s + 1)
                    sp.dma_start(ada[:, s], io["w_ada"][bass.ds(i * 2 + s // 4, 1), :, (s % 4) * SK:(s % 4 + 1) * SK]
                                 .rearrange("a p k c -> p (a k) c")).then_inc(S[f"a_w{s}"], 16)

        @block.scalar
        def _(act):
            act.dma_start(hT[:, :, 0:LAT], io["xT"]).then_inc(S["a_x"], 16)
            act.dma_start(hT[:, :, LAT:TOK], io["ctxT"]).then_inc(S["a_x"], 16)
            act.wait_ge(S["a_par"], 48)
            act.activation(csg[:], pr("c", 3 * KT).rearrange("p (k s) -> p k s", s=3), ACT.Sigmoid).then_inc(S["a_sig"], 1)
            act.wait_ge(S["a_x"], 32)
            for k in range(KT):
                if k >= 2:
                    act.wait_ge(S["a_ss"], k - 1)
                act.activation(sq[:, k % 2], hT[:, k], ACT.Square).then_inc(S["a_sq"], 1)
            act.wait_ge(S["a_ss"], KT)
            act.wait_ge(S["a_eps"], 1)
            act.activation(rstd[:, 0:LAT], ssl[:, 0:LAT], ACT.Sqrt, bias=eps[:], scale=1.0 / D).then_inc(S["a_rt"], 1)
            act.activation(rstd[:, LAT:TOK], ssc[:, 0:CTX], ACT.Sqrt, bias=eps[:], scale=1.0 / D).then_inc(S["a_rt"], 1)
            act.wait_ge(S["a_scl"], 1)
            for k in range(KT):
                act.wait_ge(S["a_xn"], k + 1)
                act.activation(hT[:, k, 0:LAT], hT[:, k, 0:LAT], ACT.Identity, bias=mod[:, k, 0:1],
                               scale=scl[:, k, 0:1]).then_inc(S["a_h"], 1)
                act.activation(hT[:, k, LAT:TOK], hT[:, k, LAT:TOK], ACT.Identity, bias=mod[:, k, 1:2],
                               scale=scl[:, k, 1:2]).then_inc(S["a_h"], 1)
            act.wait_ge(S["a_h"], 2 * KT)

        @block.tensor
        def _(pe):
            pe.wait_ge(S["a_par"], 48)
            for k in range(KT):
                pe.wait_ge(S["a_sq"], k + 1)
                pe.matmul(ssl[:, 0:LAT], ones, sq[:, k % 2, 0:LAT], start=k == 0, stop=k == KT - 1)
                pe.matmul(ssc[:, 0:CTX], ones, sq[:, k % 2, LAT:TOK], start=k == 0, stop=k == KT - 1).then_inc(S["a_ss"], 1)
            pe.wait_ge(S["a_cs"], 1)

            def groups(i):
                for b in range(2):
                    if b == 0:
                        pe.wait_ge(S["a_row"], 1 + i * 2)
                    for s in range(4):
                        pe.wait_ge(S[f"a_w{4 * b + s}"], i * 16 + 16)
                        for k in range(SK):
                            last = pe.matmul(xu[b][0:3, :], cs[:, s * SK + k], ada[:, 4 * b + s, k],
                                             start=s == 0 and k == 0, stop=s == 3 and k == SK - 1)
                        last.then_inc(S["a_used"], 1)
                for b in range(2):
                    pe.wait_ge(S["a_row"], 1 + i * 2 + b + 1)
                    for n in range(4):
                        last = pe.transpose(turned[:, b, n], modr[:, b, n * P:n * P + P], ident)
                    last.then_inc(S["a_turn"], 1)
            half_loops(pe, groups)
            rest_loops(pe, groups)

        @block.vector
        def _(dve):
            dve.memset(modr[:], 0.0).then_inc(e["w_used"], RING)
            dve.memset(eps[:], 1e-6).then_inc(S["a_eps"], 1)
            dve.wait_ge(S["a_sig"], 1)
            dve.tensor_tensor(cs[:], csg[:], pr("c", 3 * KT).rearrange("p (k s) -> p k s", s=3), ALU.mult).then_inc(S["a_cs"], 1)

            def groups(i):
                for b in range(2):
                    dve.wait_ge(S["a_used"], i * SLOTS + 4 * b + 4)
                    dve.tensor_copy(modr[0:3, b], xu[b][0:3, :]).then_inc(S["a_row"], 1)
                dve.wait_ge(S["a_turn"], i * 2 + 2)
                dve.tensor_copy(modc[:, bass.ds(i * 8, 8)].rearrange("p (b n) s -> p b n s", b=2), turned[:, :, :, 0:3]).then_inc(S["a_mc"], 1)

            half_loops(dve, groups)
            dve.wait_ge(S["a_mc"], H_GROUPS // 2)
            dve.tensor_tensor(mod[:], modc[:, 0:32, 0:2], pr("b_ada", 64).rearrange("p (n s) -> p n s", s=2), ALU.add).then_inc(S["a_d"], 1)
            dve.wait_ge(S["a_d"], 1)
            for s in range(2):
                dve.scalar_tensor_tensor(scl[:, :, s], mod[:, KT:2 * KT, s], 1.0, pr("norm_g", KT), ALU.add, ALU.mult).then_inc(S["a_d"], 1)
            dve.wait_ge(S["a_d"], 3)
            dve.wait_ge(S["a_rt"], 2)
            dve.reciprocal(rstd[:], rstd[:]).then_inc(S["a_scl"], 1)
            dve.wait_ge(S["a_scl"], 1)
            for k in range(KT):
                dve.tensor_tensor(hT[:, k], hT[:, k], rstd[:], ALU.mult).then_inc(S["a_xn"], 1)
            rest_loops(dve, groups)
            dve.wait_ge(S["a_mc"], GROUPS // 2)
            dve.tensor_tensor(gate[:], modc[:, 32:48, 0], pr("b_ada", 96).rearrange("p (n s) -> p n s", s=2)[:, 32:48, 0], ALU.add).then_inc(S["a_d"], 1)
            dve.tensor_tensor(mod2[:], modc[:, 48:96, 2], pr("b_ada2", 48), ALU.add).then_inc(S["a_d"], 1)
            dve.wait_ge(S["a_d"], 5)


def phase_gates(nc, e):
    io, hT, carve, S, pj, rows = (e[k] for k in ("io", "hT", "carve", "S", "pj", "rows"))
    ident, gate_rows = e["ident"], e["gate_rows"]
    raw = carve(3, GT + 4)
    zraw = carve(LAT)
    gw = carve(KT, 48)
    x = carve(GT)
    bt = carve(GT)
    y = carve(GT)
    z = carve(GT)
    z2 = carve(GT)
    pl = carve(GT)
    gs = [carve(GT), carve(GT)]
    gx = [carve(GT), carve(GT)]
    start16 = carve(2, LAT)
    tot = carve(2, 48)
    start4 = carve(2, 48)
    ea = carve(1)
    gc = e["gc"]
    R = slice(0, 16)
    B = slice(32, 48)
    tpos = pj[1][:, 0:4 * UN * 16].rearrange("p (q t c) -> p q t c", q=4, t=UN)
    tposb = e["xu"][0][:, 0:UN * 16].rearrange("p (t c) -> p t c", t=UN)
    w_used = e["w_used"]
    half = io["base_g"]

    with nc.Block() as block:
        @block.sync
        def _(sp):
            sp.wait_ge(S["b_z"], 4)
            sp.dma_start(gw[:, :, 0:16], io["wg"]).then_inc(S["b_w"], 16)
            sp.dma_start(gw[:, :, 32:48], io["wb"]).then_inc(S["b_w"], 16)
            for n in range(8):
                sp.wait_ge(w_used, half + n - RING + 1)
                sp.dma_start(e["ring"][:, n % RING], io["w_g"][n // 2, :, n % 2 * HK:(n % 2 + 1) * HK]).then_inc(e["w_loaded"][n % RING], 16)
            sp.wait_ge(S["b_scan"], 2)
            for d in range(2):
                sp.dma_start(gate_rows[0, d], gs[d][8 * d:8 * d + 8]).then_inc(S["b_out"], 16)
            sp.wait_ge(S["b_x"], 4)
            for d in range(2):
                sp.dma_start(gate_rows[1, d], bt[32 + 8 * d:40 + 8 * d]).then_inc(S["b_out"], 16)
            sp.wait_ge(S["b_out"], 64)

        @block.tensor
        def _(pe):
            pe.wait_ge(S["b_w"], 32)
            for k in range(KT):
                pe.matmul(pj[0][0:48, 0:LAT], gw[:, k], hT[:, k, 0:LAT], start=k == 0, stop=k == KT - 1)
                pe.matmul(pj[2][0:48, 0:CTX], gw[:, k], hT[:, k, LAT:TOK], start=k == 0, stop=k == KT - 1).then_inc(S["b_p"], 1)
            pe.wait_ge(S["b_x"], 4)
            for j in range(4):
                if j:
                    pe.wait_ge(S["b_raw"], (0, 1, 3, 5)[j])
                project(pe, e, 0, j, loads(half), pj[0][:, 0:LAT], pj[2][:, 0:CTX] if j in (1, 2) else None)
            pe.wait_ge(S["b_x"], 4)
            pe.wait_ge(S["b_scan"], 2)
            for t in range(UN):
                for q, src in enumerate((gs[0], gs[1], gx[0], gx[1])):
                    pe.transpose(tpos[:, q, t], src[R, gcol(t):gcol(t) + P], ident[R, 0:16])
                last = pe.transpose(tposb[:, t], bt[B, gcol(t):gcol(t) + P], ident[B, 32:48])
            last.then_inc(S["b_tr"], 1)

        @block.scalar
        def _(act):
            act.wait_ge(S["b_z"], 4)
            act.activation(ea[R], rows[:, 0:1], ACT.Exp).then_inc(S["b_ea"], 1)
            act.wait_ge(S["b_p"], KT)
            for n, (a, b, src) in enumerate(((0, LAT, pj[0]), (GC, GT, pj[2]))):
                act.activation(x[R, a:b], src[R, 0:b - a], ACT.Identity, bias=rows[:, 1:2]).then_inc(S["b_x"], 1)
                act.activation(bt[B, a:b], src[B, 0:b - a], ACT.Sigmoid).then_inc(S["b_x"], 1)
            act.wait_ge(S["b_x"], 4)
            act.activation(y[R], x[R], ACT.Abs).then_inc(S["b_y"], 1)
            act.wait_ge(S["b_y"], 1)
            act.activation(y[R], y[R], ACT.Exp, scale=-1.0).then_inc(S["b_y"], 1)
            for j in range(4):
                act.wait_ge(w_used, half + 2 * j + 2)
                act.activation(zraw[:] if j == 3 else raw[:, j, 2:2 + LAT], pj[0][:, 0:LAT], ACT.Copy).then_inc(S["b_raw"], 1)
                if j in (1, 2):
                    act.activation(raw[:, j, GC + 2:GT + 2], pj[2][:, 0:CTX], ACT.Copy).then_inc(S["b_raw"], 1)
            act.wait_ge(S["b_raw"], 6)

        @block.vector
        def _(dve):
            n = [0]

            def link(ins):
                n[0] += 1
                ins.then_inc(S["b_v"], 1)
                dve.wait_ge(S["b_v"], n[0])

            for t in (gw[:, :, 16:32], x[:, LAT:GC], bt[:, LAT:GC]):
                dve.memset(t, 0.0).then_inc(S["b_z"], 1)
            dve.memset(raw[:], 0.0)
            dve.memset(z[:], 0.0).then_inc(S["b_z"], 1)
            dve.wait_ge(S["b_y"], 2)
            link(dve.tensor_scalar(z[R], y[R], 2.0, None, ALU.add))
            link(dve.reciprocal(z[R], z[R]))
            link(dve.tensor_tensor(z[R], z[R], y[R], ALU.mult))
            link(dve.tensor_tensor(z2[R], z[R], z[R], ALU.mult))
            link(dve.tensor_scalar(pl[R], z2[R], 1.0 / 17, None, ALU.mult))
            for c in (15, 13, 11, 9, 7, 5, 3):
                link(dve.scalar_tensor_tensor(pl[R], pl[R], 1.0 / c, z2[R], ALU.add, ALU.mult))
            link(dve.scalar_tensor_tensor(pl[R], pl[R], 1.0, z[R], ALU.add, ALU.mult))
            link(dve.tensor_scalar(x[R], x[R], 0.0, None, ALU.max))
            link(dve.scalar_tensor_tensor(x[R], pl[R], 2.0, x[R], ALU.mult, ALU.add))
            dve.wait_ge(S["b_ea"], 1)
            link(dve.tensor_scalar(x[R], x[R], ea[R], -1.0, ALU.mult, ALU.mult))
            runs = lambda v: v.rearrange("p (n b t) -> p n b t", b=4, t=16)
            for d in range(2):
                first = 15 if d else 0
                last = 0 if d else 15
                back = slice(None, None, -1 if d else 1)
                link(dve.memset(gs[d][:, LAT:GC], 0.0))
                link(dve.memset(start16[:, d], 1.0))
                link(dve.memset(start16[:, d, first:LAT:16], 0.0))
                link(dve.memset(start4[:, d], 1.0))
                link(dve.memset(start4[:, d, 3 if d else 0:48:4], 0.0))
                for a, b, k0 in ((0, LAT, 0), (GC, GT, 32)):
                    m, k1 = b - a, k0 + (b - a) // 16
                    link(dve.tensor_tensor_scan(gs[d][R, a:b][:, back], start16[R, d, 0:m][:, back], x[R, a:b][:, back], 0.0, ALU.mult, ALU.add))
                    link(dve.tensor_copy(tot[R, d, k0:k1], gs[d][R, a + last:b:16]))
                    link(dve.tensor_tensor_scan(tot[R, d, k0:k1][:, back], start4[R, d, k0:k1][:, back], tot[R, d, k0:k1][:, back], 0.0,
                                                ALU.mult, ALU.add))
                    to = runs(gs[d][R, a:b])[:, :, 0:3] if d else runs(gs[d][R, a:b])[:, :, 1:4]
                    t4 = tot[R, d, k0:k1].rearrange("p (n b) -> p n b", b=4)
                    of = t4[:, :, 1:4] if d else t4[:, :, 0:3]
                    link(dve.tensor_tensor(to, to, of.unsqueeze(3).to_broadcast([16, m // 64, 3, 16]), ALU.add))
                link(dve.tensor_copy(gx[d][R], gs[d][R]))
                for a, b in ((0, LAT), (GC, GT)):
                    half = lambda v: v[R, a:b].rearrange("p (u h t) -> p u h t", h=2, t=64)[:, :, d]
                    end = 0 if d else 63
                    link(dve.tensor_tensor(half(gx[d]), half(gs[d]), half(gs[d])[:, :, end:end + 1].to_broadcast([16, (b - a) // P, 64]), ALU.subtract))
                dve.tensor_copy(tot[R, d, 0:1], gs[d][R, 0:1]).then_inc(S["b_scan"], 1)
            dve.wait_ge(S["b_tr"], 1)
            for d in range(2):
                dve.tensor_copy(gc[:, :, d], tpos[:, d, :, 8 * d:8 * d + 8].rearrange("p t h -> p h t")).then_inc(S["b_gc"], 1)
                dve.tensor_copy(gc[:, :, 2 + d], tposb[:, :, 8 * d:8 * d + 8].rearrange("p t h -> p h t")).then_inc(S["b_gc"], 1)
                dve.tensor_copy(gc[:, :, 4 + d], tpos[:, 2 + d, :, 8 * d:8 * d + 8].rearrange("p t h -> p h t")).then_inc(S["b_gc"], 1)
            dve.wait_ge(S["b_gc"], 6)


def project(pe, e, i, j, base, lat, ctxp, k0=0, k1=KT):
    S, ring, hT, w_loaded, w_used = (e[k] for k in ("S", "ring", "hT", "w_loaded", "w_used"))
    for kk in range(k0, k1):
        s = (2 * j + kk // HK) % RING
        if kk % HK == 0:
            pe.wait_ge(w_loaded[s], base + (i * 2 + j // 2 + 1) * 16)
        last = pe.matmul(lat, ring[:, s, kk % HK], hT[:, kk, 0:LAT], start=kk == 0, stop=kk == KT - 1)
        if ctxp is not None:
            last = pe.matmul(ctxp, ring[:, s, kk % HK], hT[:, kk, LAT:TOK], start=kk == 0, stop=kk == KT - 1)
        if kk % HK == HK - 1:
            last.then_inc(w_used, 1)


def load_tiles(sp, e, src, base_used, i, n0=0, n1=8):
    ring, w_loaded, w_used = e["ring"], e["w_loaded"], e["w_used"]
    for n in range(n0, n1):
        j, hf, s = n // 2, n % 2, n % RING
        sp.wait_ge(w_used, base_used + i * 8 + n - RING + 1)
        sp.dma_start(ring[:, s], src[bass.ds(i * 4 + j, 1), :, hf * HK:(hf + 1) * HK]
                     .rearrange("a p k c -> p (a k) c")).then_inc(w_loaded[s], 16)


def invert_pe(pe, S, q, i, lv, LT, T, TT, Xs, tp, ident, fill):
    n2 = 2 * lv
    for l in range(lv):
        b = 1 << l
        if l:
            for d in range(2):
                pe.wait_ge(S[q + "tt"], i * n2 + (l - 1) * 2 + d + 1)
                for u in range(UN):
                    last = pe.matmul(tp[:, d, u], LT[:, d, u], T[:, d, u], start=True, stop=True)
                last.then_inc(S[q + "x"], 1)
            if fill:
                fill(3 * l)
            for d in range(2):
                pe.wait_ge(S[q + "xs"], i * (n2 - 2) + (l - 1) * 2 + d + 1)
                for u in range(UN):
                    last = pe.matmul(tp[:, d, u], TT[:, d, u], twice(Xs[:, d, u]), start=True, stop=True)
                last.then_inc(S[q + "u"], 1)
            if fill:
                fill(3 * l + 1)
        for d in range(2):
            pe.wait_ge(S[q + "t"], i * n2 + l * 2 + d + 1)
            for u in range(UN):
                last = pe.transpose(tp[:, d, u], T[:, d, u] if l else TT[:, d, u], ident)
            last.then_inc(S[q + "tr"], 1)
        if fill:
            fill(3 * l + 2)


def invert_dve(dve, S, q, i, lv, T, Xs, tp, lmask):
    n2 = 2 * lv
    for l in range(1, lv):
        b = 1 << l
        for d in range(2):
            dve.wait_ge(S[q + "x"], i * (n2 - 2) + (l - 1) * 2 + d + 1)
            m = lmask(l, d).rearrange("p (n b) -> p n b", b=b).unsqueeze(1).to_broadcast([P, UN, 64 // b, b])
            dve.tensor_tensor(Xs[:, d].rearrange("p u (n b) -> p u n b", b=b), halves(tp[:, d], b, d), m, ALU.mult).then_inc(S[q + "xs"], 1)
        for d in range(2):
            dve.wait_ge(S[q + "u"], i * (n2 - 2) + (l - 1) * 2 + d + 1)
            v = halves(T[:, d], b, d)
            dve.tensor_tensor(v, v, tp[:, d, :, 0:64].rearrange("p u (n b) -> p u n b", b=b), ALU.add).then_inc(S[q + "t"], 1)


def invert_start(dve, S, q, link, d, LT, TT, Xs, ident):
    link(dve.tensor_copy(TT[:, d], ident.unsqueeze(1).to_broadcast([P, UN, P])))
    link(dve.tensor_tensor(Xs[:, d], LT[:, d, :, 1 - d:P:2], ident[:, d:P:2].unsqueeze(1).to_broadcast([P, UN, 64]), ALU.mult))
    v = TT[:, d, :, 1 - d:P:2]
    dve.tensor_tensor(v, v, Xs[:, d], ALU.subtract).then_inc(S[q + "t"], 1)


def invert_act(act, S, q, i, lv, T, TT, tp):
    n2 = 2 * lv
    for l in range(lv):
        b = 1 << l
        for d in range(2):
            act.wait_ge(S[q + "tr"], i * n2 + l * 2 + d + 1)
            o, s = (T[:, d], tp[:, d]) if l == 0 else (halves(TT[:, d], b, 1 - d), halves(tp[:, d], b, 1 - d))
            act.activation(o, s, ACT.Copy).then_inc(S[q + "tt"], 1)


def phase_gdn(nc, e):
    io, carve, S, pj, xu, tp, ident, ones, lmask, incl, pr = (
        e[k] for k in ("io", "carve", "S", "pj", "xu", "tp", "ident", "ones", "lmask", "incl", "pr"))
    gc, gate_rows, ydram, w_used = e["gc"], e["gate_rows"], e["ydram"], e["w_used"]
    raw = carve(3, GT + 4)
    zraw, zs = carve(LAT), carve(LAT)
    qkv = carve(3, GT)
    sg = carve(4, GT)
    G = carve(2, GT)
    KB = carve(2, GT)
    EG = carve(2, GT)
    KBG = carve(2, GT)
    QG = carve(2, LAT)
    ET = carve(2, UN, P)
    LT = carve(2, UN, P)
    T = carve(2, UN, P)
    TT = carve(2, UN, P)
    Xs = carve(2, UN, 64)
    MT = carve(2, 4, P)
    bV = carve(2, UN, P)
    KL = carve(2, UN, P)
    W = carve(2, P)
    SA = carve(2, P)
    St = carve(2, P)
    oT = carve(LAT)
    ybuf = carve(LAT)
    tail = carve(2, UN)
    gcs = carve(6, UN)
    hp = carve(16)
    eps = carve(1)
    half = io["base_g"]
    wb = loads(half)
    sq, nr = sg[:, 0:2], sg[:, 2:4]
    DV = io["DV_G"]

    unused = e["unused"]
    with nc.Block() as block:
        @block.gpsimd
        def _(pool):
            for n, name in enumerate(("g_y", "g_st")):
                pool.memset(unused[:, n:n + 1], 0.0).then_inc(S[name], 1)
            pool.memset(unused[:, 2:3], 0.0).then_inc(S["g_raw"], 1 + 6)

        @block.sync
        def _(sp):
            def gate_rows_of(i):
                for d in range(2):
                    sp.dma_start(G[:, d], gate_rows[0, d, bass.ds(i, 1)].rearrange("a t -> (a t)").partition_broadcast(P)).then_inc(S["g_rows"], 16)
                    sp.dma_start(KB[:, d], gate_rows[1, d, bass.ds(i, 1)].rearrange("a t -> (a t)").partition_broadcast(P)).then_inc(S["g_rows"], 16)


            gate_rows_of(0)
            with sp.Fori(0, GH - 1) as i:
                load_tiles(sp, e, io["w_g"], half, i + 1, 0, 4)
                sp.wait_ge(S["g_pre"], i + 1)
                sp.wait_ge(S["g_lt"], i * 2 + 2)
                gate_rows_of(i + 1)
                load_tiles(sp, e, io["w_g"], half, i + 1, 4, 8)

        @block.tensor
        def _(pe):
            def column(i, j, k0=0, k1=KT):
                if k0 == 0:
                    pe.wait_ge(S["g_raw"], 1 + i * 6 + (0, 1, 3, 5)[j])
                project(pe, e, i, j, wb, pj[0][:, 0:LAT], pj[2][:, 0:CTX] if j in (1, 2) else None, k0, k1)

            def turn(i, more):
                def fill(n):
                    if more and 3 <= n < 3 + KT:
                        column(i + 1, 2, n - 3, n - 2)

                def fill_scan(n):
                    if more and n < KT:
                        column(i + 1, 3, n, n + 1)

                if more:
                    column(i + 1, 0)
                pe.wait_ge(S["g_y"], 1 + i)
                pe.wait_ge(S["g_sq"], i * 3 + 1)
                pe.matmul(xu[0][:, 0:LAT], ones, sq[:, 0, 0:LAT], start=True, stop=True).then_inc(S["g_ss"], 1)
                pe.wait_ge(S["g_sq"], i * 3 + 2)
                pe.matmul(pj[1][:, 0:LAT], ones, sq[:, 1, 0:LAT], start=True, stop=True)
                pe.matmul(xu[1][:, 0:CTX], ones, sq[:, 1, GC:GT], start=True, stop=True).then_inc(S["g_ss"], 1)
                if more:
                    column(i + 1, 1, 0, KT)
                pe.wait_ge(S["g_kb"], i * 2 + 2)
                for d in range(2):
                    for u in range(UN):
                        c = gcol(u)
                        last = pe.matmul(tp[:, d, u], qkv[:, 1, c:c + P], KB[:, d, c:c + P], start=True, stop=True)
                    last.then_inc(S["g_lt"], 1)
                for d in range(2):
                    pe.wait_ge(S["g_ltc"], i * 2 + d + 1)
                    for u in range(4):
                        last = pe.matmul(tp[:, d, u], qkv[:, 1, u * P:u * P + P], qkv[:, 0, u * P:u * P + P], start=True, stop=True)
                    last.then_inc(S["g_mt"], 1)
                pe.wait_ge(S["g_mtc"], i * 2 + 2)
                for d in range(2):
                    for u in range(UN):
                        last = pe.transpose(tp[:, d, u], qkv[:, 2 - d, gcol(u):gcol(u) + P], ident)
                last.then_inc(S["g_vk"], 1)
                pe.wait_ge(S["g_vkc"], i + 1)
                invert_pe(pe, S, "g_", i, LEVELS, LT, T, TT, Xs, tp, ident, fill)
                pe.wait_ge(S["g_pre"], i + 1)
                for j in range(UN):
                    for d in range(2):
                        u = G_ORDER[d][j]
                        c = gcol(u)
                        if j == 0:
                            pe.wait_ge(S["g_tt"], i * 14 + 12 + d + 1)
                        pe.wait_ge(S["g_s"], i * 14 + 2 * j + d + 1)
                        pe.matmul(xu[d][:, 0:P], KBG[:, d, c:c + P], St[:, d], start=True, stop=True).then_inc(S["g_w"], 1)
                    fill_scan(3 * j)
                    for d in range(2):
                        u = G_ORDER[d][j]
                        pe.wait_ge(S["g_wc"], i * 12 + 2 * j + d + 1)
                        pe.matmul(xu[d][:, P:2 * P], TT[:, d, u], W[:, d], start=True, stop=True).then_inc(S["g_sa"], 1)
                    for d in range(2):
                        u = G_ORDER[d][j]
                        if u < 4:
                            if j > 2:
                                pe.wait_ge(S["g_o"], i * 8 + 2 * (j - 3) + d + 1)
                            pe.matmul(tp[:, d, 0], St[:, d], QG[:, d, u * P:u * P + P], start=True, stop=False)
                    fill_scan(3 * j + 1)
                    for d in range(2):
                        u = G_ORDER[d][j]
                        pe.wait_ge(S["g_sac"], i * 12 + 2 * j + d + 1)
                        pe.matmul(xu[d][:, 2 * P:3 * P], KL[:, d, u], SA[:, d], start=True, stop=True).then_inc(S["g_ds"], 1)
                    for d in range(2):
                        u = G_ORDER[d][j]
                        if u < 4:
                            pe.matmul(tp[:, d, 0], SA[:, d], MT[:, d, u], start=False, stop=True).then_inc(S["g_oo"], 1)
                    fill_scan(3 * j + 2)
                pe.wait_ge(S["g_sq"], i * 3 + 3)
                pe.matmul(pj[1][:, 0:LAT], ones, sq[:, 0, 0:LAT], start=True, stop=True).then_inc(S["g_ss"], 1)

            with pe.Fori(0, GH - 1) as i:
                turn(i, True)
            turn(GH - 1, False)

        @block.scalar
        def _(act):
            act.wait_ge(S["g_v0"], 3)

            def copy_column(i, j):
                act.wait_ge(w_used, half + i * 8 + 2 * j + 2)
                act.activation(zraw[:] if j == 3 else raw[:, j, 2:2 + LAT], pj[0][:, 0:LAT], ACT.Copy).then_inc(S["g_raw"], 1)
                if j in (1, 2):
                    act.activation(raw[:, j, GC + 2:GT + 2], pj[2][:, 0:CTX], ACT.Copy).then_inc(S["g_raw"], 1)

            def turn(i, more):
                act.wait_ge(S["g_raw"], 1 + i * 6 + 6)
                act.activation(sg[:, 3, 0:LAT], zraw[:], ACT.Sigmoid).then_inc(S["g_sig"], 1)
                for j in range(3):
                    act.wait_ge(S["g_conv"], i * 3 + j + 1)
                    n = LAT if j == 0 else GT
                    act.activation(sg[:, j, 0:n], qkv[:, j, 0:n], ACT.Sigmoid).then_inc(S["g_sig"], 1)
                if more:
                    copy_column(i + 1, 0)
                for j in range(2):
                    act.wait_ge(S["g_silu"], i * 4 + 4)
                    n = LAT if j == 0 else GT
                    act.activation(sq[:, j, 0:n], qkv[:, j, 0:n], ACT.Square).then_inc(S["g_sq"], 1)
                act.wait_ge(S["g_ss"], i * 3 + 2)
                act.activation(nr[:, 0, 0:LAT], xu[0][:, 0:LAT], ACT.Sqrt, bias=eps[:]).then_inc(S["g_rt"], 1)
                act.activation(nr[:, 1, 0:LAT], pj[1][:, 0:LAT], ACT.Sqrt, bias=eps[:]).then_inc(S["g_rt"], 1)
                act.activation(nr[:, 1, GC:GT], xu[1][:, 0:CTX], ACT.Sqrt, bias=eps[:]).then_inc(S["g_rt"], 1)
                act.wait_ge(S["g_rows"], i * 64 + 64)
                act.activation(EG[:], G[:], ACT.Exp).then_inc(S["g_e"], 1)
                act.wait_ge(S["g_d"], i + 1)
                act.activation(ET[:], ET[:], ACT.Exp).then_inc(S["g_e"], 1)
                act.activation(tail[:], tail[:], ACT.Exp).then_inc(S["g_e"], 1)
                if more:
                    copy_column(i + 1, 1)
                invert_act(act, S, "g_", i, LEVELS, T, TT, tp)
                if more:
                    copy_column(i + 1, 2)
                for j in range(UN):
                    for d in range(2):
                        act.wait_ge(S["g_sa"], i * 12 + 2 * j + d + 1)
                        if j:
                            act.wait_ge(S["g_ds"], i * 12 + 2 * (j - 1) + d + 1)
                        act.activation(SA[:, d], xu[d][:, P:2 * P], ACT.Copy).then_inc(S["g_sac"], 1)
                if more:
                    act.wait_ge(S["g_silu"], i * 4 + 4)
                    copy_column(i + 1, 3)
                act.wait_ge(S["g_o"], i * 8 + 8)
                act.activation(sq[:, 0, 0:LAT], oT[:], ACT.Square).then_inc(S["g_sq"], 1)
                act.wait_ge(S["g_ss"], i * 3 + 3)
                act.activation(nr[:, 0, 0:LAT], pj[1][:, 0:LAT], ACT.Sqrt, bias=eps[:], scale=1.0 / P).then_inc(S["g_rt"], 1)
                act.wait_ge(S["g_y"], 1 + i + 1)
                act.dma_start(ydram[bass.ds(i, 1)].rearrange("a p t -> p (a t)"), ybuf[:]).then_inc(S["g_st"], 16)

            with act.Fori(0, GH - 1) as i:
                turn(i, True)
            turn(GH - 1, False)
            act.wait_ge(S["g_st"], 1 + 16 * GH)

        @block.vector
        def _(dve):
            dve.memset(eps[:], 1e-6).then_inc(S["g_v0"], 1)
            dve.memset(sg[:], 1.0).then_inc(S["g_v0"], 1)
            dve.memset(qkv[:], 0.0).then_inc(S["g_v0"], 1)
            dve.wait_ge(S["g_v0"], 3)

            def turn(i):
                dve.wait_ge(S["g_y"], 1 + i)
                n = [0]

                def link(ins):
                    n[0] += 1
                    ins.then_inc(S["g_v"], 1)
                    dve.wait_ge(S["g_v"], i * DV + n[0])

                link(dve.tensor_copy(hp[:], pr("gp", 16 * GH).rearrange("p (h c) -> p h c", h=GH)[:, bass.ds(i, 1), :]
                                     .rearrange("p a c -> p (a c)")))
                link(dve.tensor_copy(gcs[:], gc[:, bass.ds(i, 1)].rearrange("p a q t -> p (a q) t")))
                for d in range(2):
                    dve.memset(St[:, d], 0.0).then_inc(S["g_s"], 1)
                link(dve.memset(oT[:], 0.0))
                for j in range(3):
                    m = LAT if j == 0 else GT
                    dve.wait_ge(S["g_raw"], 1 + i * 6 + (1, 3, 5)[j])
                    link(dve.tensor_scalar(qkv[:, j, 0:m], raw[:, j, 0:m], hp[:, 5 * j:5 * j + 1], None, ALU.mult))
                    for o in range(1, CONVK):
                        ins = dve.scalar_tensor_tensor(qkv[:, j, 0:m], raw[:, j, o:o + m], hp[:, 5 * j + o:5 * j + o + 1],
                                                       qkv[:, j, 0:m], ALU.mult, ALU.add)
                        if o < CONVK - 1:
                            link(ins)
                        else:
                            ins.then_inc(S["g_conv"], 1)
                dve.wait_ge(S["g_conv"], i * 3 + 3)
                for j in range(3):
                    m = LAT if j == 0 else GT
                    dve.wait_ge(S["g_sig"], i * 4 + j + 2)
                    dve.tensor_tensor(qkv[:, j, 0:m], qkv[:, j, 0:m], sg[:, j, 0:m], ALU.mult).then_inc(S["g_silu"], 1)
                dve.tensor_tensor(zs[:], zraw[:], sg[:, 3, 0:LAT], ALU.mult).then_inc(S["g_silu"], 1)
                dve.wait_ge(S["g_silu"], i * 4 + 4)
                dve.wait_ge(S["g_rows"], i * 64 + 64)
                for d in range(2):
                    for u in range(UN):
                        c = gcol(u)
                        for hf in range(2):
                            q = d if hf == d else 4 + d
                            dve.tensor_scalar(ET[:, d, u, 64 * hf:64 * hf + 64], G[:, d, c + 64 * hf:c + 64 * hf + 64], gcs[:, q, u:u + 1], 0.0,
                                              ALU.subtract, ALU.min)
                    end = 0 if d else P - 1
                    dve.tensor_tensor(tail[:, d, 0:4], G[:, d, end:LAT:P], gcs[:, 4 + d, 0:4], ALU.subtract)
                    last = dve.tensor_tensor(tail[:, d, 4:6], G[:, d, GC + end:GT:P], gcs[:, 4 + d, 4:6], ALU.subtract)
                last.then_inc(S["g_d"], 1)
                dve.wait_ge(S["g_rt"], i * 4 + 3)
                link(dve.reciprocal(nr[:, 0:1, 0:LAT], nr[:, 0:1, 0:LAT]))
                link(dve.reciprocal(nr[:, 1], nr[:, 1]))
                link(dve.scalar_tensor_tensor(qkv[:, 0, 0:LAT], qkv[:, 0, 0:LAT], float(P) ** -0.5, nr[:, 0, 0:LAT], ALU.mult, ALU.mult))
                link(dve.tensor_tensor(qkv[:, 1], qkv[:, 1], nr[:, 1], ALU.mult))
                for d in range(2):
                    dve.tensor_tensor(KB[:, d], KB[:, d], qkv[:, 1], ALU.mult).then_inc(S["g_kb"], 1)
                dve.wait_ge(S["g_kb"], i * 2 + 2)
                dve.wait_ge(S["g_e"], i * 3 + 3)
                for d in range(2):
                    for a, b in ((0, LAT), (GC, GT)):
                        v = EG[:, d, a:b].rearrange("p (u h t) -> p u h t", h=2, t=64)
                        end = 0 if d else 63
                        link(dve.tensor_tensor(v[:, :, 1 - d], v[:, :, 1 - d], v[:, :, d, end:end + 1].to_broadcast([P, (b - a) // P, 64]), ALU.mult))
                for d in range(2):
                    dve.tensor_tensor(KBG[:, d], KB[:, d], EG[:, d], ALU.mult)
                    last = dve.tensor_tensor(QG[:, d], qkv[:, 0, 0:LAT], EG[:, d, 0:LAT], ALU.mult)
                last.then_inc(S["g_pre"], 1)
                for d in range(2):
                    dve.wait_ge(S["g_lt"], i * 2 + d + 1)
                    dve.tensor_tensor(LT[:, d], tp[:, d], ET[:, d], ALU.mult).then_inc(S["g_ltc"], 1)
                    dve.wait_ge(S["g_ltc"], i * 2 + d + 1)
                    invert_start(dve, S, "g_", link, d, LT, TT, Xs, ident)
                for d in range(2):
                    dve.wait_ge(S["g_ltc"], i * 2 + 2)
                    link(dve.tensor_tensor(ET[:, d, 0:4], ET[:, d, 0:4], incl[d].unsqueeze(1).to_broadcast([P, 4, P]), ALU.mult))
                    dve.wait_ge(S["g_mt"], i * 2 + d + 1)
                    dve.tensor_tensor(MT[:, d], tp[:, d, 0:4], ET[:, d, 0:4], ALU.mult).then_inc(S["g_mtc"], 1)
                dve.wait_ge(S["g_vk"], i + 1)
                for d in range(2):
                    dve.tensor_tensor(bV[:, d], tp[:, 0], gcs[:, 2 + d].unsqueeze(2).to_broadcast([P, UN, P]), ALU.mult)
                    last = dve.tensor_tensor(KL[:, d], tp[:, 1], tail[:, d].unsqueeze(2).to_broadcast([P, UN, P]), ALU.mult)
                last.then_inc(S["g_vkc"], 1)
                dve.wait_ge(S["g_vkc"], i + 1)
                invert_dve(dve, S, "g_", i, LEVELS, T, Xs, tp, lmask)
                no = 0
                for j in range(UN):
                    for d in range(2):
                        u = G_ORDER[d][j]
                        dve.wait_ge(S["g_w"], i * 12 + 2 * j + d + 1)
                        dve.tensor_tensor(W[:, d], bV[:, d, u], xu[d][:, 0:P], ALU.subtract).then_inc(S["g_wc"], 1)
                    for d in range(2):
                        c = gcol(G_ORDER[d][j]) + (0 if d else P - 1)
                        dve.wait_ge(S["g_ds"], i * 12 + 2 * j + d + 1)
                        dve.scalar_tensor_tensor(St[:, d], St[:, d], EG[:, d, c:c + 1], xu[d][:, 2 * P:3 * P],
                                                 ALU.mult, ALU.add).then_inc(S["g_s"], 1)
                    for d in range(2):
                        u = G_ORDER[d][j]
                        if u < 4:
                            o = oT[:, u * P:u * P + P]
                            dve.wait_ge(S["g_oo"], i * 8 + no + 1)
                            if no:
                                dve.wait_ge(S["g_o"], i * 8 + no)
                            dve.tensor_tensor(o, o, tp[:, d, 0], ALU.add).then_inc(S["g_o"], 1)
                            no += 1
                dve.wait_ge(S["g_rt"], i * 4 + 4)
                dve.wait_ge(S["g_o"], i * 8 + 8)
                link(dve.reciprocal(nr[:, 0:1, 0:LAT], nr[:, 0:1, 0:LAT]))
                link(dve.tensor_tensor(oT[:], oT[:], nr[:, 0, 0:LAT], ALU.mult))
                dve.wait_ge(S["g_st"], 1 + i * 16)
                dve.scalar_tensor_tensor(ybuf[:], oT[:], hp[:, 15:16], zs[:], ALU.mult, ALU.mult).then_inc(S["g_y"], 1)
                e["counts"]["DV_G"] = n[0]

            with dve.Fori(0, GH - 1) as i:
                turn(i)
            turn(GH - 1)


def mix(dve, link, out, x, c, n_part=P, ctx=True, done=None):
    p = slice(0, n_part)
    lat_o, lat_x = out[p, 0:LAT], x[p, 0:LAT]
    link(dve.tensor_scalar(out[p, 0:TOK if ctx else LAT], x[p, 0:TOK if ctx else LAT], c[p, 0:1], None, ALU.mult))
    grid_o, grid_x = (v.rearrange("p (r w) -> p r w", w=64) for v in (lat_o, lat_x))
    pairs = [(grid_o[:, :, 1:64], grid_x[:, :, 0:63], 1), (grid_o[:, :, 0:63], grid_x[:, :, 1:64], 2),
             (lat_o[:, 64:LAT], lat_x[:, 0:LAT - 64], 3), (lat_o[:, 0:LAT - 64], lat_x[:, 64:LAT], 4)]
    if ctx:
        pairs += [(out[p, LAT + 1:TOK], x[p, LAT:TOK - 1], 5), (out[p, LAT:TOK - 1], x[p, LAT + 1:TOK], 6)]
    for o, s, k in pairs:
        ins = dve.scalar_tensor_tensor(o, s, c[p, k:k + 1], o, ALU.mult, ALU.add)
        if done is None or k < pairs[-1][2]:
            link(ins)
        else:
            ins.then_inc(done, 1)


def phase_lora(nc, e):
    io, carve, S, pj, pr, RP, ring, hT = (e[k] for k in ("io", "carve", "S", "pj", "pr", "RP", "ring", "hT"))
    w_loaded, w_used = e["w_loaded"], e["w_used"]
    lora = carve(4, TOK)
    raw = carve(4, TOK)
    lc = carve(4, 7)
    half = io["base_l"]
    C, cst = e["C"], e["cst"]

    with nc.Block() as block:
        @block.sync
        def _(sp):
            for n in range(8):
                sp.wait_ge(w_used, half + n - RING + 1)
                sp.dma_start(ring[:, n % RING, :, 0:LORA], io["w_l"][n // 2, :, n % 2 * HK:(n % 2 + 1) * HK]).then_inc(w_loaded[n % RING], 16)

        @block.tensor
        def _(pe):
            for j in range(4):
                if j:
                    pe.wait_ge(S["l_raw"], 2 * j)
                for hf in range(2):
                    s = (2 * j + hf) % RING
                    pe.wait_ge(w_loaded[s], loads(half) + (j // 2 + 1) * 16)
                    for k in range(HK):
                        kk = hf * HK + k
                        pe.matmul(pj[0][0:LORA, 0:LAT], ring[:, s, k, 0:LORA], hT[:, kk, 0:LAT], start=kk == 0, stop=kk == KT - 1)
                        last = pe.matmul(pj[2][0:LORA, 0:CTX], ring[:, s, k, 0:LORA], hT[:, kk, LAT:TOK],
                                         start=kk == 0, stop=kk == KT - 1)
                    last.then_inc(w_used, 1)

        @block.scalar
        def _(act):
            for j in range(4):
                act.wait_ge(w_used, half + 2 * j + 2)
                act.activation(raw[0:LORA, j, 0:LAT], pj[0][0:LORA, 0:LAT], ACT.Copy).then_inc(S["l_raw"], 1)
                act.activation(raw[0:LORA, j, LAT:TOK], pj[2][0:LORA, 0:CTX], ACT.Copy).then_inc(S["l_raw"], 1)
            for j in range(2):
                act.wait_ge(S["l_mix"], j + 1)
                act.activation(lora[0:LORA, j], lora[0:LORA, j], ACT.Tanh).then_inc(S["l_th"], 1)
            act.wait_ge(S["l_th"], 2)

        @block.vector
        def _(dve):
            n = [0]

            def link(ins):
                n[0] += 1
                ins.then_inc(S["l_v"], 1)
                dve.wait_ge(S["l_v"], n[0])

            kinds = cst[:, C["kinds"]:C["kinds"] + 24 * 7].rearrange("p (h j k) -> p h j k", h=8, k=7)
            mu = pr("mu", 24).rearrange("p (h j) -> p h j", h=8)
            for j in range(3):
                tab = RP[:, :, 7 * j:7 * j + 7]
                link(dve.tensor_tensor(tab, kinds[:, :, j], mu[:, :, j:j + 1].to_broadcast([P, 8, 7]), ALU.mult))
                link(dve.tensor_scalar(tab[:, :, 0:1], tab[:, :, 0:1], 1.0, None, ALU.add))
            link(dve.tensor_copy(RP[:, :, R_W0:R_NPAR], pr("rp", 80).rearrange("p (h c) -> p h c", h=8)))
            link(dve.tensor_scalar(RP[:, :, R_KA1:R_KA1 + 1], RP[:, :, R_KA:R_KA + 1], -1.0, 1.0, ALU.mult, ALU.add))
            lk = cst[:, C["lkinds"]:C["lkinds"] + 7]
            for j in range(4):
                link(dve.tensor_scalar(lc[:, j], lk, pr("mul", 4)[:, j:j + 1], None, ALU.mult))
                link(dve.tensor_scalar(lc[:, j, 0:1], lc[:, j, 0:1], 1.0, None, ALU.add))
            for j in range(4):
                dve.wait_ge(S["l_raw"], 2 * j + 2)
                mix(dve, link, lora[:, j], raw[:, j], lc[:, j], LORA, done=S["l_mix"])
            dve.wait_ge(S["l_mix"], 4)


def r_slots(d, hh):
    return sorted(R_ORDER[d][6 * hh:6 * hh + 6])


def r_out(hh, j, d):
    return 2 * (j - 4) + d if hh == 0 else 4 + 2 * j + d


def r_segs(d, hh):
    s, out = r_slots(d, hh), []
    for n, c in enumerate(s):
        if n and s[n - 1] == c - 1:
            out[-1][1] += 64
        else:
            out.append([64 * c, 64, n])
    return out


def phase_rwkv(nc, e):
    io, carve, S, pj, xu, tp, ident, blk, istk, lmask, incl, strict, rst, RP = (
        e[k] for k in ("io", "carve", "S", "pj", "xu", "tp", "ident", "blk", "istk", "lmask", "incl", "strict", "rst", "RP"))
    ydram, w_used = e["ydram"], e["w_used"]
    LV = LEVELS - 1
    lora = carve(4, TOK)
    tmp = carve(7, 384)
    sg, av, cs, gi, gn, bb, kd = (tmp[:, k] for k in range(7))
    flat = tmp.rearrange("p a b -> p (a b)")
    raw = [flat[:, 0:LAT], flat[:, LAT:LAT + TOK], flat[:, LAT + TOK:LAT + 2 * TOK]]
    sq, nr = flat[:, 0:TOK], flat[:, TOK:2 * TOK]
    r, k, v, z = carve(LAT), carve(TOK), carve(TOK), carve(LAT)
    kk = carve(TOK)
    KX, BX, CX, RX = carve(2, UN, P), carve(2, UN, P), carve(2, UN, P), carve(2, UN, P)
    VX = carve(12, P)
    V = carve(12, 64)
    BT, CT = carve(2, UN, P), carve(2, UN, P)
    LT, T, TT = carve(2, UN, P), carve(2, UN, P), carve(2, UN, P)
    Xs = carve(2, UN, 64)
    LC, MB, MC = carve(2, UN, P), carve(2, UN, P), carve(2, UN, P)
    lw = carve(2, 2, P)
    kds = carve(LAT)
    O = carve(8, 64)
    W, SA, St = carve(2, 64), carve(2, 64), carve(2, 64)
    egc = carve(2, UN)
    rp = carve(R_NPAR)
    mean = carve(8)
    eps = carve(2)
    ybuf = T[:, 0, 0:4].rearrange("p a b -> p (a b)")
    zs = T[:, 1, 0:4].rearrange("p a b -> p (a b)")
    bon = TT[:, 0, 0:4].rearrange("p a b -> p (a b)")
    osq = TT[:, 1, 0:4].rearrange("p a b -> p (a b)")
    yT = tp[:, 1, 0:4].rearrange("p a b -> p (a b)")
    half = io["base_r"]
    wb = loads(half)
    DV = io["DV_R"]

    def diag(view, h):
        return view[64 * h:64 * h + 64, :, 64 * h:64 * h + 64]

    def chunk_s(d):
        return tp[:, d, 4]

    def chunk_o(d):
        return tp[:, d, 0]

    def chunked(view, h):
        return view[64 * h:64 * h + 64].rearrange("p (u t) -> p u t", t=64)

    unused = e["unused"]
    with nc.Block() as block:
        @block.gpsimd
        def _(pool):
            for n, name in enumerate(("r_y", "r_st", "r_raw")):
                pool.memset(unused[:, n:n + 1], 0.0).then_inc(S[name], 1)

        @block.sync
        def _(sp):
            def lora_up(i):
                sp.dma_start(lw[0:LORA].rearrange("p a b c -> p (a b c)"), io["w_lup"][bass.ds(i, 1)].rearrange("a p c -> p (a c)")).then_inc(S["r_lw"], 16)

            lora_up(0)
            load_tiles(sp, e, io["w_r"], half, 0, 0, 6)
            with sp.Fori(0, PAIRS - 1) as i:
                load_tiles(sp, e, io["w_r"], half, i, 6, 8)
                load_tiles(sp, e, io["w_r"], half, i + 1, 0, 4)
                sp.wait_ge(S["r_lo"], i * 4 + 4)
                lora_up(i + 1)
                load_tiles(sp, e, io["w_r"], half, i + 1, 4, 6)
            load_tiles(sp, e, io["w_r"], half, PAIRS - 1, 6, 8)

        @block.tensor
        def _(pe):
            def column(i, j, k0=0, k1=KT):
                if k0 == 0:
                    pe.wait_ge(S["r_raw"], 1 + i * 6 + (0, 1, 3, 5)[j])
                project(pe, e, i, j, wb, pj[0][:, 0:LAT], pj[2][:, 0:CTX] if j in (1, 2) else None, k0, k1)

            def turn(i, more):
                def fill_products(n):
                    if more:
                        column(i + 1, 0, 4 * n, 4 * n + 4)

                def fill(n):
                    if more and 3 <= n < 3 * LV:
                        column(i + 1, 1, n - 3, n - 2)
                        if n == 3 * LV - 1:
                            column(i + 1, 1, n - 2, KT)

                def fill_scan(n):
                    if more and n < KT:
                        column(i + 1, 2, n, n + 1)

                column(i, 3)
                pe.wait_ge(S["r_y"], 1 + i)
                pe.wait_ge(S["r_sq"], i * 2 + 1)
                pe.matmul(xu[0][:, 0:LAT], blk, sq[:, 0:LAT], start=True, stop=True)
                pe.matmul(xu[1][:, 0:CTX], blk, sq[:, LAT:TOK], start=True, stop=True).then_inc(S["r_ss"], 1)
                pe.wait_ge(S["r_vx"], i * 2 + 2)
                vt = tp[:, 0].rearrange("p u t -> p (u t)")
                for c in range(12):
                    last = pe.matmul(vt[:, 64 * c:64 * c + 64], VX[:, c], istk, start=True, stop=True)
                last.then_inc(S["r_vt"], 1)
                pe.wait_ge(S["r_lw"], i * 16 + 16)
                pe.wait_ge(S["r_kk"], i + 1)
                pe.wait_ge(S["r_vc"], i + 1)
                for hh in range(2):
                    m = i * 2 + hh
                    nl = 2 if hh == 0 else 6
                    for d in range(2):
                        if hh * 2 + d:
                            pe.wait_ge(S["r_sg"], i * 8 + (hh * 2 + d) * 2)
                        for q in range(2):
                            for t0, nt, s0 in r_segs(d, hh):
                                last = pe.matmul(xu[q][:, 64 * s0:64 * s0 + nt], lw[0:LORA, d, q], lora[0:LORA, 2 * q + d, t0:t0 + nt],
                                                 start=True, stop=True)
                        last.then_inc(S["r_lo"], 1)
                        if hh:
                            fill_products(d)
                    for d in range(2):
                        pe.wait_ge(S["r_xd"], m * 2 + d + 1)
                        for u in range(UN):
                            last = pe.matmul(tp[:, d, u], BX[:, d, u], KX[:, d, u], start=True, stop=True)
                        last.then_inc(S["r_p"], 1)
                        if hh:
                            fill_products(2 + d)
                    for d in range(2):
                        pe.wait_ge(S["r_pa"], m * 6 + d + 1)
                        for u in range(UN):
                            last = pe.transpose(tp[:, d, u], BX[:, d, u], ident)
                        last.then_inc(S["r_p"], 1)
                    for d in range(2):
                        pe.wait_ge(S["r_pa"], m * 6 + 2 + d + 1)
                        for u in range(UN):
                            last = pe.transpose(tp[:, d, u], CX[:, d, u], ident)
                        last.then_inc(S["r_p"], 1)
                    for d in range(2):
                        pe.wait_ge(S["r_pa"], m * 6 + 4 + d + 1)
                        for u in range(UN):
                            last = pe.matmul(tp[:, d, u], CX[:, d, u], KX[:, d, u], start=True, stop=True)
                        last.then_inc(S["r_q"], 1)
                    for d in range(2):
                        pe.wait_ge(S["r_pd"], m * 6 + d + 1)
                        for u in range(nl):
                            last = pe.matmul(tp[:, d, u], BX[:, d, u], RX[:, d, u], start=True, stop=True)
                        last.then_inc(S["r_q"], 1)
                    for d in range(2):
                        pe.wait_ge(S["r_pd"], m * 6 + 2 + d + 1)
                        for u in range(nl):
                            last = pe.matmul(tp[:, d, u], CX[:, d, u], RX[:, d, u], start=True, stop=True)
                        last.then_inc(S["r_q"], 1)
                    pe.wait_ge(S["r_pd"], m * 6 + 6)
                    invert_pe(pe, S, "r_", m, LV, LT, T, TT, Xs, tp, ident, fill if hh else None)
                    for d in range(2):
                        pe.wait_ge(S["r_tt"], m * 2 * LV + 2 * (LV - 1) + d + 1)
                    for j in range(UN):
                        at = [(d, R_ORDER[d][6 * hh + j], r_slots(d, hh).index(R_ORDER[d][6 * hh + j])) for d in range(2)]
                        for d, c, u in at:
                            pe.matmul(xu[d][:, 0:P], LC[:, d, u], twice(V[:, c]), start=True, stop=False)
                        for d, c, u in at:
                            pe.wait_ge(S["r_s"], i * 26 + hh * 12 + 2 * j + d + 1)
                            pe.matmul(xu[d][:, 0:P], KX[:, d, u], twice(St[:, d]), start=False, stop=True).then_inc(S["r_w"], 1)
                        for d, c, u in at:
                            pe.matmul(chunk_s(d), CT[:, d, u], twice(V[:, c]), start=True, stop=False)
                        if hh:
                            fill_scan(3 * j)
                        for d, c, u in at:
                            pe.wait_ge(S["r_wc"], m * 12 + 2 * j + d + 1)
                            pe.matmul(xu[d][:, P:2 * P], TT[:, d, u], twice(W[:, d]), start=True, stop=True).then_inc(S["r_sa"], 1)
                        for d, c, u in at:
                            if c < 8:
                                o = r_out(hh, j, d)
                                if o >= 2:
                                    pe.wait_ge(S["r_oa"], i * 16 + o - 1)
                                pe.matmul(chunk_o(d), RX[:, d, u], twice(St[:, d]), start=True, stop=False)
                                pe.matmul(chunk_o(d), MC[:, d, u], twice(V[:, c]), start=False, stop=False)
                        if hh:
                            fill_scan(3 * j + 1)
                        for d, c, u in at:
                            pe.wait_ge(S["r_sac"], m * 12 + 2 * j + d + 1)
                            pe.matmul(chunk_s(d), BT[:, d, u], twice(SA[:, d]), start=False, stop=True).then_inc(S["r_ds"], 1)
                        for d, c, u in at:
                            if c < 8:
                                pe.matmul(chunk_o(d), MB[:, d, u], twice(SA[:, d]), start=False, stop=True).then_inc(S["r_o"], 1)
                        if hh:
                            fill_scan(3 * j + 2)
                pe.wait_ge(S["r_rk"], i + 1)
                pe.matmul(pj[1][:, 0:LAT], blk, bon, start=True, stop=True).then_inc(S["r_bs"], 1)
                pe.wait_ge(S["r_yx"], i * 2 + 2)
                for c in range(8):
                    last = pe.matmul(yT[:, 64 * c:64 * c + 64], VX[:, c], istk, start=True, stop=True)
                last.then_inc(S["r_yt"], 1)

            for j in range(3):
                column(0, j)
            with pe.Fori(0, PAIRS - 1) as i:
                turn(i, True)
            turn(PAIRS - 1, False)

        @block.scalar
        def _(act):
            act.wait_ge(S["r_v0"], 7)
            dsts = [[raw[0]], [raw[1][:, 0:LAT], raw[1][:, LAT:TOK]], [raw[2][:, 0:LAT], raw[2][:, LAT:TOK]], [z]]

            def copy_column(i, j):
                act.wait_ge(w_used, half + i * 8 + 2 * j + 2)
                act.activation(dsts[j][0], pj[0][:, 0:LAT], ACT.Copy).then_inc(S["r_raw"], 1)
                if j in (1, 2):
                    act.activation(dsts[j][1], pj[2][:, 0:CTX], ACT.Copy).then_inc(S["r_raw"], 1)

            def turn(i, more):
                copy_column(i, 3)
                act.wait_ge(S["r_kr"], i + 1)
                act.activation(sq, kk[:], ACT.Square).then_inc(S["r_sq"], 1)
                for h in range(2):
                    act.activation(diag(VX, h), chunked(v, h), ACT.Copy).then_inc(S["r_vx"], 1)
                act.wait_ge(S["r_ss"], i + 1)
                act.activation(nr[:, 0:LAT], xu[0][:, 0:LAT], ACT.Sqrt, bias=eps[:, 0:1]).then_inc(S["r_rt"], 1)
                act.activation(nr[:, LAT:TOK], xu[1][:, 0:CTX], ACT.Sqrt, bias=eps[:, 0:1]).then_inc(S["r_rt"], 1)
                act.wait_ge(S["r_vt"], i + 1)
                act.activation(V[:].rearrange("p c t -> p (c t)"), tp[:, 0].rearrange("p u t -> p (u t)"), ACT.Copy).then_inc(S["r_vc"], 1)
                act.wait_ge(S["r_kk"], i + 1)
                for hh in range(2):
                    m = i * 2 + hh
                    for d in range(2):
                        act.wait_ge(S["r_lo"], m * 2 + d + 1)
                        if hh * 2 + d:
                            act.wait_ge(S["r_xd"], m * 2 + d)
                        act.activation(sg, xu[0][:, 0:384], ACT.Sigmoid, bias=rp[:, R_W0 + d:R_W0 + d + 1]).then_inc(S["r_sg"], 1)
                        act.activation(av, xu[1][:, 0:384], ACT.Sigmoid, bias=rp[:, R_A0 + d:R_A0 + d + 1]).then_inc(S["r_sg"], 1)
                        act.wait_ge(S["r_cs"], m * 2 + d + 1)
                        act.activation(gi, cs, ACT.Exp, scale=-EXPM).then_inc(S["r_ex"], 1)
                        act.activation(gn, cs, ACT.Exp, scale=EXPM).then_inc(S["r_ex"], 1)
                        act.activation(sg, sg, ACT.Exp, scale=-EXPM).then_inc(S["r_ex"], 1)
                    for q, dst in enumerate((LT, BT, CT)):
                        for d in range(2):
                            act.wait_ge(S["r_p"], m * 6 + 2 * q + d + 1)
                            act.activation(dst[:, d], tp[:, d], ACT.Copy).then_inc(S["r_pa"], 1)
                    if hh and more:
                        act.wait_ge(S["r_xd"], i * 4 + 4)
                        copy_column(i + 1, 0)
                    if hh == 0:
                        act.wait_ge(S["r_st"], 1 + i * 16)
                    invert_act(act, S, "r_", m, LV, T, TT, tp)
                    if hh and more:
                        copy_column(i + 1, 1)
                    for j in range(UN):
                        for d in range(2):
                            act.wait_ge(S["r_w"], m * 12 + 2 * j + d + 1)
                            if j:
                                act.wait_ge(S["r_sa"], m * 12 + 2 * (j - 1) + d + 1)
                            act.activation(W[:, d], xu[d][:, 0:64], ACT.Copy, scale=-1.0).then_inc(S["r_wc"], 1)
                if more:
                    copy_column(i + 1, 2)
                act.wait_ge(S["r_oc"], i + 1)
                act.activation(osq, O[:].rearrange("p c t -> p (c t)"), ACT.Square).then_inc(S["r_sq"], 1)
                act.wait_ge(S["r_vr"], i + 1)
                act.activation(mean[:], mean[:], ACT.Sqrt, bias=eps[:, 1:2], scale=1.0 / 64).then_inc(S["r_sd"], 1)
                act.activation(zs, z[:], ACT.Sigmoid).then_inc(S["r_zs"], 1)
                act.wait_ge(S["r_y"], 1 + i + 1)
                act.dma_start(ydram[bass.ds(i + 8, 1)].rearrange("a p t -> p (a t)"), ybuf).then_inc(S["r_st"], 16)

            for j in range(3):
                copy_column(0, j)
            with act.Fori(0, PAIRS - 1) as i:
                turn(i, True)
            turn(PAIRS - 1, False)
            act.wait_ge(S["r_st"], 1 + 16 * PAIRS)

        @block.vector
        def _(dve):
            dve.memset(eps[:, 0:1], 1e-6).then_inc(S["r_v0"], 1)
            dve.memset(eps[:, 1:2], 64e-5).then_inc(S["r_v0"], 1)
            for t in (KX, BX, CX, RX, VX):
                dve.memset(t[:], 0.0).then_inc(S["r_v0"], 1)
            dve.wait_ge(S["r_v0"], 7)

            def turn(i):
                dve.wait_ge(S["r_y"], 1 + i)
                n = [0]

                def link(ins):
                    n[0] += 1
                    ins.then_inc(S["r_v"], 1)
                    dve.wait_ge(S["r_v"], i * DV + n[0])

                link(dve.tensor_copy(rp[:], RP[:, bass.ds(i, 1)].rearrange("p a c -> p (a c)")))
                for d in range(2):
                    dve.memset(St[:, d], 0.0).then_inc(S["r_s"], 1)
                link(dve.memset(O[:], 0.0))
                link(dve.memset(kds[:], 0.0))
                for j, dst in enumerate((r, k, v)):
                    dve.wait_ge(S["r_raw"], 1 + i * 6 + (1, 3, 5)[j])
                    mix(dve, link, dst, raw[j], rp[:, 7 * j:7 * j + 7], ctx=j > 0)
                dve.tensor_scalar(kk[:], k[:], rp[:, R_KK:R_KK + 1], None, ALU.mult).then_inc(S["r_kr"], 1)
                dve.wait_ge(S["r_kr"], i + 1)
                dve.wait_ge(S["r_rt"], i * 2 + 2)
                link(dve.reciprocal(nr, nr))
                dve.tensor_tensor(kk[:], kk[:], nr, ALU.mult).then_inc(S["r_kk"], 1)
                dve.wait_ge(S["r_kk"], i + 1)
                for hh in range(2):
                    m = i * 2 + hh
                    nl = 2 if hh == 0 else 6
                    for d in range(2):
                        back = slice(None, None, -1 if d else 1)
                        dve.wait_ge(S["r_sg"], m * 4 + 2 * d + 2)
                        link(dve.tensor_tensor_scan(cs[:, back], rst[d][:, back], sg[:, back], 0.0, ALU.mult, ALU.add))
                        dve.tensor_tensor(sg, cs, sg, ALU.subtract).then_inc(S["r_cs"], 1)
                        link(dve.tensor_scalar(kd, av, rp[:, R_KA:R_KA + 1], rp[:, R_KA1:R_KA1 + 1], ALU.mult, ALU.add))
                        for t0, nt, s0 in r_segs(d, hh):
                            o = slice(64 * s0, 64 * s0 + nt)
                            dve.tensor_tensor(bb[:, o], kk[:, t0:t0 + nt], av[:, o], ALU.mult)
                            link(dve.tensor_tensor(kd[:, o], kd[:, o], k[:, t0:t0 + nt], ALU.mult))
                            if t0 < LAT:
                                w = min(nt, LAT - t0)
                                link(dve.tensor_tensor(kds[:, t0:t0 + w], kds[:, t0:t0 + w], kd[:, 64 * s0:64 * s0 + w], ALU.add))
                        dve.wait_ge(S["r_ex"], m * 6 + 3 * d + 3)
                        for h in range(2):
                            dve.tensor_tensor(diag(BX[:, d], h), chunked(bb, h), chunked(gn, h), ALU.mult)
                            dve.tensor_tensor(diag(CX[:, d], h), chunked(kd, h), chunked(gn, h), ALU.mult)
                            for t0, nt, s0 in r_segs(d, hh):
                                us = slice(s0, s0 + nt // 64)
                                dve.tensor_tensor(diag(KX[:, d], h)[:, us], chunked(kk, h)[:, t0 // 64:(t0 + nt) // 64],
                                                  chunked(sg, h)[:, us], ALU.mult)
                            t0 = r_segs(d, hh)[0][0]
                            dve.tensor_tensor(diag(RX[:, d], h)[:, 0:nl], chunked(r, h)[:, t0 // 64:t0 // 64 + nl],
                                              chunked(gi, h)[:, 0:nl], ALU.mult)
                        end = 0 if d else 63
                        dve.tensor_copy(egc[:, d], gi[:, end:384:64]).then_inc(S["r_xd"], 1)
                    for d in range(2):
                        dve.wait_ge(S["r_pa"], m * 6 + d + 1)
                        invert_start(dve, S, "r_", link, d, LT, TT, Xs, ident)
                    for q, (dst, mask, nu) in enumerate(((LC, strict, UN), (MB, incl, nl), (MC, incl, nl))):
                        for d in range(2):
                            dve.wait_ge(S["r_q"], m * 6 + 2 * q + d + 1)
                            dve.tensor_tensor(dst[:, d, 0:nu], tp[:, d, 0:nu], mask[d].unsqueeze(1).to_broadcast([P, nu, P]),
                                              ALU.mult).then_inc(S["r_pd"], 1)
                    invert_dve(dve, S, "r_", m, LV, T, Xs, tp, lmask)
                    for j in range(UN):
                        at = [(d, R_ORDER[d][6 * hh + j], r_slots(d, hh).index(R_ORDER[d][6 * hh + j])) for d in range(2)]
                        for d, c, u in at:
                            dve.wait_ge(S["r_sa"], m * 12 + 2 * j + d + 1)
                            dve.tensor_copy(SA[:, d], xu[d][:, P:P + 64]).then_inc(S["r_sac"], 1)
                        for d, c, u in at:
                            last = dve.tensor_scalar(LT[:, d, 0, 0:64], St[:, d], egc[:, d, u:u + 1], None, ALU.mult)
                        link(last)
                        for d, c, u in at:
                            dve.wait_ge(S["r_ds"], m * 12 + 2 * j + d + 1)
                            dve.scalar_tensor_tensor(St[:, d], chunk_s(d)[:, 0:64], egc[:, d, u:u + 1], LT[:, d, 0, 0:64],
                                                     ALU.mult, ALU.add).then_inc(S["r_s"], 1)
                        for d, c, u in at:
                            if c < 8:
                                o = r_out(hh, j, d)
                                dve.wait_ge(S["r_o"], i * 16 + o + 1)
                                if o:
                                    dve.wait_ge(S["r_oa"], i * 16 + o)
                                dve.tensor_tensor(O[:, c], O[:, c], chunk_o(d)[:, 0:64], ALU.add).then_inc(S["r_oa"], 1)
                dve.wait_ge(S["r_oa"], i * 16 + 16)
                link(dve.tensor_reduce(mean[:], O[:], AX_X, ALU.add))
                link(dve.tensor_scalar(mean[:], mean[:], 1.0 / 64, None, ALU.mult))
                dve.tensor_tensor(O[:], O[:], mean.unsqueeze(2).to_broadcast([P, 8, 64]), ALU.subtract).then_inc(S["r_oc"], 1)
                link(dve.tensor_tensor(bon, r[:], kds[:], ALU.mult))
                dve.tensor_scalar(bon, bon, rp[:, R_RK:R_RK + 1], None, ALU.mult).then_inc(S["r_rk"], 1)
                dve.wait_ge(S["r_oc"], i + 1)
                dve.wait_ge(S["r_sq"], i * 2 + 2)
                dve.tensor_reduce(mean[:], osq.rearrange("p (c t) -> p c t", t=64), AX_X, ALU.add).then_inc(S["r_vr"], 1)
                dve.wait_ge(S["r_sd"], i + 1)
                link(dve.reciprocal(mean[:], mean[:]))
                for h in range(2):
                    hs = slice(64 * h, 64 * h + 64)
                    dve.tensor_tensor(diag(VX[:, 0:8], h), O[hs], mean[hs].unsqueeze(2).to_broadcast([64, 8, 64]), ALU.mult).then_inc(S["r_yx"], 1)
                dve.wait_ge(S["r_bs"], i + 1)
                link(dve.tensor_tensor(kds[:], v[:, 0:LAT], pj[1][:, 0:LAT], ALU.mult))
                dve.wait_ge(S["r_zs"], i + 1)
                link(dve.tensor_tensor(z[:], z[:], zs, ALU.mult))
                dve.wait_ge(S["r_yt"], i + 1)
                link(dve.scalar_tensor_tensor(kds[:], yT, rp[:, R_GG:R_GG + 1], kds[:], ALU.mult, ALU.add))
                dve.scalar_tensor_tensor(ybuf, kds[:], rp[:, R_GB:R_GB + 1], z[:], ALU.add, ALU.mult).then_inc(S["r_y"], 1)
                e["counts"]["DV_R"] = n[0]

            with dve.Fori(0, PAIRS - 1) as i:
                turn(i)
            turn(PAIRS - 1)


def stream(sp, e, src, half, tiles, start=0):
    ring, w_loaded, w_used = e["ring"], e["w_loaded"], e["w_used"]
    with sp.Fori(start, tiles // 2) as i:
        for s in range(RING):
            sp.wait_ge(w_used, half + (i - 1) * RING + s + 1)
            sp.dma_start(ring[:, s], src[bass.ds(i * 2 + s // 2, 1), :, (s % 2) * HK:(s % 2 + 1) * HK]
                         .rearrange("a p k c -> p (a k) c")).then_inc(w_loaded[s], 16)


DONE = 2


def split_weights(pool, e, done, loaded, first, halves_n):
    S, ring, w_loaded, w_used = (e[k] for k in ("S", "ring", "w_loaded", "w_used"))
    hi, lo = e["parts"]
    one = e["ones"][:, 0:1].to_broadcast([P, HK * P])
    with pool.Fori(0, halves_n // RING) as i:
        for s in range(RING):
            h, l = hi[:, s % 2], lo[:, s % 2]
            w = ring[:, s].rearrange("p k c -> p (k c)")
            pool.wait_ge(w_loaded[s], loaded + 16 + i * 16)
            pool.wait_ge(S[done], DONE + first + i * RING + s - 1)
            pool.tensor_tensor(h, w, one, ALU.mult).then_inc(S[done + "h"], 1)
            pool.wait_ge(S[done + "h"], first + i * RING + s + 1)
            pool.tensor_tensor(l, w, h.bitcast(F32), ALU.subtract).then_inc(w_used, 1)


def column_tile(pe, e, done, lat, ready):
    S, high, low, w_used = (e[k] for k in ("S", "high", "low", "w_used"))
    w_high, w_low = e["parts"]
    for hf in range(2):
        pe.wait_ge(w_used, ready + hf)
        wh, wl = w_high[:, hf], w_low[:, hf]
        for k in range(HK):
            kk = hf * HK + k
            c = slice(k * P, k * P + P)
            ah, al = high[:, kk], low[:, kk]
            pe.matmul(lat, wh[:, c], ah, start=kk == 0, stop=False)
            pe.matmul(lat, wh[:, c], al, start=False, stop=False)
            last = pe.matmul(lat, wl[:, c], ah, start=False, stop=kk == KT - 1)
        last.then_inc(S[done], 1)


def phase_out(nc, e):
    io, carve, S, pj, gate, mod2, pr, ones = (e[k] for k in ("io", "carve", "S", "pj", "gate", "mod2", "pr", "ones"))
    ydram, w_used, bias_rows, cst, C = e["ydram"], e["w_used"], e["bias_rows"], e["cst"], e["C"]
    xdram, x_saved, unused = e["xdram"], e["x_saved"], e["unused"]
    high, low = e["high"], e["low"]
    X = carve(KT, LAT)
    whole = carve(KT, LAT)
    sq = carve(2, LAT)
    rstd = carve(LAT)
    scl = carve(KT)
    win = carve(768)
    rel = carve(384)
    eps = carve(1)
    half = io["base_o"]
    banks = [pj[0][:, 0:LAT], e["xu"][0][:, 0:LAT]]

    with nc.Block() as block:
        @block.gpsimd
        def _(pool):
            pool.memset(unused[:, 0:1], 0.0).then_inc(S["o_r"], 2)
            pool.memset(unused[:, 1:2], 0.0).then_inc(S["o_done"], DONE)
            split_weights(pool, e, "o_done", loads(half), 0, 2 * KT)

        @block.sync
        def _(sp):
            for q in range(4):
                sp.dma_start(whole[:, 4 * q:4 * q + 4], ydram[4 * q:4 * q + 4].rearrange("k p t -> p k t")).then_inc(S["o_y"], 16)
            stream(sp, e, io["w_out"], half, KT)

        @block.scalar
        def _(act):
            act.dma_start(win[0:32], io["win"]).then_inc(S["o_w"], 16)
            act.dma_start(X[:], io["xT"]).then_inc(S["o_x"], 16)
            act.wait_ge(S["o_y"], 64)
            for k in range(KT):
                act.activation(high[:, k], whole[:, k], ACT.Copy).then_inc(S["o_yh"], 1)
            act.wait_ge(S["o_b"], 1)
            act.dma_start(bias_rows, rel[0:16]).then_inc(S["o_bd"], 16)
            act.wait_ge(S["o_bd"], 16)
            copies = bass.AP(tensor=e["bias_copies_t"], offset=0, ap=[[P * 384, 16], [384, P], [1, 384]])
            rows = bass.AP(tensor=bias_rows.tensor, offset=0, ap=[[384, 16], [0, P], [1, 384]])
            act.dma_start(copies, rows).then_inc(S["o_bd"], 16)
            act.wait_ge(S["o_bd"], 32)
            skew = bass.AP(tensor=e["bias_copies_t"], offset=127, ap=[[383, P], [P * 384, 16], [1, 256]])
            act.dma_start(e["bias"][:], skew).then_inc(S["o_bd"], 16)
            act.wait_ge(S["o_bd"], 48)
            with act.Fori(0, KT // 2) as i:
                for t in range(2):
                    act.wait_ge(S["o_r"], 2 + i * 2 + t + 1)
                    act.wait_ge(S["o_ss"], i * 2 + 1)
                    act.activation(sq[:, t], X[:, bass.ds(i * 2 + t, 1)].rearrange("p a t -> p (a t)"), ACT.Square).then_inc(S["o_sq"], 1)
            act.wait_ge(S["o_ss"], KT + 1)
            act.wait_ge(S["o_v"], 1)
            act.activation(rstd[:], pj[2][:, 0:LAT], ACT.Sqrt, bias=eps[:], scale=1.0 / D).then_inc(S["o_rt"], 1)
            act.wait_ge(S["o_done"], DONE + 2 * KT)
            for k in range(KT):
                act.wait_ge(S["o_n"], k + 1)
                act.activation(whole[:, k], X[:, k], ACT.Identity, bias=mod2[:, k:k + 1], scale=scl[:, k:k + 1]).then_inc(S["o_h"], 1)
                if k:
                    act.wait_ge(S["o_h"], k)
                    act.activation(high[:, k - 1], whole[:, k - 1], ACT.Copy).then_inc(S["o_hh"], 1)
            act.wait_ge(S["o_h"], KT)
            act.activation(high[:, KT - 1], whole[:, KT - 1], ACT.Copy).then_inc(S["o_hh"], 1)
            act.dma_start(xdram.rearrange("k p t -> p k t"), X[:]).then_inc(x_saved, 16)

        @block.tensor
        def _(pe):
            pe.wait_ge(S["o_w"], 16)
            pe.matmul(pj[1][0:16, 0:384], pr("rel", 16)[0:32], win[0:32, 0:384], start=True, stop=True).then_inc(S["o_bm"], 1)
            pe.wait_ge(S["o_v"], 2)
            pe.matmul(pj[2][:, 0:LAT], ones, sq[:, 0], start=True, stop=True).then_inc(S["o_ss"], 1)
            pe.wait_ge(S["o_yl"], KT)
            with pe.Fori(0, KT // 2) as i:
                for t in range(2):
                    pe.wait_ge(S["o_r"], 1 + i * 2 + t)
                    column_tile(pe, e, "o_done", banks[t], half + i * 4 + 2 * t + 1)
                for t in range(2):
                    pe.wait_ge(S["o_sq"], i * 2 + t + 1)
                    pe.matmul(pj[2][:, 0:LAT], ones, sq[:, t], start=False, stop=True,
                              skip_group_check=True).then_inc(S["o_ss"], 1)

        @block.vector
        def _(dve):
            dve.memset(eps[:], 1e-6).then_inc(S["o_v"], 1)
            dve.memset(sq[:, 0], 0.0).then_inc(S["o_v"], 1)
            for k in range(KT):
                dve.wait_ge(S["o_yh"], k + 1)
                dve.tensor_tensor(low[:, k], whole[:, k], high[:, k].bitcast(F32), ALU.subtract).then_inc(S["o_yl"], 1)
            dve.wait_ge(S["o_bm"], 1)
            dve.tensor_tensor(rel[0:16], pj[1][0:16, 0:384], win[0:16, 384:768], ALU.add).then_inc(S["o_b"], 1)
            dve.wait_ge(S["o_x"], 16)
            with dve.Fori(0, KT // 2) as i:
                for t in range(2):
                    dve.wait_ge(S["o_done"], DONE + i * RING + 2 * t + 2)
                    x = X[:, bass.ds(i * 2 + t, 1)].rearrange("p a t -> p (a t)")
                    g = gate[:, bass.ds(i * 2 + t, 1)]
                    dve.scalar_tensor_tensor(x, banks[t], g, x, ALU.mult, ALU.add).then_inc(S["o_r"], 1)
            dve.tensor_scalar(scl[:], mod2[:, KT:2 * KT], 1.0, None, ALU.add).then_inc(S["o_v"], 1)
            dve.wait_ge(S["o_rt"], 1)
            dve.reciprocal(rstd[:], rstd[:]).then_inc(S["o_v"], 1)
            dve.wait_ge(S["o_v"], 4)
            for k in range(KT):
                dve.scalar_tensor_tensor(X[:, k], X[:, k], pr("fng", KT)[:, k:k + 1], rstd[:], ALU.mult, ALU.mult).then_inc(S["o_n"], 1)
            for k in range(KT):
                dve.wait_ge(S["o_hh"], k + 1)
                dve.tensor_tensor(low[:, k], whole[:, k], high[:, k].bitcast(F32), ALU.subtract).then_inc(S["o_hl"], 1)
            dve.wait_ge(S["o_hl"], KT)


ALPHA = 2.0 ** 0.25


def phase_two(nc, e):
    io, ring, carve, S, pj, xu, tp8, pr, ones, ident, mod2, out = (
        e[k] for k in ("io", "ring", "carve", "S", "pj", "xu", "tp8", "pr", "ones", "ident", "mod2", "out"))
    w_loaded, w_used = e["w_loaded"], e["w_used"]
    high, low, bias = e["high"], e["low"], e["bias"]
    x_at = e["at"][0]
    Y = carve(8, LAT)
    uc = carve(8, LAT)
    X = e["arena"][:, x_at:x_at + KT * LAT].rearrange("p (k t) -> p k t", k=KT)
    kT = carve(4, LAT)
    V = carve(4, 256)
    at0 = e["at"][0]
    ks_buf = carve(LAT)
    qs, vs, ab, sb_ = carve(2, LAT), carve(4, 64), carve(LAT), carve(LAT)
    ub = carve(LAT + 30)
    ca = carve(LAT)
    sc = carve(4, 256)
    pT = carve(8, P)
    at_ = carve(2, LAT)
    ga, gs = carve(LAT), carve(LAT)
    cw, mx, sm, rd, sk, es = carve(2, 32), carve(4), carve(4), carve(4), carve(4), carve(4)
    e["at"][0] = at0
    gcv = carve(8, LAT)
    sq = carve(2, LAT)
    mean, rstd = carve(LAT), carve(LAT)
    sa_ = carve(LAT)
    eps = carve(1)
    graw = carve(2, LAT)
    yc = carve(LAT)
    half = io["base_2"]
    wb = loads(half)
    DV = io["DV_2"]
    A = 8
    BODY = 16
    half_g = half + A + 4 * BODY
    half_p = half_g + 16
    banks = [pj[0][:, 0:LAT], xu[0][:, 0:LAT]]
    half_o = half_p
    x_saved, xdram = e["x_saved"], e["xdram"]
    SLOT0 = {s: A // RING for s in range(RING)}

    unused = e["unused"]
    with nc.Block() as block:
        @block.gpsimd
        def _(pool):
            for n, name in enumerate(("n_pw", "n_y", "n_cv", "n_ev", "z_g", "z_gm", "z_y")):
                pool.memset(unused[:, n:n + 1], 0.0).then_inc(S[name], 1)
            pool.memset(unused[:, 7:8], 0.0).then_inc(S["z_r"], 2)
            pool.memset(unused[:, 8:9], 0.0).then_inc(S["n_done"], DONE)
            split_weights(pool, e, "n_done", loads(half), 0, A + 4 * BODY + 16)
            split_weights(pool, e, "n_done", loads(half_p) + 2 * 16, A + 4 * BODY + 16, 2 * KT)

        @block.sync
        def _(sp):
            stream(sp, e, io["w_kv"], half, 4)
            sp.wait_ge(S["n_kv"], 2)
            for g in range(4):
                a, b = 64 * (g % 2), 64 - 64 * (g % 2)
                sp.dma_start(kT[b:b + 64, g], kT[a:a + 64, g]).then_inc(S["n_dup"], 16)
            stream(sp, e, io["w_2"], half + A, 32)
            stream(sp, e, io["w_gc"], half_g, 8)
            with sp.Fori(0, 2) as i:
                for s in range(RING):
                    sp.wait_ge(w_used, half_p - RING + s + 1)
                    sp.wait_ge(S["n_pw"], 1 + i * RING)
                    sp.dma_start(ring[:, s], io["w_pw"][bass.ds(i * RING + s, 1)].rearrange("a p k c -> p (a k) c")).then_inc(w_loaded[s], 16)
            sp.wait_ge(x_saved, 16)
            sp.wait_ge(S["n_ysl"], 8)
            sp.dma_start(X[:, 0:8], xdram[0:8].rearrange("k p t -> p k t")).then_inc(S["n_xa"], 16)
            for n in range(RING):
                sp.wait_ge(S["n_pw"], 1 + RING + n + 1)
                sp.dma_start(ring[:, n], io["w_out2"][n // 2, :, n % 2 * HK:(n % 2 + 1) * HK]).then_inc(w_loaded[n], 16)
            sp.wait_ge(S["n_pw"], 1 + 8)
            sp.dma_start(X[:, 8:16], xdram[8:16].rearrange("k p t -> p k t")).then_inc(S["n_xa"], 16)
            stream(sp, e, io["w_out2"], half_o, KT, 1)
            for k in range(4):
                sp.wait_ge(S["z_o"], 4 * k + 4)
                sp.dma_start(out[4 * k:4 * k + 4].rearrange("k p t -> p k t"), X[:, 4 * k:4 * k + 4]).then_inc(S["z_st"], 16)
            sp.wait_ge(S["z_st"], 64)

        @block.tensor
        def _(pe):
            P0 = pj[0][:, 0:LAT]
            for j in range(4):
                if j:
                    pe.wait_ge(S["n_kv"], j)
                column_tile(pe, e, "n_done", P0, half + 2 * j + 1)
            pe.wait_ge(S["n_kv"], 4)
            for j in range(2):
                for t in range(4):
                    last = pe.transpose(tp8[:, j, t], qs[:, j, t * P:t * P + P], ident)
            last.then_inc(S["n_vt"], 1)
            pe.wait_ge(S["n_dup"], 64)
            pe.wait_ge(S["n_kv"], 6)
            with pe.Fori(0, 4) as i:
                tiles = [0]

                def tile():
                    t = tiles[0]
                    tiles[0] += 1
                    pe.wait_ge(S["n_ev"], 1 + i * 8 + t)
                    column_tile(pe, e, "n_done", P0, half + A + i * BODY + 2 * t + 1)

                def scores(h):
                    if h >= 2:
                        pe.wait_ge(S["n_at"], i * 2 + h // 2)
                    hs = slice(64 * (h % 2), 64 * (h % 2) + 64)
                    q, k = qs[hs, h // 2], ks[hs]
                    for n in range(4):
                        a = 0 if n else P
                        last = pe.matmul(tp8[:, h % 2].rearrange("p a b -> p (a b)")[:, 256 * n + a:256 * n + 256], q[:, n * P:n * P + P],
                                         k[:, (n - 1) * P + a:(n + 1) * P], start=True, stop=True)
                    last.then_inc(S["n_sc"], 1)

                def turn(h):
                    pe.wait_ge(S["n_p"], i * 4 + h + 1)
                    for n in range(4):
                        for c in range(2):
                            if n or c:
                                last = pe.transpose(xu[n // 2][:, (2 * n + c) % 4 * P:(2 * n + c) % 4 * P + P], sc[:, n, c * P:c * P + P], ident)
                    last.then_inc(S["n_tr"], 1)

                def values(h):
                    pe.wait_ge(S["n_pt"], i * 8 + 2 * h + 2)
                    hs = slice(64 * (h % 2), 64 * (h % 2) + 64)
                    for n in range(4):
                        o = pj[2][hs, n * P:n * P + P]
                        if n:
                            pe.matmul(o, vs[:, n - 1], pT[:, 2 * n], start=True, stop=False)
                        last = pe.matmul(o, vs[:, n], pT[:, 2 * n + 1], start=not n, stop=True)
                    last.then_inc(S["n_pv"], 1)

                ks = ks_buf
                pe.wait_ge(S["n_y"], 1 + i * 2)
                tile()
                tile()
                pe.wait_ge(S["n_ev"], 1 + i * 8 + 2)
                pe.wait_ge(S["n_ks"], i * 2 + 2)
                scores(0)
                tile()
                turn(0)
                scores(1)
                tile()
                values(0)
                turn(1)
                tile()
                values(1)
                scores(2)
                tile()
                turn(2)
                scores(3)
                tile()
                values(2)
                turn(3)
                tile()
                values(3)
            with pe.Fori(0, 4) as i:
                for t in range(2):
                    if t:
                        pe.wait_ge(S["z_g"], 1 + i * 2 + 1)
                    else:
                        pe.wait_ge(S["z_g"], 1 + i * 2)
                        pe.wait_ge(S["n_ev"], 1 + 32)
                    column_tile(pe, e, "n_done", P0, half_g + i * RING + 2 * t + 1)
            pe.wait_ge(S["n_cv"], 1 + 8)
            for k in range(8):
                last = pe.matmul(pj[2][:, 0:LAT], ones, uc[:, k], start=k == 0, stop=k == 7)
            last.then_inc(S["z_s"], 1)
            for k in range(8):
                pe.wait_ge(S["z_sq"], k + 1)
                last = pe.matmul(pj[2][:, 0:LAT], ones, sq[:, k % 2], start=k == 0, stop=k == 7)
                last.then_inc(S["z_ss"], 1)
            pe.wait_ge(S["z_u"], 8)
            pe.wait_ge(S["z_g"], 1 + 8)
            with pe.Fori(0, 2) as i:
                for t in range(4):
                    pe.wait_ge(S["z_y"], 1 + i * 4 + t)
                    pe.wait_ge(w_loaded[t], loads(half_p) + (i + 1) * 16)
                    for k in range(8):
                        last = pe.matmul(P0, ring[:, t, k], uc[:, k], start=k == 0, stop=k == 7)
                    last.then_inc(S["n_pw"], 1)
            pe.wait_ge(S["z_y"], 1 + 8)
            pe.wait_ge(S["n_y"], 1 + 8)
            pe.wait_ge(S["n_ysl"], KT)
            with pe.Fori(0, KT // 2) as i:
                for t in range(2):
                    pe.wait_ge(S["z_r"], 1 + i * 2 + t)
                    column_tile(pe, e, "n_done", banks[t], half_o + i * RING + 2 * t + 1)
            pe.wait_ge(S["z_r"], 2 + KT)
            for k in range(KT):
                last = pe.matmul(pj[2][:, 0:LAT], ones, X[:, k], start=k == 0, stop=k == KT - 1)
            last.then_inc(S["z_s"], 1)
            for k in range(KT):
                pe.wait_ge(S["z_sq"], 8 + k + 1)
                last = pe.matmul(pj[2][:, 0:LAT], ones, sq[:, k % 2], start=k == 0, stop=k == KT - 1)
                last.then_inc(S["z_ss"], 1)

        @block.scalar
        def _(act):
            P0 = pj[0][:, 0:LAT]
            for j in range(2):
                act.wait_ge(S["n_done"], DONE + 2 * j + 2)
                for g in (2 * j, 2 * j + 1):
                    a = 64 * (g % 2)
                    last = act.activation(kT[a:a + 64, g], pj[0][a:a + 64, 0:LAT], ACT.Copy)
                last.then_inc(S["n_kv"], 1)
            for j in range(2):
                act.wait_ge(S["n_done"], DONE + 4 + 2 * j + 2)
                act.activation(qs[:, j], P0, ACT.Copy).then_inc(S["n_kv"], 1)
            act.wait_ge(S["n_vt"], 1)
            for j in range(2):
                act.activation(V[:, :, j * P:j * P + P], tp8[:, j, 0:4], ACT.Copy).then_inc(S["n_kv"], 1)
            act.wait_ge(S["n_dup"], 64)
            act.wait_ge(S["n_kv"], 6)
            with act.Fori(0, 4) as i:
                hw = DONE + A + i * BODY
                act.wait_ge(S["n_y"], 1 + i * 2)
                act.wait_ge(S["n_cv"], 1 + i * 2)
                act.activation(ks_buf, kT[:, bass.ds(i, 1)].rearrange("p a t -> p (a t)"), ACT.Copy).then_inc(S["n_ks"], 1)
                act.activation(vs[:], V[:].rearrange("p t (g c) -> p t g c", g=4)[:, :, bass.ds(i, 1)].rearrange("p t a c -> p t (a c)"),
                               ACT.Copy).then_inc(S["n_ks"], 1)

                def soft(h):
                    act.wait_ge(S["n_m"], i * 4 + h + 1)
                    for n in range(4):
                        act.activation(sc[:, n], sc[:, n], ACT.Exp, bias=mx[:, n:n + 1], accum_out=sm[:, n:n + 1])
                    act.activation(es[:], mx[:], ACT.Exp, bias=sk[:, h:h + 1]).then_inc(S["n_x"], 1)

                def flip(h):
                    act.wait_ge(S["n_tr"], i * 4 + h + 1)
                    if h:
                        act.wait_ge(S["n_pv"], i * 4 + h)
                    act.activation(pT[:, 1:4].rearrange("p a b -> p (a b)"), xu[0][:, P:4 * P], ACT.Copy).then_inc(S["n_pt"], 1)
                    act.activation(pT[:, 4:8].rearrange("p a b -> p (a b)"), xu[1][:], ACT.Copy).then_inc(S["n_pt"], 1)

                def heads(j):
                    act.wait_ge(S["n_pv"], i * 4 + 2 * j + 2)
                    act.activation(at_[:, j], pj[2][:, 0:LAT], ACT.Copy).then_inc(S["n_at"], 1)

                act.wait_ge(S["n_done"], hw + 2)
                act.activation(qs[:, 0], P0, ACT.Copy).then_inc(S["n_ev"], 1)
                act.wait_ge(S["n_done"], hw + 4)
                act.activation(qs[:, 1], P0, ACT.Copy).then_inc(S["n_ev"], 1)
                soft(0)
                act.wait_ge(S["n_done"], hw + 6)
                act.activation(ab[:], P0, ACT.Copy).then_inc(S["n_ev"], 1)
                flip(0)
                soft(1)
                act.wait_ge(S["n_done"], hw + 8)
                act.activation(sb_[:], P0, ACT.Sigmoid).then_inc(S["n_ev"], 1)
                flip(1)
                act.wait_ge(S["n_done"], hw + 10)
                act.wait_ge(S["n_u"], i * 2 + 1)
                act.activation(ab[:], P0, ACT.Copy).then_inc(S["n_ev"], 1)
                heads(0)
                soft(2)
                act.wait_ge(S["n_done"], hw + 12)
                act.activation(sb_[:], P0, ACT.Sigmoid).then_inc(S["n_ev"], 1)
                flip(2)
                soft(3)
                act.wait_ge(S["n_done"], hw + 14)
                act.activation(ga[:], P0, ACT.Copy)
                act.activation(gs[:], P0, ACT.Sigmoid).then_inc(S["n_ev"], 1)
                flip(3)
                heads(1)
                act.wait_ge(S["n_done"], hw + 16)
                act.wait_ge(S["n_y"], 1 + i * 2 + 1)
                act.activation(ga[:], P0, ACT.Copy)
                act.activation(gs[:], P0, ACT.Sigmoid).then_inc(S["n_ev"], 1)
            act.wait_ge(S["n_y"], 1 + 8)
            act.wait_ge(S["n_cv"], 1 + 8)
            with act.Fori(0, 4) as i:
                for t in range(2):
                    act.wait_ge(S["n_done"], DONE + A + 4 * BODY + i * RING + 2 * t + 2)
                    act.wait_ge(S["z_gm"], 1 + i * 2 + t)
                    act.activation(graw[:, 0], P0, ACT.Copy)
                    act.activation(graw[:, 1], P0, ACT.Sigmoid).then_inc(S["z_g"], 1)

            def norm_squares(n, view, base):
                for k in range(n):
                    act.wait_ge(S["z_c"], base + k + 1)
                    if base + k >= 2:
                        act.wait_ge(S["z_ss"], base + k - 1)
                    act.activation(sq[:, k % 2], view[:, k], ACT.Square).then_inc(S["z_sq"], 1)
                act.wait_ge(S["z_ss"], base + n)
                act.activation(rstd[:], pj[2][:, 0:LAT], ACT.Sqrt, bias=eps[:], scale=1.0 / (n * P)).then_inc(S["z_rt"], 1)

            for k in range(8):
                act.activation(high[:, k], Y[:, k], ACT.Copy).then_inc(S["n_ysh"], 1)
            norm_squares(8, uc, 0)
            for k in range(8):
                act.wait_ge(S["z_n"], k + 1)
                if k:
                    act.wait_ge(S["z_u"], k)
                act.activation(sa_[:], uc[:, k], ACT.Sigmoid, bias=pr("cln", 16)[:, 8 + k:9 + k], scale=pr("cln", 16)[:, k:k + 1])
                act.activation(uc[:, k], uc[:, k], ACT.Identity, bias=pr("cln", 16)[:, 8 + k:9 + k], scale=pr("cln", 16)[:, k:k + 1]).then_inc(S["z_i"], 1)
            with act.Fori(0, 2) as i:
                for t in range(4):
                    y8 = bass.ds(i * 4 + t + 8, 1)
                    act.wait_ge(S["z_y"], 1 + i * 4 + t + 1)
                    act.activation(high[:, y8].rearrange("p a t -> p (a t)"), yc[:], ACT.Copy).then_inc(S["n_ysh"], 1)
            act.wait_ge(S["n_xa"], 32)
            for k in range(KT):
                act.activation(X[:, k], X[:, k], ACT.Copy, scale=ALPHA).then_inc(S["n_xs"], 1)
            norm_squares(KT, X, 8)
            for k in range(KT):
                act.wait_ge(S["z_n"], 8 + k + 1)
                act.activation(X[:, k], X[:, k], ACT.Identity, bias=pr("ln2", 32)[:, 16 + k:17 + k], scale=pr("ln2", 32)[:, k:k + 1]).then_inc(S["z_o"], 1)

        @block.vector
        def _(dve):
            dve.wait_ge(e["x_saved"], 16)
            dve.memset(sc[:], -1e30).then_inc(S["n_v0"], 1)
            dve.memset(ub[:], 0.0).then_inc(S["n_v0"], 1)
            dve.wait_ge(S["n_v0"], 2)
            with dve.Fori(0, 4) as i:
                dve.wait_ge(S["n_y"], 1 + i * 2)
                dve.wait_ge(S["n_cv"], 1 + i * 2)
                n = [0]

                def link(ins):
                    n[0] += 1
                    ins.then_inc(S["n_v"], 1)
                    dve.wait_ge(S["n_v"], i * DV + n[0])

                link(dve.tensor_copy(cw[:], pr("cw2", 8 * 32).rearrange("p (n c) -> p n c", c=32)[:, bass.ds(i * 2, 2)]))
                link(dve.tensor_copy(sk[:], pr("sink", 16)[:, bass.ds(i * 4, 4)]))

                def rows(h):
                    dve.wait_ge(S["n_sc"], i * 4 + h + 1)
                    if h:
                        dve.wait_ge(S["n_tr"], i * 4 + h)
                    b = bias[:, bass.ds(i * 4 + h, 1)]
                    t = tp8[:, h % 2].rearrange("p (n a) b -> p n (a b)", a=2)
                    dve.memset(sc[:, 0, 0:P], -1e30)
                    dve.scalar_tensor_tensor(sc[:, 0, P:256], t[:, 0, P:256], 0.125, b[:, :, P:256].rearrange("p a c -> p (a c)"), ALU.mult, ALU.add)
                    link(dve.scalar_tensor_tensor(sc[:, 1:4], t[:, 1:4], 0.125, b.to_broadcast([P, 3, 256]), ALU.mult, ALU.add))
                    link(dve.tensor_reduce(mx[:], sc[:], AX_X, ALU.max))
                    dve.tensor_scalar(mx[:], mx[:], sk[:, h:h + 1], -1.0, ALU.max, ALU.mult).then_inc(S["n_m"], 1)

                def norm(h):
                    dve.wait_ge(S["n_x"], i * 4 + h + 1)
                    link(dve.tensor_tensor(sm[:], sm[:], es[:], ALU.add))
                    link(dve.reciprocal(rd[:], sm[:]))
                    dve.tensor_tensor(sc[:], sc[:], rd.unsqueeze(2).to_broadcast([P, 4, 256]), ALU.mult).then_inc(S["n_p"], 1)

                def unit(c):
                    dve.wait_ge(S["n_ev"], 1 + i * 8 + 4 + 2 * c)
                    dve.tensor_tensor(ub[:, 30:], ab[:], sb_[:], ALU.mult).then_inc(S["n_u"], 1)
                    dve.wait_ge(S["n_u"], i * 2 + c + 1)

                def conv(c, a, b):
                    for o in range(a, b):
                        if o == 0:
                            link(dve.tensor_scalar(ca[:], ub[:, 0:LAT], cw[:, c, 0:1], cw[:, c, 31:32], ALU.mult, ALU.add))
                        elif o < 30:
                            link(dve.scalar_tensor_tensor(ca[:], ub[:, o:o + LAT], cw[:, c, o:o + 1], ca[:], ALU.mult, ALU.add))
                        else:
                            d = uc[:, bass.ds(i * 2 + c, 1)].rearrange("p a t -> p (a t)")
                            dve.scalar_tensor_tensor(d, ub[:, o:o + LAT], cw[:, c, o:o + 1], ca[:], ALU.mult, ALU.add).then_inc(S["n_cv"], 1)

                def gate(j):
                    dve.wait_ge(S["n_ev"], 1 + i * 8 + 7 + j)
                    dve.wait_ge(S["n_at"], i * 2 + j + 1)
                    link(dve.tensor_tensor(at_[:, j], at_[:, j], gs[:], ALU.mult))
                    d = Y[:, bass.ds(i * 2 + j, 1)].rearrange("p a t -> p (a t)")
                    dve.tensor_tensor(d, at_[:, j], ga[:], ALU.mult).then_inc(S["n_y"], 1)

                rows(0)
                norm(0)
                rows(1)
                norm(1)
                unit(0)
                conv(0, 0, 12)
                rows(2)
                norm(2)
                conv(0, 12, 20)
                rows(3)
                norm(3)
                conv(0, 20, 31)
                dve.wait_ge(S["n_cv"], 1 + i * 2 + 1)
                unit(1)
                gate(0)
                conv(1, 0, 15)
                gate(1)
                conv(1, 15, 31)
                e["counts"]["DV_2"] = n[0]
            dve.wait_ge(S["n_cv"], 1 + 8)
            dve.wait_ge(S["n_y"], 1 + 8)
            dve.wait_ge(S["z_g"], 1 + 1)
            dve.memset(eps[:], 1e-5).then_inc(S["n_v0"], 1)
            with dve.Fori(0, 4) as i:
                for t in range(2):
                    dve.wait_ge(S["z_g"], 1 + i * 2 + t + 1)
                    dve.tensor_tensor(gcv[:, bass.ds(i * 2 + t, 1)].rearrange("p a t -> p (a t)"), graw[:, 0], graw[:, 1], ALU.mult).then_inc(S["z_gm"], 1)

            def norm_rows(n, view, base, which):
                dve.wait_ge(S["z_s"], which)
                dve.tensor_scalar(mean[:], pj[2][:, 0:LAT], 1.0 / (n * P), None, ALU.mult).then_inc(S["z_m"], 1)
                dve.wait_ge(S["z_m"], which)
                for k in range(n):
                    dve.tensor_tensor(view[:, k], view[:, k], mean[:], ALU.subtract).then_inc(S["z_c"], 1)
                dve.wait_ge(S["z_rt"], which)
                dve.reciprocal(rstd[:], rstd[:]).then_inc(S["z_rr"], 1)
                dve.wait_ge(S["z_rr"], which)
                dve.wait_ge(S["z_c"], base + n)
                for k in range(n):
                    dve.tensor_tensor(view[:, k], view[:, k], rstd[:], ALU.mult).then_inc(S["z_n"], 1)

            for k in range(8):
                dve.wait_ge(S["n_ysh"], k + 1)
                dve.tensor_tensor(low[:, k], Y[:, k], high[:, k].bitcast(F32), ALU.subtract).then_inc(S["n_ysl"], 1)
            norm_rows(8, uc, 0, 1)
            for k in range(8):
                dve.wait_ge(S["z_i"], k + 1)
                dve.tensor_tensor(uc[:, k], uc[:, k], sa_[:], ALU.mult).then_inc(S["z_u"], 1)
            with dve.Fori(0, 2) as i:
                for t in range(4):
                    k = bass.ds(i * 4 + t, 1)
                    y8 = bass.ds(i * 4 + t + 8, 1)
                    dve.wait_ge(S["n_pw"], 1 + i * RING + t + 1)
                    dve.scalar_tensor_tensor(yc[:], pj[0][:, 0:LAT], pr("b_pw", 8)[:, k], gcv[:, k].rearrange("p a t -> p (a t)"),
                                             ALU.add, ALU.mult).then_inc(S["z_y"], 1)
                    dve.wait_ge(S["n_ysh"], 8 + i * 4 + t + 1)
                    dve.tensor_tensor(low[:, y8].rearrange("p a t -> p (a t)"), yc[:], high[:, y8].rearrange("p a t -> p (a t)").bitcast(F32),
                                      ALU.subtract).then_inc(S["n_ysl"], 1)
                    dve.wait_ge(S["n_ysl"], 8 + i * 4 + t + 1)
            dve.wait_ge(S["n_xs"], 16)
            with dve.Fori(0, KT // 2) as i:
                for t in range(2):
                    dve.wait_ge(S["n_done"], DONE + A + 4 * BODY + 16 + i * RING + 2 * t + 2)
                    x = X[:, bass.ds(i * 2 + t, 1)].rearrange("p a t -> p (a t)")
                    dve.scalar_tensor_tensor(x, banks[t], mod2[:, bass.ds(i * 2 + t + 32, 1)], x, ALU.mult, ALU.add).then_inc(S["z_r"], 1)
            dve.wait_ge(S["z_r"], 2 + KT)
            norm_rows(KT, X, 8, 2)



PHASES = [(phase_mod, "a"), (phase_gates, "b"), (phase_gdn, "g"), (phase_lora, "l"), (phase_rwkv, "r"),           (phase_out, "o"), (phase_two, "nz")]
SEMS = """a_par a_x a_sig a_sq a_ss a_eps a_rt a_scl a_xn a_h a_cs a_mc a_d a_used a_row a_turn a_w0 a_w1 a_w2 a_w3 a_w4 a_w5 a_w6 a_w7
b_z b_w b_out b_scan b_x b_p b_tr b_ea b_y b_v b_gc b_raw
g_rows g_y g_st g_raw g_sq g_ss g_kb g_lt  g_ltc g_mt g_mtc g_vk g_vkc g_x g_xs g_u g_t g_tr g_tt g_pre g_s g_w g_wc
g_sa g_sac g_ds g_o g_oo g_sig g_conv g_silu g_rt g_e g_d g_v g_v0
l_raw l_mix l_th l_v
r_y r_lw r_st r_raw r_sq r_ss r_vx r_vt r_kk r_vc r_sg r_lo r_xd r_p  r_pa r_q r_pd r_tt r_s r_w r_wc r_sa r_sac r_ds
r_rk r_bs r_yx r_yt r_o r_oa r_kr r_rt r_cs r_ex r_x r_xs r_u r_t r_tr r_oc r_vr r_sd r_zs r_v r_v0
o_y o_w o_x o_r o_ss o_sq o_v o_rt o_n o_h o_b o_bd o_bm o_done o_doneh o_yh o_yl o_hh o_hl
n_done n_doneh n_vt n_ysh n_ysl n_xa n_xs n_pw n_kv n_dup n_ev n_at n_sc n_p n_tr n_pt n_pv n_y n_ks n_cv n_m n_x n_u n_v0 n_v
z_g z_gm z_s z_sq z_ss z_u z_y z_r z_c z_rt z_n z_i z_m z_rr z_o z_st""".split()


def constants():
    import numpy as np
    cols, at, n = [], {}, 0

    def add(name, a):
        nonlocal n
        a = np.asarray(a, np.float32).reshape(P, -1)
        at[name] = n
        n += a.shape[1]
        cols.append(a)

    r = np.arange(P)
    add("ident", np.eye(P))
    add("ones", np.ones((P, P)))
    add("blk", r[:, None] // 64 == r[None] // 64)
    add("istk", r[:, None] % 64 == np.arange(64)[None])
    t = np.arange(384)
    add("rst0", np.broadcast_to(t % 64 != 0, (P, 384)))
    add("rst1", np.broadcast_to(t % 64 != 63, (P, 384)))
    add("incl", np.stack([r[:, None] <= r[None], r[:, None] >= r[None]], 1))
    add("strict", np.stack([r[:, None] < r[None], r[:, None] > r[None]], 1))
    lm = np.zeros((P, LEVELS, 2, 64))
    for lv in range(LEVELS):
        b = 1 << lv
        for d in range(2):
            c = np.arange(64)
            pair = c // b
            lm[:, lv, d] = -1.0 * (r[:, None] // b == (2 * pair + 1 - d)[None])
    add("lmask", lm)
    ch = np.arange(3456)
    q, h = 864, 1728
    kinds = np.zeros((3456, 7))
    kinds[:, 0] = -1
    for k in range(4):
        kinds[:, 1 + k] = ch // q == k
    kinds[:, 5], kinds[:, 6] = ch < h, ch >= h
    add("kinds", kinds[:3072].reshape(3, PAIRS, P, 7).transpose(2, 1, 0, 3))
    add("lkinds", np.broadcast_to(kinds[-1], (P, 7)))
    j = np.arange(384)
    dist = 255 - j
    inside = (dist >= 0) & (dist < 128)
    dd = np.maximum(dist, 1).astype(np.float32)
    large = 16 + (np.log(dd / 16) / math.log(128 / 16) * 16).astype(np.int32)
    bucket = np.where(dist < 16, dist, np.minimum(large, 31))
    onehot = np.zeros((P, 384))
    onehot[:32] = (np.arange(32)[:, None] == bucket[None]) & inside[None]
    win = np.concatenate([onehot[:32], np.broadcast_to(np.where(inside, 0.0, -1e30), (32, 384))], 1)
    return np.concatenate(cols, 1), at, win.astype(np.float32)


def kernel(**inputs):
    import numpy as np
    import concourse.bacc as _bacc
    from concourse import mybir as _mybir
    from concourse.bass_utils import run_bass_kernel_spmd as _run

    a = {k: np.asarray(v) for k, v in inputs.items()}
    a = {k: (v[0] if v.ndim > 1 and v.shape[0] == 1 else v) for k, v in a.items()}

    def cols(v):
        return v.reshape(-1, P).T

    def tiles(w, width=P):
        return np.ascontiguousarray(w.reshape(w.shape[0] // P, P, -1, width).transpose(2, 1, 0, 3))

    arr = {}
    arr["xT"] = np.ascontiguousarray(a["x"].T.reshape(KT, P, LAT).transpose(1, 0, 2))
    arr["ctxT"] = np.ascontiguousarray(a["ctx"].T.reshape(KT, P, CTX).transpose(1, 0, 2))
    arr["w_ada"] = np.concatenate([tiles(a["w_ada"], 512), tiles(a["w_ada_2"], 512)])
    w = a["w_in"]
    gd = [w[:, n * 1024:(n + 1) * 1024].reshape(D, GH, P) for n in range(4)]
    arr["w_g"] = tiles(np.stack(gd, 2).reshape(D, GH * 4 * P))
    gates = w[:, 4096:4128].reshape(KT, P, 2, 2, GH)
    arr["wg"], arr["wb"] = (np.ascontiguousarray(gates[:, :, q].reshape(KT, P, 16).transpose(1, 0, 2)) for q in range(2))
    u = w[:, 4128:]
    rk = [u[:, n * 1024:(n + 1) * 1024].reshape(D, PAIRS, P) for n in range(3)] + [u[:, 3456:].reshape(D, PAIRS, P)]
    arr["w_r"] = tiles(np.stack(rk, 2).reshape(D, PAIRS * 4 * P))
    arr["w_l"] = tiles(u[:, 3072:3456], LORA)
    up = np.stack([a["rwkv_w_up"], a["rwkv_a_up"]], 1).reshape(2, 2, LORA, PAIRS, P)
    arr["w_lup"] = np.ascontiguousarray(up.transpose(3, 2, 0, 1, 4).reshape(PAIRS, LORA, 4 * P))
    arr["rows"] = np.ascontiguousarray(np.stack([a["gdn_a_log"].reshape(16), a["gdn_dt_bias"].reshape(16)] * 2, 1))
    arr["cst"], cst_at, arr["win"] = constants()

    packs, par_at, n = [], {}, 0

    def pack(name, v):
        nonlocal n
        v = np.asarray(v).reshape(P, -1)
        par_at[name] = n
        n += v.shape[1]
        packs.append(v)

    pack("c", np.stack([cols(a["c"]), cols(a["c_ctx"]), cols(a["c_2"])], 2))
    pack("b_ada", np.stack([cols(a["b_ada"])] * 2, 2))
    pack("norm_g", cols(a["norm_g"]))
    cw = a["gdn_conv_w"].reshape(CONVK, 3, GH, P).transpose(3, 2, 1, 0).reshape(P, GH, 15)
    ng = np.broadcast_to(a["gdn_norm_g"][:, None, None], (P, GH, 1))
    pack("gp", np.concatenate([cw, ng], 2))
    mu = a["rwkv_mu"]
    pack("mu", mu[:3072].reshape(3, PAIRS, P).transpose(2, 1, 0))
    mul = np.zeros((P, 4), mu.dtype)
    mul[:LORA] = mu[3072:].reshape(4, LORA).T
    pack("mul", mul)
    pc = lambda v: v.reshape(PAIRS, P).T[:, :, None]
    w0, a0 = a["rwkv_w0"], a["rwkv_a0"]
    pack("rp", np.concatenate([pc(w0[0]), pc(w0[1]), pc(a0[0]), pc(a0[1]), pc(a["rwkv_k_k"]), pc(a["rwkv_k_a"]),
                               pc(a["rwkv_k_a"]), pc(a["rwkv_r_k"]), pc(a["rwkv_gn_g"]), pc(a["rwkv_gn_b"])], 2))
    extra(a, arr, pack, tiles, cols)
    arr["par"] = np.ascontiguousarray(np.concatenate(packs, 1))
    return launch(arr, cst_at, par_at, _bacc, _mybir, _run)


def extra(a, arr, pack, tiles, cols):
    import numpy as np
    arr["w_out"] = tiles(a["w_out"])
    w = a["w_in_2"]
    q, kv, ga, ua, ub, gc = (w[:, a0:a1] for a0, a1 in ((0, 1024), (1024, 1536), (1536, 2560), (2560, 3584), (3584, 4608), (4608, 5632)))
    arr["w_kv"] = tiles(kv)
    two = lambda v: v.reshape(D, 4, 2, P)
    q, ga, ua, ub = two(q), two(ga), two(ua), two(ub)
    arr["w_2"] = tiles(np.stack([q[:, :, 0], q[:, :, 1], ua[:, :, 0], ub[:, :, 0], ua[:, :, 1], ub[:, :, 1], ga[:, :, 0], ga[:, :, 1]], 2)
                       .reshape(D, 32 * P))
    arr["w_gc"] = tiles(gc)
    arr["w_pw"] = tiles(a["w_pw_2"])
    arr["w_out2"] = tiles(a["w_out_2"])
    pack("b_ada2", cols(a["b_ada_2"]))
    pack("fng", cols(a["final_norm_g"]))
    rel = np.zeros((P, 16), np.float32)
    rel[:32] = a["rel_bias_2"]
    pack("rel", rel)
    pack("sink", np.broadcast_to(a["sinks_2"], (P, 16)))
    cw = np.concatenate([a["conv_w_2"], a["conv_b_2"][None]], 0)
    pack("cw2", cw.reshape(32, 8, P).transpose(2, 1, 0))
    pack("cln", np.concatenate([cols(a["conv_ln_g_2"]), cols(a["conv_ln_b_2"])], 1))
    pack("b_pw", cols(a["b_pw_2"]))
    pack("ln2", np.concatenate([cols(a["ln_g_2"]), cols(a["ln_b_2"])], 1))


def launch(arr, cst_at, par_at, _bacc, _mybir, _run):
    import numpy as np
    nc = _bacc.Bacc("TRN2", target_bir_lowering=False, num_devices=1)
    io = {}
    feed = {}
    for name, v in arr.items():
        feed[f"in_{name}"] = np.ascontiguousarray(v)
        io[name] = nc.dram_tensor(f"in_{name}", v.shape, _mybir.dt.from_np(v.dtype), kind="ExternalInput").ap()
    out = nc.dram_tensor("out_xT", [KT, P, LAT], F32, kind="ExternalOutput").ap()
    io["cst_at"], io["par_at"] = cst_at, par_at
    io["arena"] = ARENA
    io["sems"], io["phases"] = SEMS, PHASES
    io["base_g"] = RING
    io["base_l"] = io["base_g"] + 8 * GH
    io["base_r"] = io["base_l"] + 8
    io["base_o"] = io["base_r"] + 8 * PAIRS
    io["base_2"] = io["base_o"] + 32
    io["DV_G"], io["DV_R"], io["DV_2"] = DV_G, DV_R, DV_2
    io["counts"] = {}
    program(nc, io, out)
    for k in ("DV_G", "DV_R", "DV_2"):
        if k in io["counts"]:
            assert io["counts"][k] == io[k], (k, io["counts"])
    r = _run(nc, [feed], core_ids=[0])
    got = r.results[0]["out_xT"]
    return np.ascontiguousarray(got.reshape(D, LAT).T)[None]


ARENA = 32584
DV_G, DV_R, DV_2 = 31, 67, 80
```
